# Optimizing a Trainium2 kernel written in Bass

```python
import math
import jax, jax.numpy as jnp
from jax import lax
import numpy as np

D_MODEL = 1024
BATCH = 1
SEQ = 512
DEPTH = 4
DEC_BATCH = 8
DEC_SEQ = 4
PAST_LEN = 1024
PAGE_SIZE = 128

N_MIXERS = 3
N_A = (DEPTH + 2) // 3
N_B = (DEPTH + 1) // 3
N_C = DEPTH // 3
DN_ALPHA = (2.0 * DEPTH) ** 0.25
DN_BETA = (8.0 * DEPTH) ** -0.25
EPS = 1e-5
CONV_W = 4
LRU_W = D_MODEL
LRU_BLOCKS = 16
LRU_BS = LRU_W // LRU_BLOCKS
LRU_C = 8.0
ATT_HEADS = 8
ATT_DH = D_MODEL // (2 * ATT_HEADS)
ATT_W = ATT_HEADS * 2 * ATT_DH
Q_BLOCK = 128
SSD_INNER = 2 * D_MODEL
SSD_HEADDIM = 64
SSD_HEADS = SSD_INNER // SSD_HEADDIM
SSD_GROUPS = 8
SSD_HPG = SSD_HEADS // SSD_GROUPS
SSD_STATE = 128
SSD_CONV_DIM = SSD_INNER + 2 * SSD_GROUPS * SSD_STATE
SSD_PROJ = SSD_INNER + SSD_CONV_DIM + SSD_HEADS
SSD_CHUNK = 128
POOL_NUM, POOL_DEN = 5, 4

kernel_name = 'hybrid_rglru_diffattn_ssd_decode_step'

def layer_norm(x, g, b):
    xf = x.astype(jnp.float32)
    mu = jnp.mean(xf, -1, keepdims=True)
    var = jnp.mean(jnp.square(xf - mu), -1, keepdims=True)
    return ((xf - mu) * lax.rsqrt(var + EPS) * g.astype(jnp.float32) + b.astype(jnp.float32)).astype(x.dtype)

def rms_norm(x, w):
    xf = x.astype(jnp.float32)
    return (xf * lax.rsqrt(jnp.mean(xf * xf, -1, keepdims=True) + EPS) * w.astype(jnp.float32)).astype(x.dtype)

def causal_dwconv(u, buf, w, b):
    t = u.shape[1]
    up = jnp.concatenate([buf.astype(u.dtype), u], axis=1)
    y = up[:, 0:t] * w[0] + b
    for k in range(1, CONV_W):
        y = y + up[:, k:k + t] * w[k]
    return y, up[:, t:]

def rglru_mixer(x, conv_buf, h0, in_w, conv_w, conv_b, r_w, r_b, i_w, i_b, lam, out_w):
    f32 = jnp.float32
    gate, u = jnp.split(x @ in_w, 2, axis=-1)
    u, new_buf = causal_dwconv(u, conv_buf, conv_w, conv_b)
    bsz, t, _ = u.shape
    ub = u.reshape(bsz, t, LRU_BLOCKS, LRU_BS)
    r = jax.nn.sigmoid(jnp.einsum('btnk,nkj->btnj', ub, r_w).reshape(bsz, t, LRU_W) + r_b)
    ig = jax.nn.sigmoid(jnp.einsum('btnk,nkj->btnj', ub, i_w).reshape(bsz, t, LRU_W) + i_b)
    log_a = -LRU_C * r.astype(f32) * jax.nn.softplus(-lam.astype(f32))
    a = jnp.exp(log_a)
    bterm = jnp.sqrt(-jnp.expm1(2.0 * log_a)) * (ig * u).astype(f32)
    bterm = bterm.at[:, 0].add(a[:, 0] * h0.astype(f32))

    def combine(left, right):
        a_l, b_l = left
        a_r, b_r = right
        return a_l * a_r, a_r * b_l + b_r

    _, h = lax.associative_scan(combine, (a, bterm), axis=1)
    y = (h.astype(x.dtype) * jax.nn.silu(gate)) @ out_w
    return y, new_buf, h[:, -1].astype(x.dtype)

def diff_lambda(lam_p, lam_init):
    lp = lam_p.astype(jnp.float32)
    return jnp.exp(jnp.sum(lp[0] * lp[1])) - jnp.exp(jnp.sum(lp[2] * lp[3])) + lam_init

def diff_attn_project(x, in_w):
    bsz, t, _ = x.shape
    q, k, v, gate = jnp.split(x @ in_w, 4, axis=-1)
    q = q.reshape(bsz, t, ATT_HEADS, 2, ATT_DH)
    k = k.reshape(bsz, t, ATT_HEADS, 2, ATT_DH)
    v = v.reshape(bsz, t, ATT_HEADS, 2 * ATT_DH)
    return q, k, v, gate

def diff_attn_prompt(q, k, v, lam):
    bsz, t = q.shape[:2]
    nblk = t // Q_BLOCK
    scale = ATT_DH ** -0.5
    qb = jnp.moveaxis(q.reshape(bsz, nblk, Q_BLOCK, ATT_HEADS, 2, ATT_DH), 1, 0)
    kpos = jnp.arange(t)

    def block(args):
        qblk, start = args
        s = jnp.einsum('bqhcd,bkhcd->bhcqk', qblk, k).astype(jnp.float32) * scale
        qpos = start + jnp.arange(Q_BLOCK)
        mask = kpos[None, :] <= qpos[:, None]
        p = jax.nn.softmax(jnp.where(mask, s, -jnp.inf), axis=-1)
        w = p[:, :, 0] - lam * p[:, :, 1]
        return jnp.einsum('bhqk,bkhe->bqhe', w.astype(v.dtype), v)

    o = lax.map(block, (qb, jnp.arange(nblk) * Q_BLOCK))
    return jnp.moveaxis(o, 0, 1).reshape(bsz, t, ATT_HEADS, 2 * ATT_DH)

def diff_attn_sample(q, k, v, k_past, v_past, lam):
    t = q.shape[1]
    n_past = k_past.shape[1]
    scale = ATT_DH ** -0.5
    s_past = jnp.einsum('bqhcd,bkhcd->bhcqk', q, k_past).astype(jnp.float32) * scale
    s_new = jnp.einsum('bqhcd,bkhcd->bhcqk', q, k).astype(jnp.float32) * scale
    s_new = jnp.where(jnp.tril(jnp.ones((t, t), bool)), s_new, -jnp.inf)
    p = jax.nn.softmax(jnp.concatenate([s_past, s_new], axis=-1), axis=-1)
    w = (p[:, :, 0] - lam * p[:, :, 1]).astype(v.dtype)
    return (jnp.einsum('bhqk,bkhe->bqhe', w[..., :n_past], v_past)
            + jnp.einsum('bhqk,bkhe->bqhe', w[..., n_past:], v))

def diff_attn_output(o, gate, lam_init, subln_w, out_w):
    bsz, t = o.shape[:2]
    o = rms_norm(o, subln_w) * (1.0 - lam_init)
    return (o.reshape(bsz, t, ATT_W) * jax.nn.silu(gate)) @ out_w

def ssd_scan(xh, dt, a, bm, cm, h0):
    f32 = jnp.float32
    bsz, t = xh.shape[:2]
    q = SSD_CHUNK if t % SSD_CHUNK == 0 else t
    nc = t // q
    xdt = (xh.astype(f32) * dt[..., None]).reshape(bsz, nc, q, SSD_GROUPS, SSD_HPG, SSD_HEADDIM)
    adt = jnp.moveaxis((dt * a).reshape(bsz, nc, q, SSD_GROUPS, SSD_HPG), 2, -1)
    bc = bm.astype(f32).reshape(bsz, nc, q, SSD_GROUPS, SSD_STATE)
    cc = cm.astype(f32).reshape(bsz, nc, q, SSD_GROUPS, SSD_STATE)
    cs = lax.cumsum(adt, axis=adt.ndim - 1)
    causal = jnp.tril(jnp.ones((q, q), bool))
    lmat = jnp.exp(jnp.where(causal, cs[..., :, None] - cs[..., None, :], -jnp.inf))
    cb = jnp.einsum('bclgn,bcsgn->bcgls', cc, bc)
    y_diag = jnp.einsum('bcgls,bcgrls,bcsgrp->bclgrp', cb, lmat, xdt)
    states = jnp.einsum('bclgn,bcgrl,bclgrp->bcgrpn', bc, jnp.exp(cs[..., -1:] - cs), xdt)

    def step(h, inp):
        decay, st = inp
        return h * decay[..., None, None] + st, h

    h_last, h_prev = lax.scan(step, h0.astype(f32),
                              (jnp.moveaxis(jnp.exp(cs[..., -1]), 1, 0), jnp.moveaxis(states, 1, 0)))
    h_prev = jnp.moveaxis(h_prev, 0, 1)
    y_off = jnp.einsum('bclgn,bcgrpn,bcgrl->bclgrp', cc, h_prev, jnp.exp(cs))
    return (y_diag + y_off).reshape(bsz, t, SSD_GROUPS, SSD_HPG, SSD_HEADDIM), h_last

def ssd_mixer(x, conv_buf, h0, in_w, conv_w, conv_b, dt_bias, a_log, d_skip, norm_w, out_w):
    f32 = jnp.float32
    bsz, t, _ = x.shape
    proj = x @ in_w
    z = proj[..., :SSD_INNER]
    xbc = proj[..., SSD_INNER:SSD_INNER + SSD_CONV_DIM]
    dt_raw = proj[..., SSD_INNER + SSD_CONV_DIM:]
    xbc, new_buf = causal_dwconv(xbc, conv_buf, conv_w, conv_b)
    xbc = jax.nn.silu(xbc)
    gn = SSD_GROUPS * SSD_STATE
    xh = xbc[..., :SSD_INNER].reshape(bsz, t, SSD_GROUPS, SSD_HPG, SSD_HEADDIM)
    bm = xbc[..., SSD_INNER:SSD_INNER + gn].reshape(bsz, t, SSD_GROUPS, SSD_STATE)
    cm = xbc[..., SSD_INNER + gn:].reshape(bsz, t, SSD_GROUPS, SSD_STATE)
    dt = jax.nn.softplus(dt_raw.astype(f32) + dt_bias.astype(f32)).reshape(bsz, t, SSD_GROUPS, SSD_HPG)
    a = -jnp.exp(a_log.astype(f32)).reshape(SSD_GROUPS, SSD_HPG)
    h0g = h0.reshape(bsz, SSD_GROUPS, SSD_HPG, SSD_HEADDIM, SSD_STATE)
    y, h_last = ssd_scan(xh, dt, a, bm, cm, h0g)
    y = y + d_skip.astype(f32).reshape(SSD_GROUPS, SSD_HPG)[..., None] * xh.astype(f32)
    y = y.reshape(bsz, t, SSD_INNER).astype(x.dtype)
    y = rms_norm(y * jax.nn.silu(z), norm_w)
    return y @ out_w, new_buf, h_last.reshape(bsz, SSD_HEADS, SSD_HEADDIM, SSD_STATE).astype(x.dtype)

def setup_inputs(seed: int = 0) -> dict:
    key = jax.random.key(seed)
    ks = iter(jax.random.split(key, 48))
    f32 = jnp.float32

    def nrm(shape, scale):
        return jax.random.normal(next(ks), shape, f32) * scale

    n_pages = PAST_LEN // PAGE_SIZE
    n_used = DEC_BATCH * n_pages
    n_pool = (POOL_NUM * n_used + POOL_DEN - 1) // POOL_DEN
    page_table = jax.random.permutation(next(ks), n_pool)[:n_used].reshape(DEC_BATCH, n_pages).astype(jnp.int32)
    u = jax.random.uniform(next(ks), (N_A, LRU_W), f32, 0.9, 0.999)
    a_base = jnp.exp(jnp.log(u) / LRU_C)
    a_lambda = jnp.log(a_base) - jnp.log1p(-a_base)
    dt0 = jnp.exp(jax.random.uniform(next(ks), (N_C, SSD_HEADS), f32, math.log(1e-3), math.log(1e-1)))
    c_dt_bias = dt0 + jnp.log(-jnp.expm1(-dt0))
    c_a_log = jnp.log(jax.random.uniform(next(ks), (N_C, SSD_HEADS), f32, 1.0, 16.0))
    return dict(
        x_prompt=nrm((BATCH, SEQ, D_MODEL), 1.0),
        x_sample=nrm((DEC_BATCH, DEC_SEQ, D_MODEL), 1.0),
        cache_k=nrm((N_B, n_pool, PAGE_SIZE, ATT_HEADS, 2, ATT_DH), 1.0),
        cache_v=nrm((N_B, n_pool, PAGE_SIZE, ATT_HEADS, 2 * ATT_DH), 1.0),
        page_table=page_table,
        state_lru_conv=nrm((N_A, DEC_BATCH, CONV_W - 1, LRU_W), 1.0),
        state_lru_h=nrm((N_A, DEC_BATCH, LRU_W), 0.5),
        state_ssd_conv=nrm((N_C, DEC_BATCH, CONV_W - 1, SSD_CONV_DIM), 1.0),
        state_ssd_h=nrm((N_C, DEC_BATCH, SSD_HEADS, SSD_HEADDIM, SSD_STATE), 0.1),
        ln_g=1.0 + nrm((DEPTH, D_MODEL), 0.01),
        ln_b=nrm((DEPTH, D_MODEL), 0.01),
        a_in_w=nrm((N_A, D_MODEL, 2 * LRU_W), D_MODEL ** -0.5),
        a_conv_w=nrm((N_A, CONV_W, LRU_W), CONV_W ** -0.5),
        a_conv_b=nrm((N_A, LRU_W), 0.01),
        a_gate_r_w=nrm((N_A, LRU_BLOCKS, LRU_BS, LRU_BS), LRU_BS ** -0.5),
        a_gate_r_b=nrm((N_A, LRU_W), 0.01),
        a_gate_i_w=nrm((N_A, LRU_BLOCKS, LRU_BS, LRU_BS), LRU_BS ** -0.5),
        a_gate_i_b=nrm((N_A, LRU_W), 0.01),
        a_lambda=a_lambda,
        a_out_w=nrm((N_A, LRU_W, D_MODEL), LRU_W ** -0.5 * DN_BETA),
        b_in_w=nrm((N_B, D_MODEL, 4 * ATT_W), D_MODEL ** -0.5),
        b_lambda=nrm((N_B, 4, ATT_DH), 0.1),
        b_subln_w=1.0 + nrm((N_B, 2 * ATT_DH), 0.01),
        b_out_w=nrm((N_B, ATT_W, D_MODEL), ATT_W ** -0.5 * DN_BETA),
        c_in_w=nrm((N_C, D_MODEL, SSD_PROJ), D_MODEL ** -0.5),
        c_conv_w=nrm((N_C, CONV_W, SSD_CONV_DIM), CONV_W ** -0.5),
        c_conv_b=nrm((N_C, SSD_CONV_DIM), 0.01),
        c_dt_bias=c_dt_bias,
        c_a_log=c_a_log,
        c_d=1.0 + nrm((N_C, SSD_HEADS), 0.01),
        c_norm_w=1.0 + nrm((N_C, SSD_INNER), 0.01),
        c_out_w=nrm((N_C, SSD_INNER, D_MODEL), SSD_INNER ** -0.5 * DN_BETA),
    )

def reference(x_prompt, x_sample, cache_k, cache_v, page_table, state_lru_conv, state_lru_h,
              state_ssd_conv, state_ssd_h, ln_g, ln_b, a_in_w, a_conv_w, a_conv_b, a_gate_r_w,
              a_gate_r_b, a_gate_i_w, a_gate_i_b, a_lambda, a_out_w, b_in_w, b_lambda, b_subln_w,
              b_out_w, c_in_w, c_conv_w, c_conv_b, c_dt_bias, c_a_log, c_d, c_norm_w, c_out_w):
    xp, xs = x_prompt, x_sample
    bp, bs = xp.shape[0], xs.shape[0]
    k_p, v_p, k_s, v_s = [], [], [], []
    lc_p, lh_p, lc_s, lh_s = [], [], [], []
    sc_p, sh_p, sc_s, sh_s = [], [], [], []
    for i in range(DEPTH):
        j = i // N_MIXERS
        kind = i % N_MIXERS
        if kind == 0:
            w = (a_in_w[j], a_conv_w[j], a_conv_b[j], a_gate_r_w[j], a_gate_r_b[j],
                 a_gate_i_w[j], a_gate_i_b[j], a_lambda[j], a_out_w[j])
            zc = jnp.zeros((bp, CONV_W - 1, LRU_W), xp.dtype)
            zh = jnp.zeros((bp, LRU_W), xp.dtype)
            fp, c1, h1 = rglru_mixer(xp, zc, zh, *w)
            fs, c2, h2 = rglru_mixer(xs, state_lru_conv[j], state_lru_h[j], *w)
            lc_p.append(c1); lh_p.append(h1); lc_s.append(c2); lh_s.append(h2)
        elif kind == 1:
            lam_init = 0.8 - 0.6 * math.exp(-0.3 * i)
            lam = diff_lambda(b_lambda[j], lam_init)
            q, k, v, g = diff_attn_project(xp, b_in_w[j])
            fp = diff_attn_output(diff_attn_prompt(q, k, v, lam), g, lam_init, b_subln_w[j], b_out_w[j])
            k_p.append(k); v_p.append(v)
            q, k, v, g = diff_attn_project(xs, b_in_w[j])
            k_past = cache_k[j, page_table].reshape(bs, -1, ATT_HEADS, 2, ATT_DH)
            v_past = cache_v[j, page_table].reshape(bs, -1, ATT_HEADS, 2 * ATT_DH)
            o = diff_attn_sample(q, k, v, k_past.astype(q.dtype), v_past.astype(v.dtype), lam)
            fs = diff_attn_output(o, g, lam_init, b_subln_w[j], b_out_w[j])
            k_s.append(k); v_s.append(v)
        else:
            w = (c_in_w[j], c_conv_w[j], c_conv_b[j], c_dt_bias[j], c_a_log[j], c_d[j], c_norm_w[j], c_out_w[j])
            zc = jnp.zeros((bp, CONV_W - 1, SSD_CONV_DIM), xp.dtype)
            zh = jnp.zeros((bp, SSD_HEADS, SSD_HEADDIM, SSD_STATE), xp.dtype)
            fp, c1, h1 = ssd_mixer(xp, zc, zh, *w)
            fs, c2, h2 = ssd_mixer(xs, state_ssd_conv[j], state_ssd_h[j], *w)
            sc_p.append(c1); sh_p.append(h1); sc_s.append(c2); sh_s.append(h2)
        xp = layer_norm(DN_ALPHA * xp + fp, ln_g[i], ln_b[i])
        xs = layer_norm(DN_ALPHA * xs + fs, ln_g[i], ln_b[i])
    return (xp, xs, jnp.stack(k_p), jnp.stack(v_p), jnp.stack(k_s), jnp.stack(v_s),
            jnp.stack(lc_p), jnp.stack(lh_p), jnp.stack(lc_s), jnp.stack(lh_s),
            jnp.stack(sc_p), jnp.stack(sh_p), jnp.stack(sc_s), jnp.stack(sh_s))


_drawn_inputs = setup_inputs


def setup_inputs(seed=0):
    import zlib

    import numpy as np

    out = dict(_drawn_inputs(seed))
    spreads = {}
    factors = {'a_gate_r_b': 26.315,
     'a_gate_i_b': 8.0,
     'b_subln_w': 45.79,
     'c_conv_b': 2.895,
     'c_d': 49.33,
     'c_norm_w': 49.344}
    for name, (base, spread) in spreads.items():
        noise = np.random.default_rng([zlib.crc32(name.encode()), seed]).standard_normal(out[name].shape)
        drawn = base * np.exp(spread * noise) if base else spread * noise
        out[name] = __import__('jax').numpy.asarray(drawn.astype(out[name].dtype))
    for name, factor in factors.items():
        out[name] = (out[name] * factor).astype(out[name].dtype)
    return out
```

```python
import math
from contextlib import ExitStack, contextmanager

import concourse.bass as bass
from concourse import mybir

F32 = mybir.dt.float32
F32R = mybir.dt.float32r
I32 = mybir.dt.int32
ALU = mybir.AluOpType
ACT = mybir.ActivationFunctionType
AX = mybir.AxisListType

P = 128
D = 1024
KT = D // P
SEQ, NB, DT = 512, 8, 4
NS = NB * DT
T = SEQ + NS
TAPS = 4
HIST = TAPS - 1
WIN = HIST + DT
UW = HIST + SEQ + NB * WIN
CW = UW - HIST
SROW = HIST + SEQ
DEPTH = 4
ALPHA = (2.0 * DEPTH) ** 0.25
EPS = 1e-5
QB = SEQ // P
CH = QB + 1
HEADS, DH = 8, 64
PAGES, PAGE = 8, 128
GROUPS, HPG, HD, STATE = 8, 4, 64, 128
SSDH = GROUPS * HPG
INNER = SSDH * HD
CT = INNER // P
CONV_C = INNER + 2 * GROUPS * STATE
NEG = -1e30
LAM_INIT = 0.8 - 0.6 * math.exp(-0.3)
HN = HIST + NB * HIST
AN = HN + 1 + NB

TAILS_OUT = 16 * 4 * (3 + 2)

STEPS = {("act", "a"): 4, ("act", "out"): 0, ("act", "b"): 24, ("act", "c"): 7, ("act", "c_out"): 0,
         ("dve", "a"): 23, ("dve", "out"): 0, ("dve", "b"): 106, ("dve", "c"): 95, ("dve", "c_out"): 2}

SLOT_A = [0, 128]
USE_A = [0, 120]
SLOT_B = USE_B = 24
SLOT_C = USE_C = 64


class Chain:

    def __init__(self, eng, sem, steps, engine):
        self.eng, self.sem, self.steps, self.engine = eng, sem, steps, engine
        self.count, self.turn, self.per = 0, None, 0

    def __call__(self, instruction):
        instruction.then_inc(self.sem, 1)
        self.count += 1
        value = self.count if self.turn is None else self.turn * self.per + self.count
        self.eng.wait_ge(self.sem, value)

    @contextmanager
    def loop(self, name, turns):
        start = self.count
        self.per = self.steps[self.engine, name]
        with self.eng.Fori(0, turns) as i:
            self.turn = i
            yield i
            took = self.count - start
        assert took == self.per, (self.engine, name, took)
        self.turn = None
        self.count = start + turns * self.per


def turns_of(chain, name, n, body, peel=False):
    with chain.loop(name, n - peel) as i:
        body(i, False)
    if peel:
        body(n - 1, True)


def tokens_of(ap):
    return ap[:, 0:SEQ], ap[:, SEQ:T]


class Chip:
    pass


def allocate(nc, ctx):
    k = Chip()

    def sb(name, shape, dtype=F32):
        return ctx.enter_context(nc.sbuf_tensor(name, shape, dtype))

    def ps(name, shape):
        return ctx.enter_context(nc.psum_tensor(name, shape, F32))

    k.sb = sb
    k.xT = sb("xT", [P, KT, T])
    k.xh = sb("xh", [P, KT, T], F32R)
    k.xl = sb("xl", [P, KT, T], F32R)
    k.gh = sb("gh", [P, KT, T], F32R)
    k.gl = sb("gl", [P, KT, T], F32R)
    k.sq = [sb(f"sq{j}", [P, 2, T]) for j in range(2)]
    k.rows = [q.rearrange("p a t -> p (a t)")[:, 0:D] for q in k.sq]
    k.raw = [sb(f"w_raw{j}", [P, KT, P]) for j in range(2)]
    k.wh = [sb(f"w_high{j}", [P, KT, P], F32R) for j in range(2)]
    k.wl = [sb(f"w_low{j}", [P, KT, P], F32R) for j in range(2)]
    k.ident = sb("ident", [P, P])
    k.tri = sb("tri", [P, P])
    k.ones_d = sb("ones_d", [P, P])
    k.eps = sb("eps", [P, 1])
    k.par_a = [sb(f"par_a{j}", [P, KT, 40]) for j in range(2)]
    k.par_m = sb("par_m", [P, KT, 10])
    k.rs = sb("rs", [P, T])

    k.proj = ps("proj", [P, 2, 512])
    k.proj_s = ps("proj_s", [P, 512])
    k.s = ps("s", [P, 2, 512])
    k.r = ps("r", [P, 2, 512])
    k.x = ps("x", [P, 512])

    names = """w_landed0 w_landed1 w_hi w_lo pe_slot p_evac0 p_evac1 s_evac x_ready
        rows_landed0 rows_landed1 rows_turned rows_read consts chain_act chain_dve chain_pool
        sp_in sp_out params x_split
        gw_landed  conv_done gates_done a_rest ti_ready t_ready rt_ready tg_ready
        tails_turned tails_read tails_out
        ln_mean ln_sub ln_sq ln_acc ln_sd ln_norm ln_x ln_xh
        table_in b_params b_consts lam_in lam_exp r_done r_read0 r_read1 s_done s_read x_done x_read
        k_landed0 k_landed1 v_landed0 v_landed1 tok_ready kv_out tgb_ready pm_ready w_ready sm_ready
        c_ready o_squared b_head
        c_params c_consts dt_raw adt_ready sums_done a_exp dec_in dt_made st_landed st_ready st_out hout_ready hp_out
        g_squared g_made g_ready acc_added ctails_turned ctails_read ctails_out y_in hts_used feat_ready group_params
        ms_done c_rms c_x c_conv c_tanh dm_ready cs_done cs_read0 cs_read1 cr_done cr_read0 cr_read1 cx_done cx_read
        y_turned y_read0 y_read1 y_out0 y_out1 done""".split()
    k.sem = {}
    for name in names:
        k.sem[name] = ctx.enter_context(nc.semaphore(name))
    return k



def load_slot(sp, k, s, par, rows):
    sp.wait_ge(k.sem["w_lo"], s)
    sp.dma_start(k.raw[par][:], rows.rearrange("(k p) n -> p k n", p=P)).then_inc(k.sem[f"w_landed{par}"], 16)


def split_high(act, k, s, half, par):
    act.wait_ge(k.sem[f"w_landed{par}"], 16 * half + 16)
    act.wait_ge(k.sem["pe_slot"], s)
    act.activation(k.wh[par][:], k.raw[par][:], ACT.Copy).then_inc(k.sem["w_hi"], 1)


def split_low(dve, k, s, par):
    dve.wait_ge(k.sem["w_hi"], s + 1)
    dve.wait_ge(k.sem["pe_slot"], s)
    dve.tensor_tensor(k.wl[par][:], k.raw[par][:], k.wh[par][:], ALU.subtract).then_inc(k.sem["w_lo"], 1)


def multiply_slot(pe, k, s, par, use, use_half, upar, mh, ml, k0=0, first=True, last=True):
    pe.wait_ge(k.sem["w_lo"], s + 2)
    if first:
        pe.wait_ge(k.sem[f"p_evac{upar}"], use_half)
    for cols, out in ((slice(0, SEQ), k.proj[:, upar, :]), (slice(SEQ, T), k.proj_s[:, 0:NS])):
        if first and cols.start:
            pe.wait_ge(k.sem["s_evac"], use)
        for i in range(KT):
            for n, (w, m) in enumerate(((k.wh, mh), (k.wh, ml), (k.wl, mh))):
                mm = pe.matmul(out, w[par][:, i, :], m[:, k0 + i, cols],
                               start=first and i == 0 and n == 0, stop=last and i == KT - 1 and n == 2)
    mm.then_inc(k.sem["pe_slot"], 1)


def await_slot(eng, k, s):
    eng.wait_ge(k.sem["pe_slot"], s + 2)



def row_jobs(a):
    xp = a["x_prompt"].rearrange("b t d -> (b t) d")
    jobs = [("x", c, P, [(0, P, xp[c * P:(c + 1) * P, :])]) for c in range(QB)]
    jobs.append(("x", QB, NS, [(0, NS, a["x_sample"].rearrange("b t d -> (b t) d"))]))
    for j in range(2):
        one = [a["a_conv_b"], a["a_gate_r_b"], a["a_gate_i_b"], a["a_lambda"]]
        jobs.append(("a", j, 40, [(0, 4, a["a_conv_w"][j])]
                     + [(4 + n, 1, v[j:j + 1, :]) for n, v in enumerate(one)]
                     + [(8, 24, a["state_lru_conv"][j].rearrange("b k d -> (b k) d")),
                        (32, 8, a["state_lru_h"][j])]))
    jobs.append(("m", 0, 10, [(0, 4, a["ln_g"]), (4, 4, a["ln_b"]),
                              (8, 2, a["c_norm_w"].rearrange("a (r d) -> (a r) d", r=2))]))
    for q in range(CONV_C // D):
        cols = slice(q * D, (q + 1) * D)
        jobs.append(("c", q, 29, [(0, 4, a["c_conv_w"][0][:, cols]), (4, 1, a["c_conv_b"][:, cols]),
                                  (5, 24, a["state_ssd_conv"][0].rearrange("b k d -> (b k) d")[:, cols])]))
    return jobs


def prologue_sync(sp, k, a):
    landed = [0, 0]
    for j, (_, _, _, parts) in enumerate(row_jobs(a)):
        if j == 2:
            for s in range(2):
                load_slot(sp, k, s, s, a_slot(a, 0, s))
        if j >= 2:
            sp.wait_ge(k.sem["rows_turned"], j - 1)
        for at, n, src in parts:
            sp.dma_start(k.rows[j % 2][at:at + n, :], src).then_inc(k.sem[f"rows_landed{j % 2}"], 16)


def a_slot(a, j, n):
    col = (1 - n % 2) * D + (n // 2) * P
    return a["a_in_w"][j][:, col:col + P]


def prologue_pool(pool, k, chain):
    sem = k.sem
    for t, v in ((k.ident, 0.0), (k.tri, 1.0), (k.ones_d, 1.0 / D), (k.eps, EPS), (k.gw, 0.0), (k.u, 0.0)):
        chain(pool.memset(t[:], v))
    chain(pool.affine_select(out=k.ident[:], in_=k.ident[:], compare_op=ALU.not_equal, fill=1.0,
                             base=0, pattern=[[-1, P]], channel_multiplier=1))
    pool.affine_select(out=k.tri[:], in_=k.tri[:], compare_op=ALU.is_ge, fill=0.0,
                       base=0, pattern=[[1, P]], channel_multiplier=-1).then_inc(sem["consts"], 1)


def prologue_tensor(pe, k, a):
    sem = k.sem
    pe.wait_ge(sem["consts"], 1)
    landed = [0, 0]
    for j, (_, _, n, parts) in enumerate(row_jobs(a)):
        landed[j % 2] += 16 * len(parts)
        pe.wait_ge(sem[f"rows_landed{j % 2}"], landed[j % 2])
        if j >= 2:
            pe.wait_ge(sem["rows_read"], j - 1)
        bank = (k.s, k.r)[j % 2]
        for i in range(KT):
            t = pe.transpose(bank[:, i // 4, (i % 4) * n:(i % 4) * n + n],
                             k.rows[j % 2][0:n, i * P:(i + 1) * P], k.ident[0:n, 0:n])
        t.then_inc(sem["rows_turned"], 1)


def prologue_vector(dve, k, a, chain):
    sem = k.sem
    dve.wait_ge(sem["consts"], 1)
    for j, (kind, c, n, _) in enumerate(row_jobs(a)):
        dve.wait_ge(sem["rows_turned"], j + 1)
        bank = (k.s, k.r)[j % 2]
        dst = {"x": lambda: k.xT[:, :, c * P:c * P + n], "a": lambda: k.par_a[c][:],
               "m": lambda: k.par_m[:], "c": lambda: k.par_c[:, c * KT:(c + 1) * KT, :]}[kind]()
        dve.tensor_copy(dst.rearrange("p (b i) n -> p b i n", b=2),
                        bank[:, :, 0:4 * n].rearrange("p b (i n) -> p b i n", i=4)).then_inc(sem["rows_read"], 1)
        if j == CH - 1:
            split_low(dve, k, 0, 0)
            dve.wait_ge(sem["x_split"], 1)
            dve.tensor_tensor(k.xl[:], k.xT[:], k.xh[:], ALU.subtract).then_inc(sem["x_ready"], 1)
    dve.wait_ge(sem["rows_read"], len(row_jobs(a)))
    for j in range(2):
        d = k.par_d[j]
        chain(dve.tensor_scalar(d[:, 0:2, :].rearrange("p c i -> p i c"), k.par_a[j][:, :, 5:7], 0.5, None, ALU.mult))
        chain(dve.tensor_scalar(k.spx[:, j * KT:(j + 1) * KT], k.par_a[j][:, :, 7], -1.0, None, ALU.mult))
    softplus_vector(dve, k, chain, k.spx[:], k.spy[:], k.spa[:, :, 0:2 * KT], 1)
    for j in range(2):
        chain(dve.tensor_scalar(k.par_d[j][:, 2, :], k.spy[:, j * KT:(j + 1) * KT], 2.0, None, ALU.mult))


def softplus_vector(dve, k, chain, x, y, tmp, call):
    a, s, p = tmp[:, 0], tmp[:, 1], tmp[:, 2]
    chain(dve.tensor_scalar(a, x, -1.0, None, ALU.mult))
    dve.tensor_tensor(a, a, x, ALU.max).then_inc(k.sem["sp_in"], 1)
    dve.wait_ge(k.sem["sp_out"], call)
    chain(dve.tensor_scalar(s, a, 2.0, None, ALU.add))
    chain(dve.reciprocal(s, s))
    chain(dve.tensor_tensor(s, s, a, ALU.mult))
    chain(dve.tensor_tensor(a, s, s, ALU.mult))
    chain(dve.tensor_scalar(p, a, 1.0 / 15, None, ALU.mult))
    for n in (13, 11, 9, 7, 5, 3):
        chain(dve.scalar_tensor_tensor(p, p, 1.0 / n, a, ALU.add, ALU.mult))
    chain(dve.scalar_tensor_tensor(p, p, 1.0, s, ALU.add, ALU.mult))
    chain(dve.tensor_scalar(a, x, 0.0, None, ALU.max))
    chain(dve.scalar_tensor_tensor(y, p, 2.0, a, ALU.mult, ALU.add))


def softplus_scalar(act, k, tmp, call):
    act.wait_ge(k.sem["sp_in"], call)
    act.activation(tmp[:, 0], tmp[:, 0], ACT.Exp, scale=-1.0).then_inc(k.sem["sp_out"], 1)


def prologue_scalar(act, k, a):
    split_high(act, k, 0, 0, 0)
    act.wait_ge(k.sem["rows_read"], CH)
    act.activation(k.xh[:], k.xT[:], ACT.Copy).then_inc(k.sem["x_split"], 1)
    softplus_scalar(act, k, k.spa[:, :, 0:2 * KT], 1)



def a_sync(sp, k, a, j, nxt):
    s0, sem = SLOT_A[j], k.sem
    g_w = [a["a_gate_r_w"][j], a["a_gate_i_w"][j]]

    def gates(i, block):
        sp.wait_ge(sem["gates_done"], 8 * j + i)
        for n in range(2):
            for h in range(2):
                sp.dma_start(k.gw[h * 64:h * 64 + 64, n, h * 64:h * 64 + 64],
                             g_w[n][bass.ds(block[h], 1), :, :].rearrange("o a b -> (o a) b")).then_inc(sem["gw_landed"], 16)

    sp.wait_ge(sem["consts"], 1 + j)
    with sp.Fori(0, KT - 1) as i:
        cols = [sp.snap(i * P + P + D), sp.snap(i * P + P)]
        block = [sp.snap(2 * i), sp.snap(2 * i + 1)]
        for h in range(2):
            load_slot(sp, k, s0 + 2 + 2 * i + h, h, a["a_in_w"][j][:, bass.ds(cols[h], P)])
        gates(i, block)
    gates(KT - 1, [2 * KT - 2, 2 * KT - 1])
    out_sync(sp, k, s0 + 16, a["a_out_w"][j])
    for h in range(2):
        if nxt:
            load_slot(sp, k, s0 + 24 + h, h, nxt[h])


def a_tensor(pe, k, j):
    s0, u0, sem = SLOT_A[j], USE_A[j], k.sem
    pe.wait_ge(sem["x_ready"], 3 * j + 1)
    with pe.Fori(0, KT) as i:
        multiply_slot(pe, k, s0 + 2 * i, 0, u0 + 2 * i, u0 // 2 + i, 0, k.xh, k.xl)
        multiply_slot(pe, k, s0 + 2 * i + 1, 1, u0 + 2 * i + 1, u0 // 2 + i, 1, k.xh, k.xl)
        n = 8 * j + i
        pe.wait_ge(sem["gw_landed"], 64 * n + 64)
        pe.wait_ge(sem["conv_done"], n + 1)
        pe.wait_ge(sem["ti_ready"], n)
        for g in range(2):
            pe.matmul(k.s[:, g, :], k.gw[:, g, :], k.cx[:, 0:SEQ], start=True, stop=True)
        for g in range(2):
            mm = pe.matmul(k.r[:, 0, g * NS:g * NS + NS], k.gw[:, g, :], k.cx[:, SEQ:T], start=True, stop=True)
        mm.then_inc(sem["gates_done"], 1)
    pe.wait_ge(sem["a_rest"], 8 * j + 8)
    for q in range(3):
        n = 3 if q < 2 else 2
        t = pe.transpose(k.x[0:n * AN, q * P:(q + 1) * P], k.tails[:, 3 * q:3 * q + n, :].rearrange("p i c -> p (i c)"), k.ident[:, :])
    t.then_inc(sem["tails_turned"], 1)
    out_tensor(pe, k, s0 + 16, u0 + 16)
    ln_tensor(pe, k, 3 * j)


def a_scalar(act, k, j, chain):
    s0, u0, sem = SLOT_A[j], USE_A[j], k.sem
    with chain.loop("a", KT) as i:
        n = 8 * j + i
        split_high(act, k, s0 + 2 * i + 1, s0 // 2 + i, 1)
        await_slot(act, k, s0 + 2 * i)
        act.wait_ge(sem["conv_done"], n)
        act.activation(k.u[:, HIST:SROW], k.proj[:, 0, :], ACT.Copy).then_inc(sem["p_evac0"], 1)
        act.activation(k.u_s[:, :, HIST:WIN], k.proj_s[:, 0:NS].rearrange("p (b t) -> p b t", b=NB),
                       ACT.Copy).then_inc(sem["s_evac"], 1)
        split_high(act, k, s0 + 2 * i + 2, s0 // 2 + i + 1, 0)
        await_slot(act, k, s0 + 2 * i + 1)
        act.wait_ge(sem["a_rest"], n)
        chain(act.activation(k.tg[:, 0:SEQ], k.proj[:, 1, :], ACT.Tanh, scale=0.5))
        act.activation(k.tg[:, SEQ:T], k.proj_s[:, 0:NS], ACT.Tanh, scale=0.5).then_inc(sem["tg_ready"], 1)
        act.wait_ge(sem["gates_done"], n + 1)
        chain(act.activation(k.tr[:, 0:SEQ], k.s[:, 0, :], ACT.Tanh, scale=0.5, bias=k.cur[:, 40:41]))
        chain(act.activation(k.tr[:, SEQ:T], k.r[:, 0, 0:NS], ACT.Tanh, scale=0.5, bias=k.cur[:, 40:41]))
        chain(act.activation(k.ti[:, 0:SEQ], k.s[:, 1, :], ACT.Tanh, scale=0.5, bias=k.cur[:, 41:42]))
        act.activation(k.ti[:, SEQ:T], k.r[:, 0, NS:2 * NS], ACT.Tanh, scale=0.5,
                       bias=k.cur[:, 41:42]).then_inc(sem["ti_ready"], 1)
        act.activation(k.t[:], k.tr[:], ACT.Tanh, scale=k.cur[:, 42:43], bias=k.cur[:, 42:43]).then_inc(sem["t_ready"], 1)
        act.wait_ge(sem["t_ready"], n + 1)
        act.activation(k.rt[:], k.t[:], ACT.Sqrt).then_inc(sem["rt_ready"], 1)
    out_scalar(act, k, s0 + 16, chain, 3 * j == k.last)
    ln_scalar(act, k, 3 * j, chain)


def convolve(dve, k, chain, cur, out, done):
    acc = k.conv
    chain(dve.tensor_scalar(acc[:], k.u[:, 0:CW], cur[:, 0:1], cur[:, 4:5], ALU.mult, ALU.add))
    for tap in (1, 2):
        chain(dve.scalar_tensor_tensor(acc[:], k.u[:, tap:tap + CW], cur[:, tap:tap + 1], acc[:], ALU.mult, ALU.add))
    chain(dve.scalar_tensor_tensor(out[:, 0:SEQ], k.u[:, HIST:SROW], cur[:, 3:4], acc[:, 0:SEQ], ALU.mult, ALU.add))
    ends = k.conv_s
    dve.scalar_tensor_tensor(out[:, SEQ:T].rearrange("p (b t) -> p b t", b=NB), k.u_s[:, :, HIST:WIN], cur[:, 3:4],
                             ends[:, :, 0:DT], ALU.mult, ALU.add).then_inc(k.sem[done], 1)


def a_vector(dve, k, j, chain):
    s0, u0, sem = SLOT_A[j], USE_A[j], k.sem
    first = slice(SEQ, T, DT)
    with chain.loop("a", KT) as i:
        n = 8 * j + i
        chain(dve.tensor_scalar(k.cur[:, 0:40], k.par_a[j][:, bass.ds(i, 1), :].rearrange("p o c -> p (o c)"), 1.0, None, ALU.mult))
        chain(dve.tensor_scalar(k.cur[:, 40:43], k.par_d[j][:, :, bass.ds(i, 1)].rearrange("p c o -> p (c o)"), 1.0, None, ALU.mult))
        chain(dve.tensor_copy(k.u_s[:, :, 0:HIST], k.cur[:, 8:32].rearrange("p (b t) -> p b t", b=NB)))
        split_low(dve, k, s0 + 2 * i + 1, 1)
        dve.wait_ge(sem["p_evac0"], u0 // 2 + i + 1)
        dve.wait_ge(sem["s_evac"], u0 + 2 * i + 1)
        tail = k.tails[:, bass.ds(i, 1), :].rearrange("p o c -> p (o c)")
        chain(dve.tensor_scalar(tail[:, 0:HIST], k.u[:, SEQ:SROW], 1.0, None, ALU.mult))
        chain(dve.tensor_scalar(tail[:, HIST:HN].rearrange("p (b t) -> p b t", b=NB), k.u_s[:, :, DT:WIN], 1.0, None, ALU.mult))
        dve.wait_ge(sem["gates_done"], n)
        convolve(dve, k, chain, k.cur, k.cx, "conv_done")
        split_low(dve, k, s0 + 2 * i + 2, 0)
        dve.wait_ge(sem["tg_ready"], n + 1)
        dve.scalar_tensor_tensor(k.sg[:, 0:SEQ], k.tg[:, 0:SEQ], 1.0, k.proj[:, 1, :], ALU.add, ALU.mult).then_inc(sem["p_evac1"], 1)
        dve.scalar_tensor_tensor(k.sg[:, SEQ:T], k.tg[:, SEQ:T], 1.0, k.proj_s[:, 0:NS], ALU.add, ALU.mult).then_inc(sem["s_evac"], 1)
        dve.wait_ge(sem["ti_ready"], n + 1)
        dve.wait_ge(sem["conv_done"], n + 1)
        chain(dve.scalar_tensor_tensor(k.gi[:], k.ti[:], 1.0, k.cx[:], ALU.add, ALU.mult))
        dve.wait_ge(sem["t_ready"], n + 1)
        chain(dve.tensor_scalar(k.q[:], k.t[:], -1.0, -1.0, ALU.mult, ALU.add))
        chain(dve.reciprocal(k.q[:], k.q[:]))
        chain(dve.scalar_tensor_tensor(k.a[:], k.t[:], 1.0, k.q[:], ALU.subtract, ALU.mult))
        dve.wait_ge(sem["rt_ready"], n + 1)
        chain(dve.scalar_tensor_tensor(k.q[:], k.rt[:], -1.0, k.q[:], ALU.mult, ALU.mult))
        chain(dve.tensor_tensor(k.gi[:], k.gi[:], k.q[:], ALU.mult))
        chain(dve.tensor_tensor(k.h0a[:], k.a[:, first], k.cur[:, 32:40], ALU.mult))
        chain(dve.tensor_tensor(k.gi[:, first], k.gi[:, first], k.h0a[:], ALU.add))
        chain(dve.memset(k.a[:, first], 0.0))
        chain(dve.tensor_tensor_scan(k.h[:], k.a[:], k.gi[:], 0.0, ALU.mult, ALU.add))
        chain(dve.tensor_scalar(tail[:, HN:HN + 1], k.h[:, SEQ - 1:SEQ], 1.0, None, ALU.mult))
        chain(dve.tensor_scalar(tail[:, HN + 1:AN], k.h[:, SEQ + DT - 1:T:DT], 1.0, None, ALU.mult))
        dve.wait_ge(sem["s_evac"], u0 + 2 * i + 2)
        dve.wait_ge(sem["p_evac1"], u0 // 2 + i + 1)
        chain(dve.scalar_tensor_tensor(k.h[:], k.h[:], 0.5, k.sg[:], ALU.mult, ALU.mult))
        high = k.gh[:, bass.ds(i, 1), :].rearrange("p o t -> p (o t)")
        low = k.gl[:, bass.ds(i, 1), :].rearrange("p o t -> p (o t)")
        chain(dve.tensor_scalar(high, k.h[:], 1.0, None, ALU.mult))
        dve.tensor_tensor(low, k.h[:], high, ALU.subtract).then_inc(sem["a_rest"], 1)
        dve.wait_ge(sem["a_rest"], n + 1)
    dve.wait_ge(sem["tails_turned"], 1 + j)
    if j:
        dve.wait_ge(sem["tails_out"], TAILS_OUT)
    dve.tensor_copy(k.tails_sb[0:3 * AN, 0:2 * P], k.x[0:3 * AN, 0:2 * P]).then_inc(sem["tails_read"], 1)
    dve.tensor_copy(k.tails_sb[0:2 * AN, 2 * P:3 * P], k.x[0:2 * AN, 2 * P:3 * P]).then_inc(sem["tails_read"], 1)
    out_vector(dve, k, s0 + 16, u0 + 16, chain, 3 * j == k.last)
    ln_vector(dve, k, 3 * j, chain)


def tails_stores(pool, k, a, o, j):
    pool.wait_ge(k.sem["tails_read"], 2 * j + 2)
    outputs = ((o["lru_conv_prompt"][j, 0], 0, HIST), (o["lru_conv_sample"][j].rearrange("b k d -> (b k) d"), HIST, NB * HIST),
               (o["lru_h_prompt"][j], HN, 1), (o["lru_h_sample"][j], HN + 1, NB))
    for r in range(3):
        for dst, at, rows in outputs:
            row = slice(r * AN + at, r * AN + at + rows)
            pool.dma_start(dst[:, 0:6 * P].rearrange("n (q r p) -> n q r p", q=2, r=3)[:, :, r, :],
                           k.tails_sb[row, 0:2 * P].rearrange("n (q p) -> n q p", q=2)).then_inc(k.sem["tails_out"], 16)
            if r < 2:
                pool.dma_start(dst[:, (6 + r) * P:(7 + r) * P], k.tails_sb[row, 2 * P:3 * P]).then_inc(k.sem["tails_out"], 16)



R_PAIR, S_PAIR, X_PAIR = 44, 18, 33


def r_turn(c):
    return c


def r_keys(n, q):
    return 4 + 5 * n + q


def r_weights(n):
    return 4 + 5 * n + 4


def s_prompt(n):
    return 2 * n


def s_sample(n):
    return 2 * n + 1


def s_rms(h):
    return 16 + h


def x_new(n):
    return 4 * n + 1


def x_prompt(n):
    return 4 * n + 2


def x_weights(n):
    return 4 * n + 3


def x_sample(n):
    return 4 * n + 4


def await_fill(eng, k, bank, i, local):
    per = {"r": R_PAIR, "s": S_PAIR, "x": X_PAIR}[bank]
    eng.wait_ge(k.sem[f"{bank}_done"], per * i + local + 1)


def may_fill(pe, k, bank, i, local):
    if bank == "r":
        pe.wait_ge(k.sem[f"r_read{local % 2}"], R_PAIR // 2 * i + local // 2)
    else:
        pe.wait_ge(k.sem[f"{bank}_read"], {"s": S_PAIR, "x": X_PAIR}[bank] * i + local)


def layer_b_buffers(k):
    k.qz = [k.sb(f"q_split{h}", [P, 2, SEQ]) for h in range(2)]
    k.qs = [k.sb(f"q_sample{h}", [P, NB, 32]) for h in range(2)]
    k.kt = [k.sb(f"k_feat{h}", [P, T]) for h in range(2)]
    k.ot = [k.sb(f"o_feat{h}", [P, T]) for h in range(2)]
    k.vt = k.ot
    k.sgb = [k.sb(f"silu_gate{h}", [P, T]) for h in range(2)]
    k.ktok = k.sb("k_tok", [P, CH, 2, P])
    k.vtok = k.sb("v_tok", [P, CH, 2, P])
    k.pp = k.sb("p_prompt", [P, 2, SEQ])
    k.tgb = k.pp.rearrange("p c t -> p (c t)")[:, 0:T]
    k.wt = k.sb("w_turned", [P, QB, P])
    k.kts = k.sb("past_k_feat", [P, 2, PAGES, P])
    k.pps = k.sb("p_sample", [64, PAGES * P])
    k.ppn = k.sb("p_new", [64, NS])
    k.ws = k.sb("w_sample", [P, (PAGES + 1) * 8])
    k.kb = [k.sb(f"k_pages{h}", [P, 4, 2 * P]) for h in range(2)]
    k.vb = [k.sb(f"v_pages{h}", [P, 4, 2 * P]) for h in range(2)]
    k.pm, k.pl, k.st = k.sb("p_max", [P, 2]), k.sb("p_sum", [P, 2]), k.sb("s_stats", [64, 6])
    k.negq = k.sb("mask_q", [P, P])
    k.qsel = k.sb("q_select", [NS, NB, 32])
    k.negs = k.sb("mask_s", [NS, NS])
    k.cp = k.sb("c_pattern", [64, 3, 8])
    k.cmat = k.sb("c_matrix", [64, 8])
    k.lam = k.sb("lam", [P, 4])
    k.blam = k.sb("lam_rows", [P, 4 * DH])
    k.subw = k.sb("subln", [P, 1])
    k.table = k.sb("table", [1, NB * PAGES], I32)


def b_cols(a, kind, h):
    return a["b_in_w"][0][:, (kind * HEADS + h) * P:(kind * HEADS + h + 1) * P]


def b_sync(sp, k, a, nxt):
    sem, s0 = k.sem, SLOT_B
    sp.wait_ge(sem["tails_out"], TAILS_OUT)
    sp.dma_start(k.table[:], a["page_table"].rearrange("(o b) n -> o (b n)", o=1)).then_inc(sem["table_in"], 16)
    sp.dma_start(k.blam[:], a["b_lambda"].rearrange("o a d -> o (a d)").broadcast_to([P, 4 * DH])).then_inc(sem["b_params"], 16)
    sp.dma_start(k.subw[:], a["b_subln_w"].rearrange("o d -> d o")).then_inc(sem["b_params"], 16)
    sp.wait_ge(sem["table_in"], 16)
    keys = a["cache_k"][0].rearrange("n t h c d -> n t (h c d)")
    values = a["cache_v"][0].rearrange("n t h d -> n t (h d)")

    def pages(i, n, col):
        page = [sp.value_load(k.table[0:1, n * PAGES + g:n * PAGES + g + 1], min_val=0, max_val=79) for g in range(PAGES)]
        if n == 0:
            sp.wait_ge(sem["b_head"], 2 * i)
        for h in range(2):
            if n:
                sp.wait_ge(sem["r_done"], R_PAIR * i + r_keys(n - 1, 2 * h + 1) + 1)
            for g in range(4):
                sp.dma_start(k.kb[h][:, g, :], keys[bass.ds(page[4 * h + g], 1), :, bass.ds(col, 2 * P)]
                             .rearrange("o t c -> (o t) c")).then_inc(sem[f"k_landed{h}"], 16)
        for h in range(2):
            if n:
                sp.wait_ge(sem["x_done"], X_PAIR * i + x_sample(n - 1) + 1)
            for g in range(4):
                sp.dma_start(k.vb[h][:, g, :], values[bass.ds(page[4 * h + g], 1), :, bass.ds(col, 2 * P)]
                             .rearrange("o t c -> (o t) c")).then_inc(sem[f"v_landed{h}"], 16)

    def turn(i, final):
        dyn = not isinstance(i, int)
        snap = (lambda v: sp.snap(v)) if dyn else (lambda v: v)
        col = snap(i * 2 * P)
        cols = [snap((i * 2 + h) * P + kind * D) for h in range(2) for kind in range(4)]
        pages(i, 0, col)
        for n in range(2, 8):
            load_slot(sp, k, s0 + 8 * i + n, n % 2, a["b_in_w"][0][:, bass.ds(cols[n], P)])
        if not final:
            for n in range(2):
                load_slot(sp, k, s0 + 8 * i + 8 + n, n, a["b_in_w"][0][:, bass.ds(snap(cols[n] + 2 * P), P)])
        else:
            for n in range(2):
                load_slot(sp, k, s0 + 32 + n, n, a["b_out_w"][0][:, n * P:(n + 1) * P])
        for n in range(1, NB):
            pages(i, n, col)

    with sp.Fori(0, 3) as i:
        turn(i, False)
    turn(3, True)
    out_rest_sync(sp, k, s0 + 32, a["b_out_w"][0])
    for h in range(2):
        if nxt:
            load_slot(sp, k, s0 + 40 + h, h, nxt[h])


def out_rest_sync(sp, k, s, w):
    with sp.Fori(1, KT // 2) as i:
        col = [sp.snap((2 * i + h) * P) for h in range(2)]
        for h in range(2):
            load_slot(sp, k, s + 2 * i + h, h, w[:, bass.ds(col[h], P)])


def b_pool(pool, k, o, chain):
    sem = k.sem
    pool.wait_ge(sem["x_ready"], 2)
    pool.wait_ge(sem["tails_out"], TAILS_OUT)
    for t in [*k.qz, *k.qs, k.negq, k.negs, k.cp, k.qsel]:
        chain(pool.memset(t[:], 0.0))
    chain(pool.affine_select(out=k.negq[:], in_=k.negq[:], compare_op=ALU.is_ge, fill=NEG,
                             base=0, pattern=[[-1, P]], channel_multiplier=1))
    chain(pool.affine_select(out=k.negs[:], in_=k.negs[:], compare_op=ALU.is_ge, fill=NEG,
                             base=0, pattern=[[-1, NS]], channel_multiplier=1))
    blocks = k.negs[:].rearrange("p (b t) -> p b t", b=NB)
    chain(pool.affine_select(out=blocks, in_=blocks, compare_op=ALU.is_ge, fill=NEG,
                             base=DT - 1, pattern=[[DT, NB], [0, DT]], channel_multiplier=-1))
    sel = k.qsel[:].rearrange("p b (c t) -> p b c t", t=DT)
    chain(pool.affine_select(out=sel, in_=sel, compare_op=ALU.not_equal, fill=1.0,
                             base=0, pattern=[[-DT, NB], [0, 8], [-1, DT]], channel_multiplier=1))
    for m in range(2):
        c = k.cp[:, m, :].rearrange("p (h t) -> p h t", h=2)
        chain(pool.affine_select(out=c, in_=c, compare_op=ALU.not_equal, fill=1.0,
                                 base=-DT * m, pattern=[[-32, 2], [-1, DT]], channel_multiplier=1))
    pool.memset(k.ws[:], 0.0).then_inc(sem["b_consts"], 1)
    kp = o["k_prompt"][0, 0].rearrange("(c p) h m d -> p c (h m d)", p=P)
    vp = o["v_prompt"][0, 0].rearrange("(c p) h d -> p c (h d)", p=P)
    ks = o["k_sample"][0].rearrange("b t h m d -> (b t) (h m d)")
    vs = o["v_sample"][0].rearrange("b t h d -> (b t) (h d)")
    for i in range(4):
        cols = slice(i * 2 * P, (i + 1) * 2 * P)
        pool.wait_ge(sem["tok_ready"], i + 1)
        for dst, dst_s, src in ((kp, ks, k.ktok), (vp, vs, k.vtok)):
            pool.dma_start(dst[:, :, cols], src[:, 0:QB].rearrange("p c h d -> p c (h d)")).then_inc(sem["kv_out"], 16)
            pool.dma_start(dst_s[:, cols], src[0:NS, QB].rearrange("p h d -> p (h d)")).then_inc(sem["kv_out"], 16)


def b_tensor(pe, k):
    sem, s0, u0 = k.sem, SLOT_B, USE_B
    pe.wait_ge(sem["x_ready"], 2)
    pe.wait_ge(sem["b_consts"], 1)

    def prompt_scores(i, n):
        h, q = n // 4, n % 4
        may_fill(pe, k, "s", i, s_prompt(n))
        for m in range(2):
            mm = pe.matmul(k.s[:, m, 0:P * (q + 1)], k.qz[h][:, m, q * P:(q + 1) * P], k.kt[h][:, 0:P * (q + 1)],
                           start=True, stop=True)
        mm.then_inc(sem["s_done"], 1)

    def past_keys(i, n):
        for q in range(4):
            if q % 2 == 0:
                pe.wait_ge(sem[f"k_landed{q // 2}"], 64 * (8 * i + n) + 64)
            may_fill(pe, k, "r", i, r_keys(n, q))
            bank = r_keys(n, q) % 2
            for g in range(2):
                for h in range(2):
                    c = (2 * g + h) * P
                    t = pe.transpose(k.r[:, bank, c:c + P], k.kb[q // 2][:, 2 * (q % 2) + g, h * P:(h + 1) * P], k.ident[:])
            t.then_inc(sem["r_done"], 1)

    def sample_output(i, n):
        pe.wait_ge(sem["c_ready"], 8 * i + n + 1)
        may_fill(pe, k, "x", i, x_weights(n))
        for g in range(PAGES):
            pe.matmul(k.x[:, 8 * g:8 * g + 8], k.pps[:, g * P:(g + 1) * P], k.cmat[:], start=True, stop=True)
        mm = pe.matmul(k.x[0:NS, 64:72], k.ppn[:], k.cmat[:], start=True, stop=True)
        mm.then_inc(sem["x_done"], 1)
        may_fill(pe, k, "x", i, x_sample(n))
        for half in range(2):
            pe.wait_ge(sem[f"v_landed{half}"], 64 * (8 * i + n) + 64)
        for h in range(2):
            out = k.x[:, 4 * h:4 * h + 4]
            for g in range(PAGES):
                pe.matmul(out, k.vb[g // 4][:, g % 4, h * P:(h + 1) * P], k.ws[:, 8 * g + 4 * h:8 * g + 4 * h + 4],
                          start=g == 0, stop=False)
            mm = pe.matmul(out, k.vtok[0:NS, QB, h, :], k.ws[0:NS, 64 + 4 * h:68 + 4 * h], start=False, stop=True)
        mm.then_inc(sem["x_done"], 1)

    def sample_scores(i, n):
        may_fill(pe, k, "s", i, s_sample(n))
        for q in range(2):
            last = r_keys(n, 2 + q)
            pe.wait_ge(sem[f"r_read{last % 2}"], R_PAIR // 2 * i + last // 2 + 1)
        for half in range(2):
            for h in range(2):
                mm = pe.matmul(k.s[32 * h:32 * h + 32, half, :], k.qs[h][:, n, :],
                               k.kts[:, h, 4 * half:4 * half + 4, :], start=True, stop=True)
        mm.then_inc(sem["s_done"], 1)
        may_fill(pe, k, "x", i, x_new(n))
        for h in range(2):
            out = k.x[32 * h:32 * h + 32, 0:NS]
            pe.matmul(out, k.qs[h][:, n, :], k.kt[h][:, SEQ:T], start=True, stop=False)
            mm = pe.matmul(out, k.qsel[:, n, :], k.negs[:], start=False, stop=True)
        mm.then_inc(sem["x_done"], 1)

    def prompt_output(i, n):
        h, q = n // 4, n % 4
        pe.wait_ge(sem["w_ready"], 8 * i + n + 1)
        f = r_weights(n)
        may_fill(pe, k, "r", i, f)
        for g in range(q + 1):
            t = pe.transpose(k.r[:, f % 2, g * P:(g + 1) * P], k.pp[:, 0, g * P:(g + 1) * P], k.ident[:])
        t.then_inc(sem["r_done"], 1)
        pe.wait_ge(sem[f"r_read{f % 2}"], R_PAIR // 2 * i + f // 2 + 1)
        may_fill(pe, k, "x", i, x_prompt(n))
        for g in range(q + 1):
            mm = pe.matmul(k.x[:, 0:P], k.vtok[:, g, h, :], k.wt[:, g, :], start=g == 0, stop=g == q)
        mm.then_inc(sem["x_done"], 1)

    with pe.Fori(0, 4) as i:
        for n in range(8):
            multiply_slot(pe, k, s0 + 8 * i + n, n % 2, u0 + 8 * i + n, u0 // 2 + 4 * i + n // 2, n % 2, k.xh, k.xl)
        pe.wait_ge(sem["p_evac0"], u0 // 2 + 4 * i + 4)
        pe.wait_ge(sem["p_evac1"], u0 // 2 + 4 * i + 4)
        pe.wait_ge(sem["s_evac"], u0 + 8 * i + 8)
        may_fill(pe, k, "x", i, 0)
        for c in range(4):
            src = (k.kt, k.vt)[c % 2][c // 2]
            may_fill(pe, k, "r", i, r_turn(c))
            for g in range(QB):
                t = pe.transpose(k.r[:, c % 2, g * P:(g + 1) * P], src[:, g * P:(g + 1) * P], k.ident[:])
            t.then_inc(sem["r_done"], 1)
            t = pe.transpose(k.x[0:NS, c * P:(c + 1) * P], src[:, SEQ:T], k.ident[:])
        t.then_inc(sem["x_done"], 1)
        pe.wait_ge(sem["tok_ready"], i + 1)
        for n in range(9):
            if n < 8:
                prompt_scores(i, n)
                past_keys(i, n)
            if n:
                sample_output(i, n - 1)
            if n < 8:
                sample_scores(i, n)
                prompt_output(i, n)
        for h in range(2):
            pe.wait_ge(sem["o_squared"], 2 * i + h + 1)
            may_fill(pe, k, "s", i, s_rms(h))
            pe.matmul(k.s[:, 0, :], k.ones_d[:], k.sq[h][:, 0, 0:SEQ], start=True, stop=True)
            mm = pe.matmul(k.s[:, 1, 0:NS], k.ones_d[:], k.sq[h][:, 0, SEQ:T], start=True, stop=True)
            mm.then_inc(sem["s_done"], 1)
    pe.wait_ge(sem["b_head"], 8)
    out_tensor(pe, k, s0 + 32, u0 + 32)
    ln_tensor(pe, k, 1)


def b_scalar(act, k, chain):
    sem, s0, u0 = k.sem, SLOT_B, USE_B
    act.wait_ge(sem["b_consts"], 1)
    act.wait_ge(sem["lam_in"], 1)
    act.activation(k.lam[:, 0:2], k.lam[:, 0:2], ACT.Exp).then_inc(sem["lam_exp"], 1)

    def keys_copy(i, n, q):
        f = r_keys(n, q)
        if q == 0:
            act.wait_ge(sem["s_done"], S_PAIR * i + s_sample(n - 1) + 1) if n else None
        await_fill(act, k, "r", i, f)
        act.activation(k.kts[:, :, 2 * q:2 * q + 2, :].rearrange("p h g c -> p g h c"),
                       k.r[:, f % 2, :].rearrange("p (g h c) -> p g h c", g=2, h=2), ACT.Copy).then_inc(sem[f"r_read{f % 2}"], 1)

    with chain.loop("b", 4) as i:
        for n in range(8):
            h, kind = n // 4, n % 4
            par, half = (n + 1) % 2, s0 // 2 + 4 * i + (n + 1) // 2
            split_high(act, k, s0 + 8 * i + n + 1, half, par)
            if kind == 1:
                continue
            await_slot(act, k, s0 + 8 * i + n)
            if kind == 0:
                for m in range(2):
                    lo = slice(64 * m, 64 * m + 64)
                    step = act.activation(k.qz[h][lo, m, :], k.proj[lo, 0, :], ACT.Copy, scale=DH ** -0.5)
                    chain(step) if m == 0 else step.then_inc(sem["p_evac0"], 1)
                for m in range(2):
                    lo = slice(64 * m, 64 * m + 64)
                    step = act.activation(k.qs[h][lo, :, 4 * m:4 * m + 4], k.proj_s[lo, 0:NS].rearrange("p (b t) -> p b t", b=NB),
                                          ACT.Copy, scale=DH ** -0.5)
                    chain(step) if m == 0 else step.then_inc(sem["s_evac"], 1)
            elif kind == 2:
                act.wait_ge(sem["b_head"], 2 * i)
                act.activation(k.vt[h][:, 0:SEQ], k.proj[:, 0, :], ACT.Copy).then_inc(sem["p_evac0"], 1)
                act.activation(k.vt[h][:, SEQ:T], k.proj_s[:, 0:NS], ACT.Copy).then_inc(sem["s_evac"], 1)
            else:
                if h:
                    act.wait_ge(sem["s_evac"], u0 + 8 * i + 4)
                chain(act.activation(k.tgb[:, 0:SEQ], k.proj[:, 1, :], ACT.Tanh, scale=0.5))
                act.activation(k.tgb[:, SEQ:T], k.proj_s[:, 0:NS], ACT.Tanh, scale=0.5).then_inc(sem["tgb_ready"], 1)
        for n in range(8):
            q = n % 4
            keys_copy(i, n, 0)
            act.wait_ge(sem["pm_ready"], 8 * i + n + 1)
            for m in range(2):
                step = act.activation(k.pp[:, m, 0:P * (q + 1)], k.s[:, m, 0:P * (q + 1)], ACT.Exp,
                                      bias=k.pm[:, m:m + 1], accum_out=k.pl[:, m:m + 1])
                chain(step) if m == 0 else step.then_inc(sem["s_read"], 1)
            keys_copy(i, n, 2)
            f = r_weights(n)
            if n:
                act.wait_ge(sem["x_done"], X_PAIR * i + x_prompt(n - 1) + 1)
            await_fill(act, k, "r", i, f)
            act.activation(k.wt[:, 0:q + 1, :], k.r[:, f % 2, 0:P * (q + 1)].rearrange("p (g c) -> p g c", c=P),
                           ACT.Copy).then_inc(sem[f"r_read{f % 2}"], 1)
            if n:
                act.wait_ge(sem["x_done"], X_PAIR * i + x_weights(n - 1) + 1)
            act.wait_ge(sem["sm_ready"], 8 * i + n + 1)
            chain(act.activation(k.ppn[:], k.ppn[:], ACT.Exp, bias=k.st[:, 2:3], accum_out=k.st[:, 4:5]))
            act.activation(k.pps[:], k.s[0:64, :, :].rearrange("p b c -> p (b c)"), ACT.Exp, bias=k.st[:, 2:3],
                           accum_out=k.st[:, 3:4]).then_inc(sem["s_read"], 1)
        for h in range(2):
            act.wait_ge(sem["x_read"], X_PAIR * i + X_PAIR)
            act.activation(k.sq[h][:, 0, :], k.ot[h][:], ACT.Square).then_inc(sem["o_squared"], 1)
        for h in range(2):
            await_fill(act, k, "s", i, s_rms(h))
            if h:
                act.wait_ge(sem["b_head"], 2 * i + 1)
            chain(act.activation(k.rs[:, 0:SEQ], k.s[:, 0, :], ACT.Sqrt, bias=k.eps[:], scale=float(D // P)))
            act.activation(k.rs[:, SEQ:T], k.s[:, 1, 0:NS], ACT.Sqrt, bias=k.eps[:], scale=float(D // P)).then_inc(sem["s_read"], 1)
    out_scalar(act, k, s0 + 32, chain, 1 == k.last)
    ln_scalar(act, k, 1, chain)


def b_vector(dve, k, chain):
    sem, s0, u0 = k.sem, SLOT_B, USE_B
    dve.wait_ge(sem["b_consts"], 1)
    dve.wait_ge(sem["b_params"], 32)
    lam = k.blam[:].rearrange("p (a c d) -> p a c d", a=2, c=2)
    chain(dve.tensor_tensor(lam[:, :, 0, :], lam[:, :, 0, :], lam[:, :, 1, :], ALU.mult))
    dve.tensor_reduce(k.lam[:, 0:2], lam[:, :, 0, :], AX.X, ALU.add).then_inc(sem["lam_in"], 1)
    dve.wait_ge(sem["lam_exp"], 1)
    chain(dve.tensor_tensor(k.lam[:, 2:3], k.lam[:, 1:2], k.lam[:, 0:1], ALU.subtract))
    chain(dve.tensor_scalar(k.lam[:, 3:4], k.lam[:, 2:3], LAM_INIT, None, ALU.subtract))
    chain(dve.tensor_scalar(k.cp[:, 1, :], k.cp[:, 1, :], k.lam[0:64, 3:4], None, ALU.mult))
    chain(dve.tensor_tensor(k.cp[:, 2, :], k.cp[:, 0, :], k.cp[:, 1, :], ALU.add))
    chain(dve.tensor_scalar(k.subw[:], k.subw[:], 0.5 * (1.0 - LAM_INIT), None, ALU.mult))

    def keys_copy(i, n, q):
        f = r_keys(n, q)
        await_fill(dve, k, "r", i, f)
        if n:
            dve.wait_ge(sem["s_done"], S_PAIR * i + s_sample(n - 1) + 1)
        dve.tensor_copy(k.kts[:, :, 2 * q:2 * q + 2, :].rearrange("p h g c -> p g h c"),
                        k.r[:, f % 2, :].rearrange("p (g h c) -> p g h c", g=2, h=2)).then_inc(sem[f"r_read{f % 2}"], 1)

    def sample_output(i, n):
        await_fill(dve, k, "x", i, x_weights(n))
        chain(dve.tensor_copy(k.ws[:, 0:64], k.x[:, 0:64]))
        dve.tensor_copy(k.ws[0:NS, 64:72], k.x[0:NS, 64:72]).then_inc(sem["x_read"], 1)
        await_fill(dve, k, "x", i, x_sample(n))
        at = SEQ + DT * n
        chain(dve.tensor_copy(k.ot[0][:, at:at + DT], k.x[:, 0:DT]))
        dve.tensor_copy(k.ot[1][:, at:at + DT], k.x[:, DT:2 * DT]).then_inc(sem["x_read"], 1)

    with chain.loop("b", 4) as i:
        for n in range(8):
            h, kind = n // 4, n % 4
            split_low(dve, k, s0 + 8 * i + n + 1, (n + 1) % 2)
            if kind == 1:
                await_slot(dve, k, s0 + 8 * i + n)
                dve.tensor_copy(k.kt[h][:, 0:SEQ], k.proj[:, 1, :]).then_inc(sem["p_evac1"], 1)
                dve.tensor_copy(k.kt[h][:, SEQ:T], k.proj_s[:, 0:NS]).then_inc(sem["s_evac"], 1)
            if kind == 3:
                dve.wait_ge(sem["tgb_ready"], 2 * i + h + 1)
                dve.scalar_tensor_tensor(k.sgb[h][:, 0:SEQ], k.tgb[:, 0:SEQ], 1.0, k.proj[:, 1, :], ALU.add, ALU.mult).then_inc(sem["p_evac1"], 1)
                dve.scalar_tensor_tensor(k.sgb[h][:, SEQ:T], k.tgb[:, SEQ:T], 1.0, k.proj_s[:, 0:NS], ALU.add, ALU.mult).then_inc(sem["s_evac"], 1)
        dve.wait_ge(sem["kv_out"], 64 * i)
        for c in range(4):
            await_fill(dve, k, "r", i, r_turn(c))
            dve.tensor_copy((k.ktok, k.vtok)[c % 2][:, 0:QB, c // 2, :],
                            k.r[:, c % 2, :].rearrange("p (g d) -> p g d", g=QB)).then_inc(sem[f"r_read{c % 2}"], 1)
        await_fill(dve, k, "x", i, 0)
        new = k.x[0:NS, :].rearrange("p (h c d) -> p h c d", h=2, c=2)
        chain(dve.tensor_copy(k.ktok[0:NS, QB], new[:, :, 0, :]))
        dve.tensor_copy(k.vtok[0:NS, QB], new[:, :, 1, :]).then_inc(sem["x_read"], 1)
        dve.wait_ge(sem["x_read"], X_PAIR * i + 1)
        for b in range(2):
            dve.wait_ge(sem[f"r_read{b}"], R_PAIR // 2 * i + 2)
        chain(dve.memset(k.st[:, 5:6], 0.0))
        dve.sem_inc(sem["tok_ready"], 1)
        for n in range(8):
            q = n % 4
            await_fill(dve, k, "s", i, s_prompt(n))
            diagonal = k.s[:, :, q * P:(q + 1) * P]
            chain(dve.tensor_tensor(diagonal, diagonal, k.negq[:].unsqueeze(1).broadcast_to([P, 2, P]), ALU.add))
            chain(dve.tensor_reduce(k.pm[:], k.s[:, :, 0:P * (q + 1)], AX.X, ALU.max))
            dve.tensor_scalar(k.pm[:], k.pm[:], -1.0, None, ALU.mult).then_inc(sem["pm_ready"], 1)
            keys_copy(i, n, 1)
            keys_copy(i, n, 3)
            dve.wait_ge(sem["s_read"], S_PAIR * i + s_prompt(n) + 1)
            chain(dve.reciprocal(k.pl[:], k.pl[:]))
            chain(dve.tensor_scalar(k.pl[:, 1:2], k.pl[:, 1:2], k.lam[:, 3:4], None, ALU.mult))
            w0, w1 = k.pp[:, 0, 0:P * (q + 1)], k.pp[:, 1, 0:P * (q + 1)]
            chain(dve.tensor_scalar(w0, w0, k.pl[:, 0:1], None, ALU.mult))
            dve.scalar_tensor_tensor(w0, w1, k.pl[:, 1:2], w0, ALU.mult, ALU.add).then_inc(sem["w_ready"], 1)
            if n:
                sample_output(i, n - 1)
            await_fill(dve, k, "s", i, s_sample(n))
            chain(dve.tensor_reduce(k.st[:, 0:1], k.s[0:64, :, :], AX.XY, ALU.max))
            await_fill(dve, k, "x", i, x_new(n))
            if n:
                dve.wait_ge(sem["x_done"], X_PAIR * i + x_weights(n - 1) + 1)
            dve.tensor_copy(k.ppn[:], k.x[0:64, 0:NS]).then_inc(sem["x_read"], 1)
            dve.wait_ge(sem["x_read"], X_PAIR * i + x_new(n) + 1)
            chain(dve.tensor_reduce(k.st[:, 1:2], k.ppn[:], AX.X, ALU.max))
            chain(dve.tensor_tensor(k.st[:, 2:3], k.st[:, 0:1], k.st[:, 1:2], ALU.max))
            dve.tensor_scalar(k.st[:, 2:3], k.st[:, 2:3], -1.0, None, ALU.mult).then_inc(sem["sm_ready"], 1)
            await_fill(dve, k, "x", i, x_prompt(n))
            dve.tensor_copy(k.ot[n // 4][:, q * P:(q + 1) * P], k.x[:, 0:P]).then_inc(sem["x_read"], 1)
            dve.wait_ge(sem["s_read"], S_PAIR * i + s_sample(n) + 1)
            chain(dve.tensor_tensor(k.st[:, 5:6], k.st[:, 3:4], k.st[:, 4:5], ALU.add))
            chain(dve.reciprocal(k.st[:, 5:6], k.st[:, 5:6]))
            dve.tensor_scalar(k.cmat[:], k.cp[:, 2, :], k.st[:, 5:6], None, ALU.mult).then_inc(sem["c_ready"], 1)
        sample_output(i, 7)
        for h in range(2):
            dve.wait_ge(sem["s_read"], S_PAIR * i + s_rms(h) + 1)
            dve.wait_ge(sem["x_read"], X_PAIR * i + X_PAIR)
            chain(dve.reciprocal(k.rs[:], k.rs[:]))
            chain(dve.scalar_tensor_tensor(k.ot[h][:], k.ot[h][:], k.subw[:], k.rs[:], ALU.mult, ALU.mult))
            chain(dve.tensor_tensor(k.ot[h][:], k.ot[h][:], k.sgb[h][:], ALU.mult))
            high = k.gh[:, bass.ds(2 * i + h, 1), :].rearrange("p o t -> p (o t)")
            low = k.gl[:, bass.ds(2 * i + h, 1), :].rearrange("p o t -> p (o t)")
            chain(dve.tensor_scalar(high, k.ot[h][:], 1.0, None, ALU.mult))
            dve.tensor_tensor(low, k.ot[h][:], high, ALU.subtract).then_inc(sem["b_head"], 1)
            dve.wait_ge(sem["b_head"], 2 * i + h + 1)
    out_vector(dve, k, s0 + 32, u0 + 32, chain, 1 == k.last)
    ln_vector(dve, k, 1, chain)



CS_TURN, CR_TURN, CX_TURN = 12, 14, 5


def cs_tok(n):
    return n


def cs_sums(c):
    return 3 + c


def cs_state(n):
    return 8 + n


CR_TOK = 0


def cr_scores(c):
    return (1, 2, 4, 6, 9)[c]


def cr_update(c):
    return (3, 5, 7, 8)[c]


def cr_state(n):
    return 10 + n


def c_filled(eng, k, bank, g, local):
    per = {"s": CS_TURN, "r": CR_TURN, "x": CX_TURN}[bank]
    eng.wait_ge(k.sem[f"c{bank}_done"], per * g + local + 1)


def c_read(k, bank, local):
    return k.sem["cx_read" if bank == "x" else f"c{bank}_read{local % 2}"]


def c_was_read(eng, k, bank, g, local):
    per = {"s": CS_TURN, "r": CR_TURN, "x": CX_TURN}[bank]
    if bank == "x":
        eng.wait_ge(k.sem["cx_read"], per * g + local + 1)
    else:
        eng.wait_ge(k.sem[f"c{bank}_read{local % 2}"], per // 2 * g + local // 2 + 1)


def c_may_fill(pe, k, bank, g, local):
    per = {"s": CS_TURN, "r": CR_TURN, "x": CX_TURN}[bank]
    if bank == "x":
        pe.wait_ge(k.sem["cx_read"], per * g + local)
    else:
        pe.wait_ge(k.sem[f"c{bank}_read{local % 2}"], per // 2 * g + local // 2)


def layer_c_buffers(k):
    k.gh2 = k.sb("gh2", [P, KT, T], F32R)
    k.gl2 = k.sb("gl2", [P, KT, T], F32R)
    flat = k.xT[:].rearrange("p i t -> p (i t)")
    at = [0]

    def view(n):
        at[0] += n
        return flat[:, at[0] - n:at[0]]

    k.st0 = view(2 * NB * STATE).rearrange("p (j b n) -> p j b n", j=2, b=NB)
    k.btok = view(CH * STATE).rearrange("p (c n) -> p c n", c=CH)
    k.xtok = view(CH * 2 * P).rearrange("p (c q) -> p c q", c=CH)
    k.dt, k.adt, k.cs, k.dec = (k.sb(n, [P, CH, SSDH]) for n in ("dt", "adt", "cs", "dec"))
    k.dt_g, k.adt_g, k.cs_g, k.dec_g = (k.sb(n, [P, CH, HPG]) for n in ("dt_g", "adt_g", "cs_g", "dec_g"))
    k.wdt = k.sb("w_dt", [P, KT, SSDH])
    k.rowp = k.sb("row_params", [P, 3, SSDH])
    k.dsk = k.sb("d_skip", [P, CT])
    k.curc = view(4 * 29).rearrange("p (n c) -> p n c", n=4)
    k.feat = [k.sb(n, [P, T]) for n in ("b_feat", "c_feat", "x_feat0", "x_feat1")]
    k.cc, k.th = k.sb("cc", [P, T]), k.sb("th", [P, T])
    k.sz = [k.sb(f"sz{j}", [P, T]) for j in range(2)]
    k.xdt, k.xdd = k.sb("xdt", [P, 2 * P]), k.sb("xdd", [P, 2 * P])
    k.dm, k.e, k.m = (k.sb(n, [P, HPG, P]) for n in ("dm", "e", "m"))
    k.edec = k.sb("edec", [P, HPG])
    k.decp = k.sb("decp", [P, 2, NB])
    k.ht = view(2 * P)
    k.hout = k.sb("h_out", [P, 2, P])
    k.hts = [k.sb(f"h_sample{j}", [P, 4, P]) for j in range(2)]
    k.bm = k.sq[0].rearrange("p a t -> p (a t)")[0:NS, 0:NB * STATE].rearrange("p (b n) -> p b n", b=NB)
    k.acc = k.sb("acc", [P, T])
    k.negc = k.sb("mask_c", [P, P])
    k.negcs = k.sb("mask_cs", [NS, NS])
    k.tris = k.sb("tri_s", [NS, NS])
    k.blk = k.sb("block_s", [NS, NS])
    k.ctails = k.sb("c_tails", [P, CONV_C // P, HN])


def c_cols(g, n):
    return [INNER * 2 + P * g, INNER * 2 + GROUPS * STATE + P * g, INNER + 2 * P * g, INNER + 2 * P * g + P,
            2 * P * g, 2 * P * g + P][n]


def c_sync(sp, k, a, nxt):
    sem, s0, w = k.sem, SLOT_C, a["c_in_w"][0]
    sp.wait_ge(sem["x_ready"], 3)
    sp.dma_start(k.wdt[:], w[:, INNER + CONV_C:].rearrange("(k p) n -> p k n", p=P)).then_inc(sem["c_params"], 16)
    for n, v in enumerate((a["c_dt_bias"], a["c_a_log"], a["c_d"])):
        sp.dma_start(k.rowp[:, n, :], v.broadcast_to([P, SSDH])).then_inc(sem["c_params"], 16)
    states = a["state_ssd_h"][0].rearrange("b (q j h) p n -> q j (h p) b n", j=2, h=2)
    with sp.Fori(1, GROUPS) as following:
        g = following - 1
        c_turn_sync(sp, k, g, states, w, [sp.snap(c_cols(following, n) - (c_cols(1, n) - c_cols(0, n))) for n in range(6)],
                    [sp.snap(c_cols(following, n)) for n in range(2)])
    g = GROUPS - 1
    c_turn_sync(sp, k, g, states, w, [c_cols(g, n) for n in range(6)], None)
    ow = a["c_out_w"][0]
    for n in range(2):
        load_slot(sp, k, SLOT_C + 48 + n, n, ow[n * D:(n + 1) * D, 0:P])
    with sp.Fori(1, KT) as m:
        col = sp.snap(m * P)
        for n in range(2):
            load_slot(sp, k, SLOT_C + 48 + 2 * m + n, n, ow[n * D:(n + 1) * D, bass.ds(col, P)])
    for h in range(2):
        if nxt:
            load_slot(sp, k, SLOT_C + 64 + h, h, nxt[h])


def c_turn_sync(sp, k, g, states, w, cols, nxt):
    sem = k.sem
    sp.wait_ge(sem["dt_made"], 1)
    sp.wait_ge(sem["st_out"], 32 * g)
    for j in range(2):
        sp.dma_start(k.st0[:, j], states[bass.ds(g, 1), j].rearrange("o p b n -> (o p) b n")).then_inc(sem["st_landed"], 16)
    for n in range(2, 6):
        load_slot(sp, k, SLOT_C + 6 * g + n, n % 2, w[:, bass.ds(cols[n], P)])
    for n in range(2):
        if nxt:
            load_slot(sp, k, SLOT_C + 6 * g + 6 + n, n, w[:, bass.ds(nxt[n], P)])


def c_pool(pool, k, o, chain):
    sem = k.sem
    pool.wait_ge(sem["x_ready"], 3)
    for t, v in ((k.negc, 0.0), (k.negcs, 0.0), (k.tris, 1.0), (k.blk, 1.0), (k.acc, 0.0), (k.dt, 0.0), (k.cs, 0.0), (k.dec, 0.0)):
        chain(pool.memset(t[:], v))
    chain(pool.affine_select(out=k.negc[:], in_=k.negc[:], compare_op=ALU.is_ge, fill=NEG,
                             base=0, pattern=[[1, P]], channel_multiplier=-1))
    for t, fill, causal in ((k.negcs, NEG, True), (k.tris, 0.0, True), (k.blk, 0.0, False)):
        v = t[:].rearrange("p (b t) -> p b t", b=NB)
        chain(pool.affine_select(out=v, in_=v, compare_op=ALU.is_ge, fill=fill, base=0,
                                 pattern=[[-DT, NB], [0, DT]], channel_multiplier=1))
        if causal:
            chain(pool.affine_select(out=t[:], in_=t[:], compare_op=ALU.is_ge, fill=fill, base=0,
                                     pattern=[[1, NS]], channel_multiplier=-1))
        else:
            chain(pool.affine_select(out=v, in_=v, compare_op=ALU.is_ge, fill=fill, base=DT - 1,
                                     pattern=[[DT, NB], [0, DT]], channel_multiplier=-1))
    pool.memset(k.edec[:], 0.0).then_inc(sem["c_consts"], 1)
    hp = o["ssd_h_prompt"][0, 0].rearrange("(g j h) p n -> g (h p) j n", j=2, h=2)
    hs = o["ssd_h_sample"][0].rearrange("b (q j h) p n -> q j (h p) b n", j=2, h=2)
    for g in range(GROUPS):
        pool.wait_ge(sem["hout_ready"], g + 1)
        pool.dma_start(hp[g], k.hout[:]).then_inc(sem["hp_out"], 16)
        pool.wait_ge(sem["st_ready"], g + 1)
        for j in range(2):
            pool.dma_start(hs[g, j], k.st0[:, j]).then_inc(sem["st_out"], 16)
        for j in range(2):
            pool.wait_ge(sem["g_squared"], 2 * g + j + 1)
            pool.tensor_tensor(k.acc[:], k.acc[:], k.sq[1][:, j, :], ALU.add).then_inc(sem["acc_added"], 1)
            pool.wait_ge(sem["acc_added"], 2 * g + j + 1)
    pool.wait_ge(sem["ctails_read"], 1)
    cp = o["ssd_conv_prompt"][0, 0].rearrange("n (u r p) -> n u r p", r=4, p=P)
    cs = o["ssd_conv_sample"][0].rearrange("b n (u r p) -> (b n) u r p", r=4, p=P)
    for r in range(4):
        src = k.rows[1][HN * r:HN * r + HN, :].rearrange("n (u p) -> n u p", p=P)
        pool.dma_start(cp[:, :, r, :], src[0:HIST]).then_inc(sem["ctails_out"], 16)
        pool.dma_start(cs[:, :, r, :], src[HIST:HN]).then_inc(sem["ctails_out"], 16)


def c_tensor(pe, k):
    sem, s0, u0 = k.sem, SLOT_C, USE_C
    pe.wait_ge(sem["x_ready"], 3)
    pe.wait_ge(sem["c_consts"], 1)
    pe.wait_ge(sem["c_params"], 64)
    for c in range(CH):
        n = P if c < QB else NS
        for i in range(KT):
            mm = pe.matmul(k.x[0:n, c * SSDH:(c + 1) * SSDH], k.xT[:, i, c * P:c * P + n], k.wdt[:, i, :],
                           start=i == 0, stop=i == KT - 1)
    mm.then_inc(sem["dt_raw"], 1)
    pe.wait_ge(sem["adt_ready"], 1)
    prompt, sample = k.adt[:, 0:QB, :], k.adt[0:NS, QB, :]
    pe.matmul(k.s[:, 0, 0:P], k.tri[:], prompt, start=True, stop=True)
    pe.matmul(k.s[0:NS, 0, P:P + SSDH], k.tris[:], sample, start=True, stop=True)
    pe.matmul(k.s[:, 1, 0:P], k.ones_d[:], prompt, start=True, stop=True)
    pe.matmul(k.s[0:NS, 1, P:P + SSDH], k.blk[:], sample, start=True, stop=True).then_inc(sem["sums_done"], 1)
    pe.wait_ge(sem["dt_made"], 1)

    def sums(g, c):
        f = cs_sums(c)
        c_may_fill(pe, k, "s", g, f)
        n, tri = (P, k.tri) if c < QB else (NS, k.tris)
        for r in range(HPG):
            mm = pe.matmul(k.s[:, f % 2, r * n:(r + 1) * n], k.adt_g[0:n, c, r:r + 1].broadcast_to([n, P]), tri[:],
                           start=True, stop=True)
        mm.then_inc(sem["cs_done"], 1)
        f, cols = cr_scores(c), slice(c * P, c * P + n)
        c_may_fill(pe, k, "r", g, f)
        mm = pe.matmul(k.r[0:n, f % 2, 0:n], k.feat[0][:, cols], k.feat[1][:, cols], start=True, stop=True)
        if c == QB:
            c_was_read(pe, k, "r", g, cr_update(QB - 1))
            for j in range(2):
                mm = pe.transpose(k.r[:, f % 2, P + j * P:2 * P + j * P], k.ht[:, j * P:(j + 1) * P], k.ident[:])
        mm.then_inc(sem["cr_done"], 1)

    def outputs(g, c):
        pe.wait_ge(sem["y_in"], 5 * g + c + 1)
        c_may_fill(pe, k, "x", g, c)
        if c:
            c_was_read(pe, k, "r", g, cr_update(c - 1))
        for r in range(HPG):
            out = k.x[64 * (r % 2):64 * (r % 2) + 64, r // 2 * P:r // 2 * P + P]
            pe.matmul(out, k.xdt[:, 64 * r:64 * r + 64], k.m[:, r, :], start=True, stop=False)
            mm = pe.matmul(out, k.ht[:, 64 * r:64 * r + 64], k.e[:, r, :], start=False, stop=True)
        mm.then_inc(sem["cx_done"], 1)
        f = cr_update(c)
        c_may_fill(pe, k, "r", g, f)
        pe.matmul(k.r[:, f % 2, 0:2 * P], k.btok[:, c, :], k.xdd[:], start=True, stop=True).then_inc(sem["cr_done"], 1)

    def sample_outputs(g):
        def old_states(n):
            f = cr_state(n)
            c_may_fill(pe, k, "r", g, f)
            for b in range(2):
                for j in range(2):
                    t = pe.transpose(k.r[:, f % 2, (2 * b + j) * P:(2 * b + j + 1) * P], k.st0[:, j, 2 * n + b, :], k.ident[:])
            t.then_inc(sem["cr_done"], 1)
        pe.wait_ge(sem["st_landed"], 32 * g + 32)
        old_states(0)
        pe.wait_ge(sem["y_in"], 5 * g + QB + 1)
        c_may_fill(pe, k, "x", g, QB)
        for r in range(HPG):
            out = k.x[64 * (r % 2):64 * (r % 2) + 64, r // 2 * P:r // 2 * P + NS]
            pe.matmul(out, k.xdt[0:NS, 64 * r:64 * r + 64], k.m[0:NS, r, 0:NS], start=r < 2, stop=False, skip_group_check=True)
        for n in range(4):
            if n < 3:
                old_states(n + 1)
            c_was_read(pe, k, "r", g, cr_state(n))
            for b in range(2):
                for r in range(HPG):
                    at = (2 * n + b) * DT
                    out = k.x[64 * (r % 2):64 * (r % 2) + 64, r // 2 * P + at:r // 2 * P + at + DT]
                    mm = pe.matmul(out, k.hts[n % 2][:, 2 * b + r // 2, 64 * (r % 2):64 * (r % 2) + 64],
                                   k.e[:, r, at:at + DT], start=False, stop=n == 3 and b == 1, skip_group_check=True)
            if n == 3:
                mm.then_inc(sem["cx_done"], 1)
            else:
                mm.then_inc(sem["hts_used"], 1)
        for n in range(4):
            f = cs_state(n)
            c_may_fill(pe, k, "s", g, f)
            pe.matmul(k.s[:, f % 2, :], k.xdd[0:NS, n // 2 * P:n // 2 * P + P], k.bm[:, n % 2 * 4:n % 2 * 4 + 4, :],
                      start=True, stop=True).then_inc(sem["cs_done"], 1)

    with pe.Fori(0, GROUPS) as g:
        for n in range(6):
            multiply_slot(pe, k, s0 + 6 * g + n, n % 2, u0 + 6 * g + n, u0 // 2 + 3 * g + n // 2, n % 2, k.xh, k.xl)
            if n == 1:
                pe.wait_ge(sem["feat_ready"], 4 * g + 1)
        for n in range(3):
            src = (k.feat[0], k.feat[2], k.feat[3])[n]
            pe.wait_ge(sem["feat_ready"], 4 * g + (1, 3, 4)[n])
            c_may_fill(pe, k, "s", g, cs_tok(n))
            if n == 0:
                c_may_fill(pe, k, "r", g, CR_TOK)
            for c in range(QB):
                t = pe.transpose(k.s[:, n % 2, c * P:(c + 1) * P], src[:, c * P:(c + 1) * P], k.ident[:])
            t.then_inc(sem["cs_done"], 1)
            t = pe.transpose(k.r[0:NS, 0, n * P:(n + 1) * P], src[:, SEQ:T], k.ident[:])
        t.then_inc(sem["cr_done"], 1)
        pe.wait_ge(sem["group_params"], g + 1)
        sums(g, 0)
        for c in range(CH):
            if c < QB:
                if c < QB - 1:
                    sums(g, c + 1)
                outputs(g, c)
                if c == QB - 1:
                    sums(g, QB)
            else:
                sample_outputs(g)
    pe.wait_ge(sem["acc_added"], 2 * GROUPS)
    pe.matmul(k.s[:, 0, :], k.ones_d[:], k.acc[:, 0:SEQ], start=True, stop=True)
    pe.matmul(k.s[:, 1, 0:NS], k.ones_d[:], k.acc[:, SEQ:T], start=True, stop=True).then_inc(sem["ms_done"], 1)
    for u in range(8):
        t = pe.transpose(k.r[0:4 * HN, u // 4, (u % 4) * P:(u % 4) * P + P],
                         k.ctails[:, 4 * u:4 * u + 4, :].rearrange("p i c -> p (i c)"), k.ident[:])
    t.then_inc(sem["ctails_turned"], 1)
    pe.wait_ge(sem["g_ready"], 2 * GROUPS)
    s, u = s0 + 48, u0 + 48
    with pe.Fori(0, KT // 2) as i:
        for h in range(2):
            for n in range(2):
                multiply_slot(pe, k, s + 4 * i + 2 * h + n, n, u + 2 * i + h, u // 2 + i, h,
                              (k.gh, k.gh2)[n], (k.gl, k.gl2)[n], first=n == 0, last=n == 1)
    ln_tensor(pe, k, 2)


def c_scalar(act, k, chain):
    sem, s0, u0 = k.sem, SLOT_C, USE_C
    act.wait_ge(sem["c_consts"], 1)
    act.wait_ge(sem["c_params"], 64)
    softplus_scalar(act, k, k.spa[:], 2)
    act.activation(k.rowp[:, 1, :], k.rowp[:, 1, :], ACT.Exp).then_inc(sem["a_exp"], 1)
    act.wait_ge(sem["dec_in"], 1)
    act.activation(k.dec[:], k.dec[:], ACT.Exp).then_inc(sem["dt_made"], 1)
    with chain.loop("c", GROUPS) as g:
        for n in range(6):
            split_high(act, k, s0 + 6 * g + n + 1, s0 // 2 + 3 * g + (n + 1) // 2, (n + 1) % 2)
            await_slot(act, k, s0 + 6 * g + n)
            if n < 4:
                act.wait_ge(sem["c_conv"], 4 * g + n)
                act.activation(k.u[:, HIST:SROW], k.proj[:, n % 2, :], ACT.Copy).then_inc(sem[f"p_evac{n % 2}"], 1)
                act.activation(k.u_s[:, :, HIST:WIN], k.proj_s[:, 0:NS].rearrange("p (b t) -> p b t", b=NB),
                               ACT.Copy).then_inc(sem["s_evac"], 1)
                act.wait_ge(sem["c_conv"], 4 * g + n + 1)
                act.activation(k.th[:], k.cc[:], ACT.Tanh).then_inc(sem["c_tanh"], 1)
            else:
                if n == 4:
                    act.wait_ge(sem["feat_ready"], 4 * g + 4)
                else:
                    act.wait_ge(sem["s_evac"], u0 + 6 * g + 5)
                chain(act.activation(k.th[:, 0:SEQ], k.proj[:, n % 2, :], ACT.Tanh, scale=0.5))
                act.activation(k.th[:, SEQ:T], k.proj_s[:, 0:NS], ACT.Tanh, scale=0.5).then_inc(sem["c_tanh"], 1)
        for n, f in ((1, cs_tok(1)), (2, cs_tok(2))):
            c_filled(act, k, "s", g, f)
            act.activation(k.xtok[:, 0:QB, (n - 1) * P:n * P], k.s[:, f % 2, :].rearrange("p (c q) -> p c q", c=QB),
                           ACT.Copy).then_inc(c_read(k, "s", f), 1)
        for c in range(CH):
            f, m = cs_sums(c), P if c < QB else NS
            act.wait_ge(sem["dm_ready"], 5 * g + c + 1)
            chain(act.activation(k.dm[0:m, :, 0:m], k.dm[0:m, :, 0:m], ACT.Exp))
            if c:
                c_filled(act, k, "x", g, c - 1)
            act.activation(k.e[:, :, 0:m], k.s[:, f % 2, 0:HPG * m].rearrange("p (r l) -> p r l", r=HPG),
                           ACT.Exp).then_inc(c_read(k, "s", f), 1)
        for n in range(4):
            f = cr_state(n)
            c_filled(act, k, "r", g, f)
            if n >= 2:
                act.wait_ge(sem["hts_used"], 3 * g + n - 1)
            act.activation(k.hts[n % 2][:].rearrange("p q n -> p (q n)"), k.r[:, f % 2, :], ACT.Copy).then_inc(c_read(k, "r", f), 1)
        for j in range(2):
            act.wait_ge(sem["g_made"], 2 * g + j + 1)
            act.wait_ge(sem["acc_added"], 2 * g)
            act.activation(k.sq[1][:, j, :], k.feat[2 + j][:], ACT.Square).then_inc(sem["g_squared"], 1)
    act.wait_ge(sem["ms_done"], 1)
    chain(act.activation(k.rs[:, 0:SEQ], k.s[:, 0, :], ACT.Sqrt, bias=k.eps[:], scale=D / INNER))
    act.activation(k.rs[:, SEQ:T], k.s[:, 1, 0:NS], ACT.Sqrt, bias=k.eps[:], scale=D / INNER).then_inc(sem["c_rms"], 1)
    s = s0 + 48

    def body(i, final):
        for n in range(4):
            if not (final and n == 3 and k.last == 2):
                split_high(act, k, s + 4 * i + n + 1, s // 2 + 2 * i + (n + 1) // 2, (n + 1) % 2)
    turns_of(chain, "c_out", KT // 2, body, peel=True)
    act.wait_ge(sem["ctails_out"], 128)
    ln_scalar(act, k, 2, chain)


def c_vector(dve, k, chain):
    sem, s0, u0 = k.sem, SLOT_C, USE_C
    dve.wait_ge(sem["c_consts"], 1)
    dve.wait_ge(sem["c_params"], 64)
    chain(dve.tensor_scalar(k.par_c[:, :, 0:5], k.par_c[:, :, 0:5], 0.5, None, ALU.mult))
    for r in range(2):
        chain(dve.tensor_copy(k.dsk[64 * r:64 * r + 64, :], k.rowp[64 * r:64 * r + 64, 2, r::2]))
    dve.wait_ge(sem["dt_raw"], 1)
    bias = k.rowp[:, 0, :].unsqueeze(1)
    chain(dve.tensor_tensor(k.dt[:, 0:QB], k.x[:, 0:P].rearrange("p (c h) -> p c h", c=QB), bias.broadcast_to([P, QB, SSDH]), ALU.add))
    chain(dve.tensor_tensor(k.dt[0:NS, QB], k.x[0:NS, P:P + SSDH], k.rowp[0:NS, 0, :], ALU.add))
    flat = [t[:].rearrange("p c h -> p (c h)") for t in (k.dt, k.adt)]
    softplus_vector(dve, k, chain, flat[0], flat[1], k.spa[:], 2)
    chain(dve.tensor_copy(k.dt[:], k.adt[:]))
    dve.wait_ge(sem["a_exp"], 1)
    chain(dve.tensor_scalar(k.rowp[:, 1, :], k.rowp[:, 1, :], -1.0, None, ALU.mult))
    dve.tensor_tensor(k.adt[:], k.dt[:], k.rowp[:, 1:2, :].broadcast_to([P, CH, SSDH]), ALU.mult).then_inc(sem["adt_ready"], 1)
    dve.wait_ge(sem["sums_done"], 1)
    chain(dve.tensor_copy(k.cs[:, 0:QB], k.s[:, 0, 0:P].rearrange("p (c h) -> p c h", c=QB)))
    chain(dve.tensor_copy(k.cs[0:NS, QB], k.s[0:NS, 0, P:P + SSDH]))
    chain(dve.scalar_tensor_tensor(k.dec[:, 0:QB], k.s[:, 1, 0:P].rearrange("p (c h) -> p c h", c=QB), float(D), k.cs[:, 0:QB],
                                   ALU.mult, ALU.subtract))
    dve.tensor_tensor(k.dec[0:NS, QB], k.s[0:NS, 1, P:P + SSDH], k.cs[0:NS, QB], ALU.subtract).then_inc(sem["dec_in"], 1)
    dve.wait_ge(sem["dt_made"], 1)

    def turn(half, i):
        g = 4 * half + i
        for n, tile in enumerate((CT + g, CT + GROUPS + g, 2 * g, 2 * g + 1)):
            chain(dve.tensor_scalar(k.curc[:, n, :], k.par_c[:, bass.ds(tile, 1), :].rearrange("p o c -> p (o c)"), 1.0, None, ALU.mult))
        for dst, src in ((k.dt_g, k.dt), (k.adt_g, k.adt), (k.cs_g, k.cs)):
            chain(dve.tensor_scalar(dst[:], src[:, :, bass.ds(HPG * g, HPG)], 1.0, None, ALU.mult))
        dve.tensor_scalar(k.dec_g[:], k.dec[:, :, bass.ds(HPG * g, HPG)], 1.0, None, ALU.mult).then_inc(sem["group_params"], 1)
        dve.wait_ge(sem["group_params"], g + 1)
        for n in range(6):
            if n == 0:
                chain(dve.memset(k.ht[:], 0.0))
            if n < 4:
                cur = k.curc[:, n, :]
                chain(dve.tensor_copy(k.u_s[:, :, 0:HIST], cur[:, 5:29].rearrange("p (b t) -> p b t", b=NB)))
            split_low(dve, k, s0 + 6 * g + n + 1, (n + 1) % 2)
            dve.wait_ge(sem["s_evac"] if n < 4 else sem["c_tanh"], u0 + 6 * g + n + 1 if n < 4 else 6 * g + n + 1)
            if n < 4:
                dve.wait_ge(sem[f"p_evac{n % 2}"], u0 // 2 + 3 * g + n // 2 + 1)
                tile = (CT + g, CT + GROUPS + g, 2 * g, 2 * g + 1)[n]
                tail = k.ctails[:, bass.ds(tile, 1), :].rearrange("p o c -> p (o c)")
                chain(dve.tensor_scalar(tail[:, 0:HIST], k.u[:, SEQ:SROW], 1.0, None, ALU.mult))
                chain(dve.tensor_scalar(tail[:, HIST:HN].rearrange("p (b t) -> p b t", b=NB), k.u_s[:, :, DT:WIN], 1.0, None, ALU.mult))
                convolve(dve, k, chain, cur, k.cc, "c_conv")
                dve.wait_ge(sem["c_tanh"], 6 * g + n + 1)
                dve.scalar_tensor_tensor(k.feat[n][:], k.th[:], 1.0, k.cc[:], ALU.add, ALU.mult).then_inc(sem["feat_ready"], 1)
                dve.wait_ge(sem["feat_ready"], 4 * g + n + 1)
            else:
                sz = k.sz[n - 4]
                dve.scalar_tensor_tensor(sz[:, 0:SEQ], k.th[:, 0:SEQ], 1.0, k.proj[:, n % 2, :], ALU.add, ALU.mult).then_inc(sem[f"p_evac{n % 2}"], 1)
                dve.scalar_tensor_tensor(sz[:, SEQ:T], k.th[:, SEQ:T], 1.0, k.proj_s[:, 0:NS], ALU.add, ALU.mult).then_inc(sem["s_evac"], 1)
        c_filled(dve, k, "s", g, cs_tok(0))
        dve.tensor_copy(k.btok[:, 0:QB], k.s[:, 0, :].rearrange("p (c n) -> p c n", c=QB)).then_inc(c_read(k, "s", 0), 1)
        c_filled(dve, k, "r", g, CR_TOK)
        chain(dve.tensor_copy(k.btok[0:NS, QB], k.r[0:NS, 0, 0:P]))
        dve.tensor_copy(k.xtok[0:NS, QB], k.r[0:NS, 0, P:3 * P]).then_inc(c_read(k, "r", CR_TOK), 1)
        c_was_read(dve, k, "s", g, cs_tok(0))
        c_was_read(dve, k, "r", g, CR_TOK)
        for n in (1, 2):
            c_was_read(dve, k, "s", g, cs_tok(n))
        chain(dve.tensor_tensor(k.bm, k.btok[0:NS, QB:CH].broadcast_to([NS, NB, STATE]),
                                k.blk[:, 0:NS:DT].unsqueeze(2).broadcast_to([NS, NB, STATE]), ALU.mult))

        def differences(c):
            n, mask, f = (P, k.negc, cs_sums(c)) if c < QB else (NS, k.negcs, cs_sums(c))
            c_filled(dve, k, "s", g, f)
            for r in range(HPG):
                step = dve.scalar_tensor_tensor(k.dm[0:n, r, 0:n], k.s[0:n, f % 2, r * n:r * n + n], k.cs_g[0:n, c, r:r + 1],
                                                mask[:], ALU.subtract, ALU.add)
                chain(step) if r < HPG - 1 else step.then_inc(sem["dm_ready"], 1)

        for c in range(CH):
            n = P if c < QB else NS
            cols = slice(c * P, c * P + n)
            differences(c)
            if c:
                c_filled(dve, k, "x", g, c - 1)
                c_filled(dve, k, "r", g, cr_update(c - 1))
            x3 = k.xtok[0:n, c].rearrange("p (r q) -> p r q", r=HPG)
            xdt, xdd = (t[0:n].rearrange("p (r q) -> p r q", r=HPG) for t in (k.xdt, k.xdd))
            chain(dve.tensor_tensor(xdt, x3, k.dt_g[0:n, c].unsqueeze(2).broadcast_to([n, HPG, HD]), ALU.mult))
            chain(dve.tensor_tensor(xdd, xdt, k.dec_g[0:n, c].unsqueeze(2).broadcast_to([n, HPG, HD]), ALU.mult))
            f = cs_sums(c)
            c_was_read(dve, k, "s", g, f)
            f = cr_scores(c)
            c_filled(dve, k, "r", g, f)
            step = dve.tensor_tensor(k.m[0:n, :, 0:n], k.dm[0:n, :, 0:n], k.r[0:n, f % 2, 0:n].unsqueeze(1).broadcast_to([n, HPG, n]), ALU.mult)
            if c < QB:
                step.then_inc(c_read(k, "r", f), 1)
                chain(dve.tensor_copy(k.edec[:], k.e[:, :, P - 1]))
            else:
                chain(step)
                dve.wait_ge(sem["hp_out"], 16 * g)
                dve.tensor_copy(k.hout[:], k.r[:, f % 2, P:3 * P].rearrange("p (j n) -> p j n", j=2)).then_inc(c_read(k, "r", f), 1)
                c_was_read(dve, k, "r", g, f)
                for h in range(2):
                    lo = slice(64 * h, 64 * h + 64)
                    chain(dve.tensor_copy(k.decp[lo], k.e[lo, h:HPG:2, DT - 1:NS:DT]))
                dve.sem_inc(sem["hout_ready"], 1)
            dve.tensor_tensor(k.e[:, :, 0:n], k.e[:, :, 0:n], k.feat[1][:, cols].unsqueeze(1).broadcast_to([P, HPG, n]),
                              ALU.mult).then_inc(sem["y_in"], 1)
            c_filled(dve, k, "x", g, c)
            for j in range(2):
                t = k.feat[2 + j][:, cols]
                step = dve.scalar_tensor_tensor(t, t, k.dsk[:, bass.ds(2 * g + j, 1)], k.x[:, j * P:j * P + n], ALU.mult, ALU.add)
                chain(step) if j == 0 else step.then_inc(sem["cx_read"], 1)
            if c < QB:
                f = cr_update(c)
                c_filled(dve, k, "r", g, f)
                h3 = k.ht[:].rearrange("p (r q) -> p r q", r=HPG)
                chain(dve.tensor_tensor(h3, h3, k.edec[:].unsqueeze(2).broadcast_to([P, HPG, HD]), ALU.mult))
                dve.tensor_tensor(k.ht[:], k.ht[:], k.r[:, f % 2, 0:2 * P], ALU.add).then_inc(c_read(k, "r", f), 1)
                c_was_read(dve, k, "r", g, f)
        for n in range(4):
            f = cs_state(n)
            c_filled(dve, k, "s", g, f)
            for b in range(4):
                at = n % 2 * 4 + b
                h = k.st0[:, n // 2, at, :]
                step = dve.scalar_tensor_tensor(h, h, k.decp[:, n // 2, at:at + 1], k.s[:, f % 2, b * P:(b + 1) * P], ALU.mult, ALU.add)
                chain(step) if b < 3 else step.then_inc(c_read(k, "s", f), 1)
            c_was_read(dve, k, "s", g, f)
        dve.sem_inc(sem["st_ready"], 1)
        c_was_read(dve, k, "x", g, QB)
        for j in range(2):
            t = k.feat[2 + j][:]
            dve.scalar_tensor_tensor(t, t, 0.5, k.sz[j][:], ALU.mult, ALU.mult).then_inc(sem["g_made"], 1)
            dve.wait_ge(sem["g_made"], 2 * g + j + 1)
            dve.wait_ge(sem["g_squared"], 2 * g + j + 1)
            chain(dve.tensor_scalar(t, t, k.par_m[:, bass.ds(2 * i + j, 1), 8 + half].rearrange("p o -> p o"), None, ALU.mult))
            high, low = (t2[:, bass.ds(2 * i + j, 1), :].rearrange("p o t -> p (o t)") for t2 in ((k.gh, k.gl), (k.gh2, k.gl2))[half])
            chain(dve.tensor_scalar(high, t, 1.0, None, ALU.mult))
            dve.tensor_tensor(low, t, high, ALU.subtract).then_inc(sem["g_ready"], 1)
            dve.wait_ge(sem["g_ready"], 2 * g + j + 1)

    for half in range(2):
        with chain.loop("c", 4) as i:
            turn(half, i)
    dve.wait_ge(sem["ctails_turned"], 1)
    dve.tensor_copy(k.rows[1][0:4 * HN, :].rearrange("p (b c) -> p b c", b=2), k.r[0:4 * HN]).then_inc(sem["ctails_read"], 1)
    dve.wait_ge(sem["c_rms"], 1)
    chain(dve.reciprocal(k.rs[:], k.rs[:]))
    dve.wait_ge(sem["st_out"], 32 * GROUPS)
    s, u = s0 + 48, u0 + 48

    def body(i, final):
        for h in range(2):
            for n in range(2):
                if not (final and h == 1 and n == 1 and k.last == 2):
                    split_low(dve, k, s + 4 * i + 2 * h + n + 1, 1 - n)
            await_slot(dve, k, s + 4 * i + 2 * h + 1)
            dve.tensor_tensor(k.cc[:, 0:SEQ], k.proj[:, h, :], k.rs[:, 0:SEQ], ALU.mult).then_inc(sem[f"p_evac{h}"], 1)
            dve.tensor_tensor(k.cc[:, SEQ:T], k.proj_s[:, 0:NS], k.rs[:, SEQ:T], ALU.mult).then_inc(sem["s_evac"], 1)
            dve.wait_ge(sem[f"p_evac{h}"], u // 2 + i + 1)
            dve.wait_ge(sem["s_evac"], u + 2 * i + h + 1)
            x, high, low = (t[:, bass.ds(2 * i + h, 1), :].rearrange("p o t -> p (o t)") for t in (k.xT, k.xh, k.xl))
            chain(dve.tensor_tensor(x, high, low, ALU.add))
            dve.scalar_tensor_tensor(x, x, ALPHA, k.cc[:], ALU.mult, ALU.add).then_inc(sem["c_x"], 1)
            dve.wait_ge(sem["c_x"], 2 * i + h + 1)
    turns_of(chain, "c_out", KT // 2, body, peel=True)
    ln_vector(dve, k, 2, chain)



USE_END = [24, 64, 120, 144]


def out_sync(sp, k, s, w):
    with sp.Fori(0, KT // 2) as i:
        col = [sp.snap((2 * i + h) * P) for h in range(2)]
        for h in range(2):
            load_slot(sp, k, s + 2 * i + h, h, w[:, bass.ds(col[h], P)])


def out_tensor(pe, k, s, u):
    with pe.Fori(0, KT // 2) as i:
        for h in range(2):
            multiply_slot(pe, k, s + 2 * i + h, h, u + 2 * i + h, u // 2 + i, h, k.gh, k.gl)


def out_scalar(act, k, s, chain, last):
    def body(i, final):
        split_high(act, k, s + 2 * i + 1, s // 2 + i, 1)
        if not (final and last):
            split_high(act, k, s + 2 * i + 2, s // 2 + i + 1, 0)
    turns_of(chain, "out", KT // 2, body, peel=True)


def out_vector(dve, k, s, u, chain, last):
    def body(i, final):
        for h in range(2):
            if h == 0 or not (final and last):
                split_low(dve, k, s + 2 * i + h + 1, 1 - h)
            await_slot(dve, k, s + 2 * i + h)
            x = k.xT[:, bass.ds(2 * i + h, 1), :].rearrange("p o t -> p (o t)")
            dve.scalar_tensor_tensor(x[:, 0:SEQ], x[:, 0:SEQ], ALPHA, k.proj[:, h, :], ALU.mult, ALU.add).then_inc(k.sem[f"p_evac{h}"], 1)
            dve.scalar_tensor_tensor(x[:, SEQ:T], x[:, SEQ:T], ALPHA, k.proj_s[:, 0:NS], ALU.mult, ALU.add).then_inc(k.sem["s_evac"], 1)
    turns_of(chain, "out", KT // 2, body, peel=True)


def ln_tensor(pe, k, layer):
    sem, u = k.sem, USE_END[layer]
    for h in range(2):
        pe.wait_ge(sem[f"p_evac{h}"], u // 2)
    pe.wait_ge(sem["s_evac"], u)
    if layer == 2:
        pe.wait_ge(sem["c_x"], KT)
    for i in range(KT):
        pe.matmul(k.s[:, 0, :], k.ones_d[:], k.xT[:, i, 0:SEQ], start=i == 0, stop=i == KT - 1)
    for i in range(KT):
        mm = pe.matmul(k.r[:, 0, 0:NS], k.ones_d[:], k.xT[:, i, SEQ:T], start=i == 0, stop=i == KT - 1)
    mm.then_inc(sem["ln_mean"], 1)
    for i in range(KT):
        if i % 2 == 0:
            pe.wait_ge(sem["ln_sq"], 4 * layer + i // 2 + 1)
        pe.matmul(k.s[:, 1, :], k.ones_d[:], k.sq[i // 2 % 2][:, i % 2, 0:SEQ], start=i == 0, stop=i == KT - 1)
        mm = pe.matmul(k.r[:, 1, 0:NS], k.ones_d[:], k.sq[i // 2 % 2][:, i % 2, SEQ:T], start=i == 0, stop=i == KT - 1)
        if i % 2:
            mm.then_inc(sem["ln_acc"], 1)


def ln_scalar(act, k, layer, chain):
    sem = k.sem
    for j in range(KT // 2):
        act.wait_ge(sem["ln_sub"], 4 * layer + j + 1)
        if 4 * layer + j >= 2:
            act.wait_ge(sem["ln_acc"], 4 * layer + j - 1)
        act.activation(k.sq[j % 2][:], k.xT[:, 2 * j:2 * j + 2, :], ACT.Square).then_inc(sem["ln_sq"], 1)
    act.wait_ge(sem["ln_acc"], 4 * layer + 4)
    chain(act.activation(k.rs[:, 0:SEQ], k.s[:, 1, :], ACT.Sqrt, bias=k.eps[:]))
    act.activation(k.rs[:, SEQ:T], k.r[:, 1, 0:NS], ACT.Sqrt, bias=k.eps[:]).then_inc(sem["ln_sd"], 1)
    for i in range(KT):
        act.wait_ge(sem["ln_norm"], 8 * layer + i + 1)
        bias = k.par_m[:, i, 4 + layer:5 + layer]
        act.activation(k.xT[:, i, :], k.xT[:, i, :], ACT.Identity, bias=bias).then_inc(sem["ln_x"], 1)
        if layer < k.last:
            act.wait_ge(sem["ln_x"], 8 * layer + i + 1)
            act.activation(k.xh[:, i, :], k.xT[:, i, :], ACT.Copy).then_inc(sem["ln_xh"], 1)


def ln_vector(dve, k, layer, chain):
    sem = k.sem
    dve.wait_ge(sem["ln_mean"], layer + 1)
    for j in range(KT // 2):
        x = k.xT[:, 2 * j:2 * j + 2, :]
        chain(dve.tensor_tensor(x[:, :, 0:SEQ], x[:, :, 0:SEQ], k.s[:, 0:1, :].broadcast_to([P, 2, SEQ]), ALU.subtract))
        dve.tensor_tensor(x[:, :, SEQ:T], x[:, :, SEQ:T], k.r[:, 0:1, 0:NS].broadcast_to([P, 2, NS]),
                          ALU.subtract).then_inc(sem["ln_sub"], 1)
    dve.wait_ge(sem["ln_sd"], layer + 1)
    chain(dve.reciprocal(k.rs[:], k.rs[:]))
    dve.wait_ge(sem["ln_sub"], 4 * layer + 4)

    def low(i):
        dve.wait_ge(sem["ln_xh"], 8 * layer + i + 1)
        sub = dve.tensor_tensor(k.xl[:, i, :], k.xT[:, i, :], k.xh[:, i, :], ALU.subtract)
        chain(sub) if i < KT - 1 else sub.then_inc(sem["x_ready"], 1)

    for i in range(KT + 1):
        if i < KT:
            dve.scalar_tensor_tensor(k.xT[:, i, :], k.xT[:, i, :], k.par_m[:, i, layer:layer + 1], k.rs[:],
                                     ALU.mult, ALU.mult).then_inc(sem["ln_norm"], 1)
        if i and layer < k.last:
            low(i - 1)



def y_tensor(pe, k, layer):
    pe.wait_ge(k.sem["ln_x"], 8 * layer + 8)
    for c in range(CH):
        n = P if c < QB else NS
        bank = (k.s, k.r)[c % 2]
        if c >= 2:
            pe.wait_ge(k.sem[f"y_read{c % 2}"], c // 2)
        for i in range(KT):
            t = pe.transpose(bank[0:n, i // 4, (i % 4) * P:(i % 4) * P + P], k.xT[:, i, c * P:c * P + n], k.ident[:, :])
        t.then_inc(k.sem["y_turned"], 1)


def y_copy(eng, k, c, op):
    n = P if c < QB else NS
    eng.wait_ge(k.sem["y_turned"], c + 1)
    if c >= 2:
        eng.wait_ge(k.sem[f"y_out{c % 2}"], 16 * (c // 2))
    op(k.rows[c % 2][0:n, :].rearrange("p (b c) -> p b c", b=2), (k.s, k.r)[c % 2][0:n, :, :]).then_inc(k.sem[f"y_read{c % 2}"], 1)


def y_sync(sp, k, o):
    for c in range(CH):
        n = P if c < QB else NS
        dst = o["y_prompt"][0, c * P:(c + 1) * P, :] if c < QB else o["y_sample"].rearrange("b t d -> (b t) d")
        sp.wait_ge(k.sem[f"y_read{c % 2}"], c // 2 + 1)
        sp.dma_start(dst, k.rows[c % 2][0:n, :]).then_inc(k.sem[f"y_out{c % 2}"], 16)
    sp.wait_ge(k.sem["y_out0"], 48)
    sp.wait_ge(k.sem["y_out1"], 32)



def layer_a_buffers(k):
    k.cur = k.sb("cur", [P, 43])
    k.gw = k.sb("gate_w", [P, 2, P])
    k.tg, k.tr, k.ti, k.t, k.rt = (k.sb(n, [P, T]) for n in ("tg", "tr", "ti", "t", "rt"))
    k.sg, k.q, k.a, k.gi, k.h, k.cx = (k.sb(n, [P, T]) for n in ("sg", "q", "a", "gi", "h", "cx"))
    k.h0a = k.sb("h0a", [P, NB])
    k.tails_sb = k.sb("tails_sb", [P, 3 * P])
    k.tails = k.sb("tails", [P, KT, AN])


def conv_buffers(k):
    k.u = k.sb("u", [P, UW])
    k.u_s = k.u[:, SROW:UW].rearrange("p (b t) -> p b t", b=NB)
    conv = k.sb("conv", [P, UW])
    k.conv_s = conv[:, SROW:UW].rearrange("p (b t) -> p b t", b=NB)
    k.conv = conv[:, 0:CW]


def scoped(nc, k, make):
    with ExitStack() as ctx:
        k.sb = lambda name, shape, dtype=F32: ctx.enter_context(nc.sbuf_tensor(name, shape, dtype))
        make(k)


def build(nc, a, o):
    with ExitStack() as ctx:
        k = allocate(nc, ctx)
        k.last = DEPTH - 1
        k.par_c = k.sb("par_c", [P, CONV_C // P, 29])
        k.par_d = [k.sb(f"par_d{j}", [P, 3, KT]) for j in range(2)]
        k.spx, k.spy = k.sb("spx", [P, 2 * KT]), k.sb("spy", [P, 2 * KT])
        k.spa = k.rs[:, 0:3 * CH * SSDH].rearrange("p (a n) -> p a n", a=3)
        conv_buffers(k)
        scoped(nc, k, layer_a_buffers)
        scoped(nc, k, layer_b_buffers)
        scoped(nc, k, layer_c_buffers)
        block = ctx.enter_context(nc.Block())

        @block.sync
        def _(sp):
            prologue_sync(sp, k, a)
            a_sync(sp, k, a, 0, [b_cols(a, 0, 0), b_cols(a, 1, 0)])
            b_sync(sp, k, a, [a["c_in_w"][0][:, c_cols(0, n):c_cols(0, n) + P] for n in range(2)])
            c_sync(sp, k, a, [a_slot(a, 1, n) for n in range(2)])
            a_sync(sp, k, a, 1, None)
            y_sync(sp, k, o)

        @block.gpsimd
        def _(pool):
            chain = Chain(pool, k.sem["chain_pool"], STEPS, "pool")
            prologue_pool(pool, k, chain)
            tails_stores(pool, k, a, o, 0)
            b_pool(pool, k, o, chain)
            c_pool(pool, k, o, chain)
            pool.wait_ge(k.sem["ctails_out"], 128)
            pool.wait_ge(k.sem["st_out"], 256)
            pool.wait_ge(k.sem["hp_out"], 128)
            pool.wait_ge(k.sem["x_ready"], 4)
            pool.memset(k.gw[:], 0.0).then_inc(k.sem["consts"], 1)
            tails_stores(pool, k, a, o, 1)
            pool.wait_ge(k.sem["kv_out"], 256)
            pool.wait_ge(k.sem["tails_out"], TAILS_OUT * 2)

        @block.tensor
        def _(pe):
            pe.sem_inc(k.sem["pe_slot"], 1)
            prologue_tensor(pe, k, a)
            a_tensor(pe, k, 0)
            b_tensor(pe, k)
            c_tensor(pe, k)
            a_tensor(pe, k, 1)
            y_tensor(pe, k, k.last)

        @block.scalar
        def _(act):
            chain = Chain(act, k.sem["chain_act"], STEPS, "act")
            prologue_scalar(act, k, a)
            a_scalar(act, k, 0, chain)
            b_scalar(act, k, chain)
            c_scalar(act, k, chain)
            a_scalar(act, k, 1, chain)
            for c in range(0, CH, 2):
                y_copy(act, k, c, lambda d, s: act.activation(d, s, ACT.Copy))

        @block.vector
        def _(dve):
            chain = Chain(dve, k.sem["chain_dve"], STEPS, "dve")
            dve.sem_inc(k.sem["w_lo"], 1)
            prologue_vector(dve, k, a, chain)
            a_vector(dve, k, 0, chain)
            b_vector(dve, k, chain)
            c_vector(dve, k, chain)
            a_vector(dve, k, 1, chain)
            for c in range(1, CH, 2):
                y_copy(dve, k, c, dve.tensor_copy)


INS = """x_prompt x_sample cache_k cache_v page_table state_lru_conv state_lru_h state_ssd_conv state_ssd_h
    ln_g ln_b a_in_w a_conv_w a_conv_b a_gate_r_w a_gate_r_b a_gate_i_w a_gate_i_b a_lambda a_out_w
    b_in_w b_lambda b_subln_w b_out_w c_in_w c_conv_w c_conv_b c_dt_bias c_a_log c_d c_norm_w c_out_w""".split()
OUTS = dict(
    y_prompt=(1, 512, 1024), y_sample=(8, 4, 1024), k_prompt=(1, 1, 512, 8, 2, 64), v_prompt=(1, 1, 512, 8, 128),
    k_sample=(1, 8, 4, 8, 2, 64), v_sample=(1, 8, 4, 8, 128), lru_conv_prompt=(2, 1, 3, 1024),
    lru_h_prompt=(2, 1, 1024), lru_conv_sample=(2, 8, 3, 1024), lru_h_sample=(2, 8, 1024),
    ssd_conv_prompt=(1, 1, 3, 4096), ssd_h_prompt=(1, 1, 32, 64, 128), ssd_conv_sample=(1, 8, 3, 4096),
    ssd_h_sample=(1, 8, 32, 64, 128))


def kernel(**inputs):
    import numpy as np
    import concourse.bacc as bacc
    from concourse.bass_utils import run_bass_kernel_spmd

    nc = bacc.Bacc("TRN2", target_bir_lowering=False, num_devices=1)
    arrays, a, o = {}, {}, {}
    for name in INS:
        arrays[f"in_{name}"] = np.ascontiguousarray(inputs[name])
        a[name] = nc.dram_tensor(f"in_{name}", arrays[f"in_{name}"].shape,
                                 mybir.dt.from_np(arrays[f"in_{name}"].dtype), kind="ExternalInput").ap()
    for name, shape in OUTS.items():
        o[name] = nc.dram_tensor(f"out_{name}", shape, F32, kind="ExternalOutput").ap()
    build(nc, a, o)
    r = run_bass_kernel_spmd(nc, [arrays], core_ids=[0])
    return tuple(r.results[0][f"out_{name}"] for name in OUTS)
```

```python
import math
from contextlib import ExitStack, contextmanager

import concourse.bass as bass
from concourse import mybir

F32 = mybir.dt.float32
F32R = mybir.dt.float32r
I32 = mybir.dt.int32
ALU = mybir.AluOpType
ACT = mybir.ActivationFunctionType
AX = mybir.AxisListType

P = 128
D = 1024
KT = D // P
SEQ, NB, DT = 512, 8, 4
NS = NB * DT
T = SEQ + NS
TAPS = 4
HIST = TAPS - 1
WIN = HIST + DT
UW = HIST + SEQ + NB * WIN
CW = UW - HIST
SROW = HIST + SEQ
HALF = SEQ // 2
DEPTH = 4
ALPHA = (2.0 * DEPTH) ** 0.25
EPS = 1e-5
QB = SEQ // P
CH = QB + 1
HEADS, DH = 8, 64
PAGES, PAGE = 8, 128
GROUPS, HPG, HD, STATE = 8, 4, 64, 128
SSDH = GROUPS * HPG
INNER = SSDH * HD
CT = INNER // P
CONV_C = INNER + 2 * GROUPS * STATE
NEG = -1e30
LAM_INIT = 0.8 - 0.6 * math.exp(-0.3)
HN = HIST + NB * HIST
AN = HN + 1 + NB

TAILS_OUT = 16 * 4 * (3 + 2)

STEPS = {("act", "a"): 6, ("act", "out"): 0, ("act", "b"): 29, ("act", "c"): 11, ("act", "c_out"): 0,
         ("dve", "a"): 18, ("dve", "out"): 0, ("dve", "b"): 106, ("dve", "c"): 98, ("dve", "c_out"): 0}

SLOT_A = [0, 128]
USE_A = [0, 120]
SLOT_B = USE_B = 24
SLOT_C = USE_C = 64


class Chain:

    def __init__(self, eng, sem, steps, engine):
        self.eng, self.sem, self.steps, self.engine = eng, sem, steps, engine
        self.count, self.turn, self.per = 0, None, 0

    def __call__(self, instruction):
        instruction.then_inc(self.sem, 1)
        self.count += 1
        value = self.count if self.turn is None else self.turn * self.per + self.count
        self.eng.wait_ge(self.sem, value)

    @contextmanager
    def loop(self, name, turns):
        start = self.count
        self.per = self.steps[self.engine, name]
        with self.eng.Fori(0, turns) as i:
            self.turn = i
            yield i
            took = self.count - start
        assert took == self.per, (self.engine, name, took)
        self.turn = None
        self.count = start + turns * self.per


def turns_of(chain, name, n, body, peel=False):
    with chain.loop(name, n - peel) as i:
        body(i, False)
    if peel:
        body(n - 1, True)


def tokens_of(ap):
    return ap[:, 0:SEQ], ap[:, SEQ:T]


class Chip:
    pass


def allocate(nc, ctx):
    k = Chip()

    def sb(name, shape, dtype=F32):
        return ctx.enter_context(nc.sbuf_tensor(name, shape, dtype))

    def ps(name, shape):
        return ctx.enter_context(nc.psum_tensor(name, shape, F32))

    k.sb = sb
    k.xT = sb("xT", [P, KT, T])
    k.xh = sb("xh", [P, KT, T], F32R)
    k.xl = sb("xl", [P, KT, T], F32R)
    with nc.sbuf_tensor("branch", [P, CT, T], F32) as k.out:
        pass
    k.g = sb("g", [P, 2 * KT, T], F32R)
    k.gh, k.gl = k.g[:, 0:KT, :], k.g[:, KT:2 * KT, :]
    k.sq = [sb(f"sq{j}", [P, 2, T]) for j in range(2)]
    k.rows = [q.rearrange("p a t -> p (a t)")[:, 0:D] for q in k.sq]
    k.raw = [sb(f"w_raw{j}", [P, KT, P]) for j in range(2)]
    k.wh = [sb(f"w_high{j}", [P, KT, P], F32R) for j in range(2)]
    k.wl = [sb(f"w_low{j}", [P, KT, P], F32R) for j in range(2)]
    k.ident = sb("ident", [P, P])
    k.tri = sb("tri", [P, P])
    k.ones_d = sb("ones_d", [P, P])
    k.eps = sb("eps", [P, 1])
    k.par_a = [sb(f"par_a{j}", [P, KT, 40]) for j in range(2)]
    k.par_m = sb("par_m", [P, KT, 10])
    k.rs = sb("rs", [P, T])

    k.proj = ps("proj", [P, 2, 512])
    k.proj_lo = ps("proj_lo", [P, 512])
    k.s = ps("s", [P, 2, 512])
    k.r = ps("r", [P, 2, 512])
    k.x = ps("x", [P, 512])

    names = """w_landed0 w_landed1 w_hi w_lo pe_slot p_evac0 p_evac1 s_evac x_ready
        rows_landed0 rows_landed1 rows_turned rows_read consts chain_act chain_dve chain_pool
        sp_in sp_out params x_split
        gw_landed  conv_done gates_done a_rest al_ready gi_ready q_in ti_ready t_ready rt_ready tg_ready
        tails_turned tails_read tails_out
        ln_mean ln_sub ln_sq ln_acc ln_sd ln_norm ln_x ln_xh
        table_in b_params b_consts lam_in lam_exp r_done r_read0 r_read1 s_done s_read x_done x_read
        q_ready gates_copied x_back k_landed0 k_landed1 v_landed0 v_landed1 tok_ready kv_out tgb_ready pm_ready w_ready sm_ready
        c_ready o_squared b_head
        c_params c_consts dt_raw adt_ready sums_done a_exp dec_in dt_made st_landed st_ready st_out hout_ready hp_out
        g_squared g_made g_ready g_high g_split acc_added ctails_turned ctails_read ctails_out y_in hts_used feat_ready group_params
        ms_done c_rms c_x c_conv c_tanh dm_ready cs_done cs_read0 cs_read1 cr_done cr_read0 cr_read1 cx_done cx_read
        y_turned y_read0 y_read1 y_out0 y_out1 done""".split()
    k.sem = {}
    for name in names:
        k.sem[name] = ctx.enter_context(nc.semaphore(name))
    return k



def load_slot(sp, k, s, par, rows):
    sp.wait_ge(k.sem["w_lo"], s)
    sp.dma_start(k.raw[par][:], rows.rearrange("(k p) n -> p k n", p=P)).then_inc(k.sem[f"w_landed{par}"], 16)


def split_high(act, k, s, half, par):
    act.wait_ge(k.sem[f"w_landed{par}"], 16 * half + 16)
    act.wait_ge(k.sem["pe_slot"], s)
    act.activation(k.wh[par][:], k.raw[par][:], ACT.Copy).then_inc(k.sem["w_hi"], 1)


def split_low(dve, k, s, par):
    dve.wait_ge(k.sem["w_hi"], s + 1)
    dve.wait_ge(k.sem["pe_slot"], s)
    dve.tensor_tensor(k.wl[par][:], k.raw[par][:], k.wh[par][:], ALU.subtract).then_inc(k.sem["w_lo"], 1)


def multiply_slot(pe, k, s, par, use, use_half, upar, mh, ml, k0=0, first=True, last=True):
    pe.wait_ge(k.sem["w_lo"], s + 2)
    if first:
        pe.wait_ge(k.sem[f"p_evac{upar}"], use_half)
    for cols, out in ((slice(HALF, T), k.proj[:, upar, 0:T - HALF]), (slice(0, HALF), k.proj_lo[:, 0:HALF])):
        if first and cols.start == 0:
            pe.wait_ge(k.sem["s_evac"], use)
        for i in range(KT):
            for n, (w, m) in enumerate(((k.wh, mh), (k.wh, ml), (k.wl, mh))):
                mm = pe.matmul(out, w[par][:, i, :], m[:, k0 + i, cols],
                               start=first and i == 0 and n == 0, stop=last and i == KT - 1 and n == 2)
    mm.then_inc(k.sem["pe_slot"], 1)


def await_slot(eng, k, s):
    eng.wait_ge(k.sem["pe_slot"], s + 2)



def row_jobs(a):
    xp = a["x_prompt"].rearrange("b t d -> (b t) d")
    jobs = [("x", c, P, [(0, P, xp[c * P:(c + 1) * P, :])]) for c in range(QB)]
    jobs.append(("x", QB, NS, [(0, NS, a["x_sample"].rearrange("b t d -> (b t) d"))]))
    for j in range(2):
        one = [a["a_conv_b"], a["a_gate_r_b"], a["a_gate_i_b"], a["a_lambda"]]
        jobs.append(("a", j, 40, [(0, 4, a["a_conv_w"][j])]
                     + [(4 + n, 1, v[j:j + 1, :]) for n, v in enumerate(one)]
                     + [(8, 24, a["state_lru_conv"][j].rearrange("b k d -> (b k) d")),
                        (32, 8, a["state_lru_h"][j])]))
    jobs.append(("m", 0, 10, [(0, 4, a["ln_g"]), (4, 4, a["ln_b"]),
                              (8, 2, a["c_norm_w"].rearrange("a (r d) -> (a r) d", r=2))]))
    for q in range(CONV_C // D):
        cols = slice(q * D, (q + 1) * D)
        jobs.append(("c", q, 29, [(0, 4, a["c_conv_w"][0][:, cols]), (4, 1, a["c_conv_b"][:, cols]),
                                  (5, 24, a["state_ssd_conv"][0].rearrange("b k d -> (b k) d")[:, cols])]))
    return jobs


def prologue_sync(sp, k, a):
    landed = [0, 0]
    for j, (_, _, _, parts) in enumerate(row_jobs(a)):
        if j == 2:
            for s in range(2):
                load_slot(sp, k, s, s, a_slot(a, 0, s))
        if j >= 2:
            sp.wait_ge(k.sem["rows_turned"], j - 1)
        for at, n, src in parts:
            sp.dma_start(k.rows[j % 2][at:at + n, :], src).then_inc(k.sem[f"rows_landed{j % 2}"], 16)


def a_slot(a, j, n):
    col = (1 - n % 2) * D + (n // 2) * P
    return a["a_in_w"][j][:, col:col + P]


def prologue_pool(pool, k, chain):
    sem = k.sem
    for t, v in ((k.ident, 0.0), (k.tri, 1.0), (k.ones_d, 1.0 / D), (k.eps, EPS), (k.gw, 0.0), (k.u, 0.0)):
        chain(pool.memset(t[:], v))
    chain(pool.affine_select(out=k.ident[:], in_=k.ident[:], compare_op=ALU.not_equal, fill=1.0,
                             base=0, pattern=[[-1, P]], channel_multiplier=1))
    pool.affine_select(out=k.tri[:], in_=k.tri[:], compare_op=ALU.is_ge, fill=0.0,
                       base=0, pattern=[[1, P]], channel_multiplier=-1).then_inc(sem["consts"], 1)


def prologue_tensor(pe, k, a):
    sem = k.sem
    pe.wait_ge(sem["consts"], 1)
    landed = [0, 0]
    for j, (_, _, n, parts) in enumerate(row_jobs(a)):
        landed[j % 2] += 16 * len(parts)
        pe.wait_ge(sem[f"rows_landed{j % 2}"], landed[j % 2])
        if j >= 2:
            pe.wait_ge(sem["rows_read"], j - 1)
        bank = (k.s, k.r)[j % 2]
        for i in range(KT):
            t = pe.transpose(bank[:, i // 4, (i % 4) * n:(i % 4) * n + n],
                             k.rows[j % 2][0:n, i * P:(i + 1) * P], k.ident[0:n, 0:n])
        t.then_inc(sem["rows_turned"], 1)


def prologue_vector(dve, k, a, chain):
    sem = k.sem
    dve.wait_ge(sem["consts"], 1)
    for j, (kind, c, n, _) in enumerate(row_jobs(a)):
        dve.wait_ge(sem["rows_turned"], j + 1)
        bank = (k.s, k.r)[j % 2]
        dst = {"x": lambda: k.xT[:, :, c * P:c * P + n], "a": lambda: k.par_a[c][:],
               "m": lambda: k.par_m[:], "c": lambda: k.par_c[:, c * KT:(c + 1) * KT, :]}[kind]()
        dve.tensor_copy(dst.rearrange("p (b i) n -> p b i n", b=2),
                        bank[:, :, 0:4 * n].rearrange("p b (i n) -> p b i n", i=4)).then_inc(sem["rows_read"], 1)
        if j == CH - 1:
            split_low(dve, k, 0, 0)
            dve.wait_ge(sem["x_split"], 1)
            dve.tensor_tensor(k.xl[:], k.xT[:], k.xh[:], ALU.subtract).then_inc(sem["x_ready"], 1)
    dve.wait_ge(sem["rows_read"], len(row_jobs(a)))
    for j in range(2):
        d = k.par_d[j]
        chain(dve.tensor_scalar(d[:, 0:2, :].rearrange("p c i -> p i c"), k.par_a[j][:, :, 5:7], 0.5, None, ALU.mult))
        chain(dve.tensor_scalar(k.spx[:, j * KT:(j + 1) * KT], k.par_a[j][:, :, 7], -1.0, None, ALU.mult))
    softplus_vector(dve, k, chain, k.spx[:], k.spy[:], k.spa[:, :, 0:2 * KT], 1)
    for j in range(2):
        for n, factor in enumerate((4.0, -4.0, -8.0)):
            chain(dve.tensor_scalar(k.par_d[j][:, 2 + n, :], k.spy[:, j * KT:(j + 1) * KT], factor, None, ALU.mult))


def softplus_vector(dve, k, chain, x, y, tmp, call):
    a, s, p = tmp[:, 0], tmp[:, 1], tmp[:, 2]
    chain(dve.tensor_scalar(a, x, -1.0, None, ALU.mult))
    dve.tensor_tensor(a, a, x, ALU.max).then_inc(k.sem["sp_in"], 1)
    dve.wait_ge(k.sem["sp_out"], call)
    chain(dve.tensor_scalar(s, a, 2.0, None, ALU.add))
    chain(dve.reciprocal(s, s))
    chain(dve.tensor_tensor(s, s, a, ALU.mult))
    chain(dve.tensor_tensor(a, s, s, ALU.mult))
    chain(dve.tensor_scalar(p, a, 1.0 / 15, None, ALU.mult))
    for n in (13, 11, 9, 7, 5, 3):
        chain(dve.scalar_tensor_tensor(p, p, 1.0 / n, a, ALU.add, ALU.mult))
    chain(dve.scalar_tensor_tensor(p, p, 1.0, s, ALU.add, ALU.mult))
    chain(dve.tensor_scalar(a, x, 0.0, None, ALU.max))
    chain(dve.scalar_tensor_tensor(y, p, 2.0, a, ALU.mult, ALU.add))


def softplus_scalar(act, k, tmp, call):
    act.wait_ge(k.sem["sp_in"], call)
    act.activation(tmp[:, 0], tmp[:, 0], ACT.Exp, scale=-1.0).then_inc(k.sem["sp_out"], 1)


def prologue_scalar(act, k, a):
    split_high(act, k, 0, 0, 0)
    act.wait_ge(k.sem["rows_read"], CH)
    act.activation(k.xh[:], k.xT[:], ACT.Copy).then_inc(k.sem["x_split"], 1)
    softplus_scalar(act, k, k.spa[:, :, 0:2 * KT], 1)



def a_sync(sp, k, a, j, nxt):
    s0, sem = SLOT_A[j], k.sem
    g_w = [a["a_gate_r_w"][j], a["a_gate_i_w"][j]]

    def gates(i, block):
        sp.wait_ge(sem["gates_done"], 8 * j + i)
        for n in range(2):
            for h in range(2):
                sp.dma_start(k.gw[h * 64:h * 64 + 64, n, h * 64:h * 64 + 64],
                             g_w[n][bass.ds(block[h], 1), :, :].rearrange("o a b -> (o a) b")).then_inc(sem["gw_landed"], 16)

    sp.wait_ge(sem["consts"], 1 + j)
    with sp.Fori(0, KT - 1) as i:
        cols = [sp.snap(i * P + P + D), sp.snap(i * P + P)]
        block = [sp.snap(2 * i), sp.snap(2 * i + 1)]
        for h in range(2):
            load_slot(sp, k, s0 + 2 + 2 * i + h, h, a["a_in_w"][j][:, bass.ds(cols[h], P)])
        gates(i, block)
    gates(KT - 1, [2 * KT - 2, 2 * KT - 1])
    out_sync(sp, k, s0 + 16, a["a_out_w"][j])
    for h in range(2):
        if nxt:
            load_slot(sp, k, s0 + 24 + h, h, nxt[h])


def a_tensor(pe, k, j):
    s0, u0, sem = SLOT_A[j], USE_A[j], k.sem
    pe.wait_ge(sem["x_ready"], 3 * j + 1)
    with pe.Fori(0, KT) as i:
        multiply_slot(pe, k, s0 + 2 * i, 0, u0 + 2 * i, u0 // 2 + i, 0, k.xh, k.xl)
        multiply_slot(pe, k, s0 + 2 * i + 1, 1, u0 + 2 * i + 1, u0 // 2 + i, 1, k.xh, k.xl)
        n = 8 * j + i
        pe.wait_ge(sem["gw_landed"], 64 * n + 64)
        pe.wait_ge(sem["conv_done"], n + 1)
        pe.wait_ge(sem["ti_ready"], n)
        for g in range(2):
            pe.matmul(k.s[:, g, :], k.gw[:, g, :], k.cx[:, 0:SEQ], start=True, stop=True)
        for g in range(2):
            mm = pe.matmul(k.r[:, 0, g * NS:g * NS + NS], k.gw[:, g, :], k.cx[:, SEQ:T], start=True, stop=True)
        mm.then_inc(sem["gates_done"], 1)
    pe.wait_ge(sem["a_rest"], 8 * j + 8)
    for q in range(3):
        n = 3 if q < 2 else 2
        t = pe.transpose(k.x[0:n * AN, q * P:(q + 1) * P], k.tails[:, 3 * q:3 * q + n, :].rearrange("p i c -> p (i c)"), k.ident[:, :])
    t.then_inc(sem["tails_turned"], 1)
    out_tensor(pe, k, s0 + 16, u0 + 16)
    ln_tensor(pe, k, 3 * j)


def row_of_inputs(act, k, par, chain):
    bank = k.proj[:, par]
    act.activation(k.u[:, HIST:HIST + HALF], k.proj_lo[:, 0:HALF], ACT.Copy).then_inc(k.sem["s_evac"], 1)
    chain(act.activation(k.u[:, HIST + HALF:SROW], bank[:, 0:SEQ - HALF], ACT.Copy))
    act.activation(k.u_s[:, :, HIST:WIN], bank[:, SEQ - HALF:T - HALF].rearrange("p (b t) -> p b t", b=NB),
                   ACT.Copy).then_inc(k.sem[f"p_evac{par}"], 1)


def a_scalar(act, k, j, chain):
    s0, u0, sem = SLOT_A[j], USE_A[j], k.sem
    split_high(act, k, s0 + 1, s0 // 2, 1)
    with chain.loop("a", KT) as i:
        n = 8 * j + i
        await_slot(act, k, s0 + 2 * i)
        act.wait_ge(sem["conv_done"], n)
        row_of_inputs(act, k, 0, chain)
        split_high(act, k, s0 + 2 * i + 2, s0 // 2 + i + 1, 0)
        await_slot(act, k, s0 + 2 * i + 1)
        act.wait_ge(sem["s_evac"], u0 + 2 * i)
        chain(act.activation(k.tg[:, HALF:T], k.proj[:, 1, 0:T - HALF], ACT.Tanh, scale=0.5))
        act.activation(k.tg[:, 0:HALF], k.proj_lo[:, 0:HALF], ACT.Tanh, scale=0.5).then_inc(sem["tg_ready"], 1)
        split_high(act, k, s0 + 2 * i + 3, s0 // 2 + i + 1, 1)
        act.wait_ge(sem["gates_done"], n + 1)
        chain(act.activation(k.tr[:, 0:SEQ], k.s[:, 0, :], ACT.Tanh, scale=0.5, bias=k.cur[:, 40:41]))
        chain(act.activation(k.tr[:, SEQ:T], k.r[:, 0, 0:NS], ACT.Tanh, scale=0.5, bias=k.cur[:, 40:41]))
        act.wait_ge(sem["gi_ready"], n)
        chain(act.activation(k.ti[:, 0:SEQ], k.s[:, 1, :], ACT.Tanh, scale=0.5, bias=k.cur[:, 41:42]))
        act.activation(k.ti[:, SEQ:T], k.r[:, 0, NS:2 * NS], ACT.Tanh, scale=0.5,
                       bias=k.cur[:, 41:42]).then_inc(sem["ti_ready"], 1)
        chain(act.activation(k.a2[:], k.tr[:], ACT.Exp, scale=k.cur[:, 44:45], bias=k.cur[:, 44:45]))
        act.activation(k.t[:], k.tr[:], ACT.Tanh, scale=k.cur[:, 42:43], bias=k.cur[:, 42:43]).then_inc(sem["t_ready"], 1)
        act.wait_ge(sem["a_rest"], n)
        act.activation(k.a[:], k.tr[:], ACT.Exp, scale=k.cur[:, 43:44], bias=k.cur[:, 43:44]).then_inc(sem["al_ready"], 1)
        act.wait_ge(sem["q_in"], n + 1)
        act.activation(k.rt[:], k.q[:], ACT.Sqrt, scale=0.25).then_inc(sem["rt_ready"], 1)
    out_scalar(act, k, s0 + 16, chain, 3 * j == k.last, ahead=2)
    ln_scalar(act, k, 3 * j, chain)


def convolve(dve, k, chain, cur, out, done):
    acc = k.conv
    chain(dve.tensor_scalar(acc[:], k.u[:, 0:CW], cur[:, 0:1], cur[:, 4:5], ALU.mult, ALU.add))
    for tap in (1, 2):
        chain(dve.scalar_tensor_tensor(acc[:], k.u[:, tap:tap + CW], cur[:, tap:tap + 1], acc[:], ALU.mult, ALU.add))
    chain(dve.scalar_tensor_tensor(out[:, 0:SEQ], k.u[:, HIST:SROW], cur[:, 3:4], acc[:, 0:SEQ], ALU.mult, ALU.add))
    ends = k.conv_s
    dve.scalar_tensor_tensor(out[:, SEQ:T].rearrange("p (b t) -> p b t", b=NB), k.u_s[:, :, HIST:WIN], cur[:, 3:4],
                             ends[:, :, 0:DT], ALU.mult, ALU.add).then_inc(k.sem[done], 1)


def a_vector(dve, k, j, chain):
    s0, u0, sem = SLOT_A[j], USE_A[j], k.sem
    first = slice(SEQ, T, DT)

    def convolution(i):
        n = 8 * j + i
        dve.wait_ge(sem["al_ready"], n)
        chain(dve.tensor_scalar(k.cur[:, 0:40], k.par_a[j][:, bass.ds(i, 1), :].rearrange("p o c -> p (o c)"), 1.0, None, ALU.mult))
        chain(dve.tensor_scalar(k.cur[:, 40:45], k.par_d[j][:, :, bass.ds(i, 1)].rearrange("p c o -> p (c o)"), 1.0, None, ALU.mult))
        chain(dve.tensor_copy(k.u_s[:, :, 0:HIST], k.cur[:, 8:32].rearrange("p (b t) -> p b t", b=NB)))
        dve.wait_ge(sem["p_evac0"], u0 // 2 + i + 1)
        dve.wait_ge(sem["s_evac"], u0 + 2 * i + 1)
        dve.wait_ge(sem["gates_done"], n)
        tail = k.tails[:, bass.ds(i, 1), :].rearrange("p o c -> p (o c)")
        chain(dve.tensor_scalar(tail[:, 0:HIST], k.u[:, SEQ:SROW], 1.0, None, ALU.mult))
        chain(dve.tensor_scalar(tail[:, HIST:HN].rearrange("p (b t) -> p b t", b=NB), k.u_s[:, :, DT:WIN], 1.0, None, ALU.mult))
        convolve(dve, k, chain, k.cur, k.cx, "conv_done")
        split_low(dve, k, s0 + 2 * i + 2, 0)

    def gates(i):
        n = 8 * j + i
        dve.wait_ge(sem["tg_ready"], n + 1)
        dve.scalar_tensor_tensor(k.sg[:, 0:HALF], k.tg[:, 0:HALF], 1.0, k.proj_lo[:, 0:HALF], ALU.add, ALU.mult).then_inc(sem["s_evac"], 1)
        dve.scalar_tensor_tensor(k.sg[:, HALF:T], k.tg[:, HALF:T], 1.0, k.proj[:, 1, 0:T - HALF], ALU.add, ALU.mult).then_inc(sem["p_evac1"], 1)
        split_low(dve, k, s0 + 2 * i + 3, 1)
        dve.wait_ge(sem["t_ready"], n + 1)
        dve.scalar_tensor_tensor(k.q[:], k.a2[:], 1.0, k.t[:], ALU.add, ALU.mult).then_inc(sem["q_in"], 1)
        dve.wait_ge(sem["ti_ready"], n + 1)
        dve.wait_ge(sem["conv_done"], n + 1)
        dve.scalar_tensor_tensor(k.gi[:], k.ti[:], 1.0, k.cx[:], ALU.add, ALU.mult).then_inc(sem["gi_ready"], 1)
        dve.wait_ge(sem["al_ready"], n + 1)
        chain(dve.tensor_tensor(k.h0a[:], k.a[:, first], k.cur[:, 32:40], ALU.mult))

    def scan(i):
        n = 8 * j + i
        tail = k.tails[:, bass.ds(i, 1), :].rearrange("p o c -> p (o c)")
        dve.wait_ge(sem["rt_ready"], n + 1)
        dve.wait_ge(sem["gi_ready"], n + 1)
        chain(dve.tensor_tensor(k.gi[:], k.gi[:], k.rt[:], ALU.mult))
        chain(dve.tensor_tensor(k.gi[:, first], k.gi[:, first], k.h0a[:], ALU.add))
        chain(dve.memset(k.a[:, first], 0.0))
        chain(dve.tensor_tensor_scan(k.h[:], k.a[:], k.gi[:], 0.0, ALU.mult, ALU.add))
        chain(dve.tensor_scalar(tail[:, HN:HN + 1], k.h[:, SEQ - 1:SEQ], 1.0, None, ALU.mult))
        chain(dve.tensor_scalar(tail[:, HN + 1:AN], k.h[:, SEQ + DT - 1:T:DT], 1.0, None, ALU.mult))
        dve.wait_ge(sem["s_evac"], u0 + 2 * i + 2)
        dve.wait_ge(sem["p_evac1"], u0 // 2 + i + 1)
        chain(dve.scalar_tensor_tensor(k.h[:], k.h[:], 0.5, k.sg[:], ALU.mult, ALU.mult))
        high = k.gh[:, bass.ds(i, 1), :].rearrange("p o t -> p (o t)")
        low = k.gl[:, bass.ds(i, 1), :].rearrange("p o t -> p (o t)")
        chain(dve.tensor_scalar(high, k.h[:], 1.0, None, ALU.mult))
        dve.tensor_tensor(low, k.h[:], high, ALU.subtract).then_inc(sem["a_rest"], 1)
        dve.wait_ge(sem["a_rest"], n + 1)

    split_low(dve, k, s0 + 1, 1)
    convolution(0)
    gates(0)
    with chain.loop("a", KT - 1) as i:
        convolution(i + 1)
        scan(i)
        gates(i + 1)
    scan(KT - 1)
    dve.wait_ge(sem["tails_turned"], 1 + j)
    if j:
        dve.wait_ge(sem["tails_out"], TAILS_OUT)
    dve.tensor_copy(k.tails_sb[0:3 * AN, 0:2 * P], k.x[0:3 * AN, 0:2 * P]).then_inc(sem["tails_read"], 1)
    dve.tensor_copy(k.tails_sb[0:2 * AN, 2 * P:3 * P], k.x[0:2 * AN, 2 * P:3 * P]).then_inc(sem["tails_read"], 1)
    out_vector(dve, k, s0 + 16, u0 + 16, chain, 3 * j == k.last, ahead=2)
    ln_vector(dve, k, 3 * j, chain)


def tails_stores(pool, k, a, o, j):
    pool.wait_ge(k.sem["tails_read"], 2 * j + 2)
    outputs = ((o["lru_conv_prompt"][j, 0], 0, HIST), (o["lru_conv_sample"][j].rearrange("b k d -> (b k) d"), HIST, NB * HIST),
               (o["lru_h_prompt"][j], HN, 1), (o["lru_h_sample"][j], HN + 1, NB))
    for r in range(3):
        for dst, at, rows in outputs:
            row = slice(r * AN + at, r * AN + at + rows)
            pool.dma_start(dst[:, 0:6 * P].rearrange("n (q r p) -> n q r p", q=2, r=3)[:, :, r, :],
                           k.tails_sb[row, 0:2 * P].rearrange("n (q p) -> n q p", q=2)).then_inc(k.sem["tails_out"], 16)
            if r < 2:
                pool.dma_start(dst[:, (6 + r) * P:(7 + r) * P], k.tails_sb[row, 2 * P:3 * P]).then_inc(k.sem["tails_out"], 16)



R_PAIR, S_PAIR, X_PAIR = 44, 18, 33


def r_turn(c):
    return c


def r_keys(n, q):
    return 4 + 5 * n + q


def r_weights(n):
    return 4 + 5 * n + 4


def s_prompt(n):
    return 2 * n


def s_sample(n):
    return 2 * n + 1


def s_rms(h):
    return 16 + h


def x_new(n):
    return 4 * n if n else 1


def x_prompt(n):
    return 4 * n + 2


def x_weights(n):
    return 4 * n + 3


def x_sample(n):
    return 4 * n + 5 if n < 7 else 32


def await_fill(eng, k, bank, i, local):
    per = {"r": R_PAIR, "s": S_PAIR, "x": X_PAIR}[bank]
    eng.wait_ge(k.sem[f"{bank}_done"], per * i + local + 1)


def may_fill(pe, k, bank, i, local):
    if bank == "r":
        pe.wait_ge(k.sem[f"r_read{local % 2}"], R_PAIR // 2 * i + local // 2)
    else:
        pe.wait_ge(k.sem[f"{bank}_read"], {"s": S_PAIR, "x": X_PAIR}[bank] * i + local)


def layer_b_buffers(k):
    k.qz = [k.sb(f"q_split{h}", [P, 2, SEQ]) for h in range(2)]
    k.qs = [k.sb(f"q_sample{h}", [P, NB, 32]) for h in range(2)]
    k.kt = [k.sb(f"k_feat{h}", [P, T]) for h in range(2)]
    k.ot = [k.sb(f"o_feat{h}", [P, T]) for h in range(2)]
    k.stage = [[k.xT[:, 4 * h + n, :] for n in range(4)] for h in range(2)]
    k.sgb = [k.sb(f"silu_gate{h}", [P, T]) for h in range(2)]
    k.ktok = k.sb("k_tok", [P, CH, 2, P])
    k.vtok = k.sb("v_tok", [P, CH, 2, P])
    k.pp = k.sb("p_prompt", [P, 2, SEQ])
    k.tgb = k.rs
    k.wt = k.sb("w_turned", [P, QB, P])
    k.kts = k.sb("past_k_feat", [P, 2, PAGES, P])
    k.pps = k.sb("p_sample", [64, PAGES * P])
    k.ppn = k.sb("p_new", [64, NS])
    k.ws = k.sb("w_sample", [P, (PAGES + 1) * 8])
    k.kb = [k.sb(f"k_pages{h}", [P, 4, 2 * P]) for h in range(2)]
    k.vb = [k.sb(f"v_pages{h}", [P, 4, 2 * P]) for h in range(2)]
    k.pm, k.pl, k.st = k.sb("p_max", [P, 2]), k.sb("p_sum", [P, 2]), k.sb("s_stats", [64, 6])
    k.negq = k.sb("mask_q", [P, P])
    k.qsel = k.sb("q_select", [NS, NB, 32])
    k.negs = k.sb("mask_s", [NS, NS])
    k.cp = k.sb("c_pattern", [64, 3, 8])
    k.cmat = k.sb("c_matrix", [64, 8])
    k.lam = k.sb("lam", [P, 4])
    k.blam = k.sb("lam_rows", [P, 4 * DH])
    k.subw = k.sb("subln", [P, 1])
    k.table = k.sb("table", [1, NB * PAGES], I32)


def b_cols(a, kind, h):
    return a["b_in_w"][0][:, (kind * HEADS + h) * P:(kind * HEADS + h + 1) * P]


def b_sync(sp, k, a, nxt):
    sem, s0 = k.sem, SLOT_B
    sp.wait_ge(sem["tails_out"], TAILS_OUT)
    sp.dma_start(k.table[:], a["page_table"].rearrange("(o b) n -> o (b n)", o=1)).then_inc(sem["table_in"], 16)
    sp.dma_start(k.blam[:], a["b_lambda"].rearrange("o a d -> o (a d)").broadcast_to([P, 4 * DH])).then_inc(sem["b_params"], 16)
    sp.dma_start(k.subw[:], a["b_subln_w"].rearrange("o d -> d o")).then_inc(sem["b_params"], 16)
    sp.wait_ge(sem["table_in"], 16)
    keys = a["cache_k"][0].rearrange("n t h c d -> n t (h c d)")
    values = a["cache_v"][0].rearrange("n t h d -> n t (h d)")

    def pages(n, col, buffers, cache, landed, free=None):
        page = [sp.value_load(k.table[0:1, n * PAGES + g:n * PAGES + g + 1], min_val=0, max_val=79) for g in range(PAGES)]
        if free:
            sp.wait_ge(sem[free[0]], free[1])
        for g in range(PAGES):
            sp.dma_start(buffers[g // 4][:, g % 4, :], cache[bass.ds(page[g], 1), :, bass.ds(col, 2 * P)]
                         .rearrange("o t c -> (o t) c")).then_inc(sem[f"{landed}{g // 4}"], 16)

    def key_pages(n, col, after=None):
        pages(n, col, k.kb, keys, "k_landed", after and ("r_done", R_PAIR * after[0] + r_keys(after[1], 3) + 1))

    def value_pages(n, col, after=None):
        pages(n, col, k.vb, values, "v_landed", after and ("x_done", X_PAIR * after[0] + x_sample(after[1]) + 1))

    def stage(i, u, slots, units, final=False):
        fixed = final or not (slots and units)
        cols = [(i * 2 + n // 4) * P + n % 4 * D for n in range(8)] + [(i * 2 + 2) * P, (i * 2 + 2) * P + D]
        at, following = u * 2 * P, u * 2 * P + 2 * P
        if not fixed:
            cols = [sp.snap(c) for c in cols]
            at, following = sp.snap(at), sp.snap(following)
        if not units:
            key_pages(0, 0)
        for n in range(8):
            if slots and final and n >= 6:
                load_slot(sp, k, s0 + 26 + n, n % 2, a["b_out_w"][0][:, (n - 6) * P:(n - 5) * P])
            elif slots:
                load_slot(sp, k, s0 + 8 * i + n + 2, n % 2, a["b_in_w"][0][:, bass.ds(cols[n + 2], P)])
            if units and n < 7:
                key_pages(n + 1, at, (u, n))
            elif units and slots:
                key_pages(0, following, (u, 7))
            if units and n:
                value_pages(n, at, (u, n - 1))
        if slots:
            value_pages(0, following, (u, 7) if units else None)

    stage(0, -1, True, False)
    with sp.Fori(0, 2) as j:
        stage(j + 1, j, True, True)
    stage(3, 2, True, True, final=True)
    stage(4, 3, False, True)
    out_rest_sync(sp, k, s0 + 32, a["b_out_w"][0])
    for h in range(2):
        if nxt:
            load_slot(sp, k, s0 + 40 + h, h, nxt[h])


def out_rest_sync(sp, k, s, w):
    with sp.Fori(1, KT // 2) as i:
        col = [sp.snap((2 * i + h) * P) for h in range(2)]
        for h in range(2):
            load_slot(sp, k, s + 2 * i + h, h, w[:, bass.ds(col[h], P)])


def b_pool(pool, k, o, chain):
    sem = k.sem
    pool.wait_ge(sem["x_ready"], 2)
    pool.wait_ge(sem["tails_out"], TAILS_OUT)
    for t in [*k.qz, *k.qs, k.negq, k.negs, k.cp, k.qsel]:
        chain(pool.memset(t[:], 0.0))
    chain(pool.affine_select(out=k.negq[:], in_=k.negq[:], compare_op=ALU.is_ge, fill=NEG,
                             base=0, pattern=[[-1, P]], channel_multiplier=1))
    chain(pool.affine_select(out=k.negs[:], in_=k.negs[:], compare_op=ALU.is_ge, fill=NEG,
                             base=0, pattern=[[-1, NS]], channel_multiplier=1))
    blocks = k.negs[:].rearrange("p (b t) -> p b t", b=NB)
    chain(pool.affine_select(out=blocks, in_=blocks, compare_op=ALU.is_ge, fill=NEG,
                             base=DT - 1, pattern=[[DT, NB], [0, DT]], channel_multiplier=-1))
    sel = k.qsel[:].rearrange("p b (c t) -> p b c t", t=DT)
    chain(pool.affine_select(out=sel, in_=sel, compare_op=ALU.not_equal, fill=1.0,
                             base=0, pattern=[[-DT, NB], [0, 8], [-1, DT]], channel_multiplier=1))
    for m in range(2):
        c = k.cp[:, m, :].rearrange("p (h t) -> p h t", h=2)
        chain(pool.affine_select(out=c, in_=c, compare_op=ALU.not_equal, fill=1.0,
                                 base=-DT * m, pattern=[[-32, 2], [-1, DT]], channel_multiplier=1))
    pool.memset(k.ws[:], 0.0).then_inc(sem["b_consts"], 1)
    kp = o["k_prompt"][0, 0].rearrange("(c p) h m d -> p c (h m d)", p=P)
    vp = o["v_prompt"][0, 0].rearrange("(c p) h d -> p c (h d)", p=P)
    ks = o["k_sample"][0].rearrange("b t h m d -> (b t) (h m d)")
    vs = o["v_sample"][0].rearrange("b t h d -> (b t) (h d)")
    for i in range(4):
        cols = slice(i * 2 * P, (i + 1) * 2 * P)
        pool.wait_ge(sem["tok_ready"], i + 1)
        for dst, dst_s, src in ((kp, ks, k.ktok), (vp, vs, k.vtok)):
            pool.dma_start(dst[:, :, cols], src[:, 0:QB].rearrange("p c h d -> p c (h d)")).then_inc(sem["kv_out"], 16)
            pool.dma_start(dst_s[:, cols], src[0:NS, QB].rearrange("p h d -> p (h d)")).then_inc(sem["kv_out"], 16)
    pool.wait_ge(sem["q_ready"], 4)
    pool.wait_ge(sem["gates_copied"], 4)
    pool.tensor_tensor(k.xT[:], k.xh[:], k.xl[:], ALU.add).then_inc(sem["x_back"], 1)


def b_tensor(pe, k):
    sem, s0, u0 = k.sem, SLOT_B, USE_B
    pe.wait_ge(sem["x_ready"], 2)
    pe.wait_ge(sem["b_consts"], 1)

    def prompt_scores(i, n):
        h, q = n // 4, n % 4
        may_fill(pe, k, "s", i, s_prompt(n))
        for m in range(2):
            mm = pe.matmul(k.s[:, m, 0:P * (q + 1)], k.qz[h][:, m, q * P:(q + 1) * P], k.kt[h][:, 0:P * (q + 1)],
                           start=True, stop=True)
        mm.then_inc(sem["s_done"], 1)

    def past_keys(i, n):
        for q in range(4):
            if q % 2 == 0:
                pe.wait_ge(sem[f"k_landed{q // 2}"], 64 * (8 * i + n) + 64)
            may_fill(pe, k, "r", i, r_keys(n, q))
            bank = r_keys(n, q) % 2
            for g in range(2):
                for h in range(2):
                    c = (2 * g + h) * P
                    t = pe.transpose(k.r[:, bank, c:c + P], k.kb[q // 2][:, 2 * (q % 2) + g, h * P:(h + 1) * P], k.ident[:])
            t.then_inc(sem["r_done"], 1)

    def sample_weights(i, n):
        pe.wait_ge(sem["c_ready"], 8 * i + n + 1)
        may_fill(pe, k, "x", i, x_weights(n))
        for g in range(PAGES):
            pe.matmul(k.x[:, 8 * g:8 * g + 8], k.pps[:, g * P:(g + 1) * P], k.cmat[:], start=True, stop=True)
        mm = pe.matmul(k.x[0:NS, 64:72], k.ppn[:], k.cmat[:], start=True, stop=True)
        mm.then_inc(sem["x_done"], 1)

    def sample_output(i, n):
        may_fill(pe, k, "x", i, x_sample(n))
        for half in range(2):
            pe.wait_ge(sem[f"v_landed{half}"], 64 * (8 * i + n) + 64)
        for h in range(2):
            out = k.x[:, 4 * h:4 * h + 4]
            for g in range(PAGES):
                pe.matmul(out, k.vb[g // 4][:, g % 4, h * P:(h + 1) * P], k.ws[:, 8 * g + 4 * h:8 * g + 4 * h + 4],
                          start=g == 0, stop=False)
            mm = pe.matmul(out, k.vtok[0:NS, QB, h, :], k.ws[0:NS, 64 + 4 * h:68 + 4 * h], start=False, stop=True)
        mm.then_inc(sem["x_done"], 1)

    def sample_scores(i, n):
        may_fill(pe, k, "s", i, s_sample(n))
        for q in range(2):
            last = r_keys(n, 2 + q)
            pe.wait_ge(sem[f"r_read{last % 2}"], R_PAIR // 2 * i + last // 2 + 1)
        for half in range(2):
            for h in range(2):
                mm = pe.matmul(k.s[32 * h:32 * h + 32, half, :], k.qs[h][:, n, :],
                               k.kts[:, h, 4 * half:4 * half + 4, :], start=True, stop=True)
        mm.then_inc(sem["s_done"], 1)
        may_fill(pe, k, "x", i, x_new(n))
        for h in range(2):
            out = k.x[32 * h:32 * h + 32, 0:NS]
            pe.matmul(out, k.qs[h][:, n, :], k.kt[h][:, SEQ:T], start=True, stop=False)
            mm = pe.matmul(out, k.qsel[:, n, :], k.negs[:], start=False, stop=True)
        mm.then_inc(sem["x_done"], 1)

    def prompt_weights(i, n):
        q = n % 4
        pe.wait_ge(sem["w_ready"], 8 * i + n + 1)
        f = r_weights(n)
        may_fill(pe, k, "r", i, f)
        for g in range(q + 1):
            t = pe.transpose(k.r[:, f % 2, g * P:(g + 1) * P], k.pp[:, 0, g * P:(g + 1) * P], k.ident[:])
        t.then_inc(sem["r_done"], 1)

    def prompt_output(i, n):
        h, q, f = n // 4, n % 4, r_weights(n)
        pe.wait_ge(sem[f"r_read{f % 2}"], R_PAIR // 2 * i + f // 2 + 1)
        may_fill(pe, k, "x", i, x_prompt(n))
        for g in range(q + 1):
            mm = pe.matmul(k.x[:, 0:P], k.vtok[:, g, h, :], k.wt[:, g, :], start=g == 0, stop=g == q)
        mm.then_inc(sem["x_done"], 1)

    def stage(i, u, slots, units):
        if units:
            pe.wait_ge(sem["q_ready"], u + 1)
            pe.wait_ge(sem["tok_ready"], u + 1)
        for n in range(9):
            if units and n < 8:
                past_keys(u, n)
                prompt_scores(u, n)
            if slots and n < 8:
                multiply_slot(pe, k, s0 + 8 * i + n, n % 2, u0 + 8 * i + n, u0 // 2 + 4 * i + n // 2, n % 2, k.xh, k.xl)
            if units:
                if n:
                    sample_weights(u, n - 1)
                if n < 8:
                    prompt_weights(u, n)
                    sample_scores(u, n)
                if n:
                    sample_output(u, n - 1)
                if n < 8:
                    prompt_output(u, n)
        if slots:
            pe.wait_ge(sem["p_evac0"], u0 // 2 + 4 * i + 4)
            pe.wait_ge(sem["p_evac1"], u0 // 2 + 4 * i + 4)
            pe.wait_ge(sem["s_evac"], u0 + 8 * i + 8)
            may_fill(pe, k, "x", i, 0)
            for c in range(4):
                src = k.stage[c // 2][1 + c % 2]
                may_fill(pe, k, "r", i, r_turn(c))
                for g in range(QB):
                    t = pe.transpose(k.r[:, c % 2, g * P:(g + 1) * P], src[:, g * P:(g + 1) * P], k.ident[:])
                t.then_inc(sem["r_done"], 1)
                t = pe.transpose(k.x[0:NS, c * P:(c + 1) * P], src[:, SEQ:T], k.ident[:])
            t.then_inc(sem["x_done"], 1)
        for h in range(2):
            if units:
                pe.wait_ge(sem["o_squared"], 2 * u + h + 1)
                may_fill(pe, k, "s", u, s_rms(h))
                pe.matmul(k.s[:, 0, :], k.ones_d[:], k.sq[h][:, 0, 0:SEQ], start=True, stop=True)
                mm = pe.matmul(k.s[:, 1, 0:NS], k.ones_d[:], k.sq[h][:, 0, SEQ:T], start=True, stop=True)
                mm.then_inc(sem["s_done"], 1)

    stage(0, -1, True, False)
    with pe.Fori(0, 3) as j:
        stage(j + 1, j, True, True)
    stage(4, 3, False, True)
    pe.wait_ge(sem["b_head"], 8)
    out_tensor(pe, k, s0 + 32, u0 + 32)
    ln_tensor(pe, k, 1)


def b_scalar(act, k, chain):
    sem, s0, u0 = k.sem, SLOT_B, USE_B
    act.wait_ge(sem["b_consts"], 1)
    act.wait_ge(sem["lam_in"], 1)
    act.activation(k.lam[:, 0:2], k.lam[:, 0:2], ACT.Exp).then_inc(sem["lam_exp"], 1)

    def keys_copy(u, n, q):
        f = r_keys(n, q)
        if n:
            act.wait_ge(sem["s_done"], S_PAIR * u + s_sample(n - 1) + 1)
        await_fill(act, k, "r", u, f)
        act.activation(k.kts[:, :, 2 * q:2 * q + 2, :].rearrange("p h g c -> p g h c"),
                       k.r[:, f % 2, :].rearrange("p (g h c) -> p g h c", g=2, h=2), ACT.Copy).then_inc(sem[f"r_read{f % 2}"], 1)

    def before_slot(u, n):
        q = n % 4
        keys_copy(u, n, 0)
        keys_copy(u, n, 2)
        act.wait_ge(sem["pm_ready"], 8 * u + n + 1)
        for m in range(2):
            step = act.activation(k.pp[:, m, 0:P * (q + 1)], k.s[:, m, 0:P * (q + 1)], ACT.Exp,
                                  bias=k.pm[:, m:m + 1], accum_out=k.pl[:, m:m + 1])
            chain(step) if m == 0 else step.then_inc(sem["s_read"], 1)

    def slot(i, n, units):
        h, kind = n // 4, n % 4
        split_high(act, k, s0 + 8 * i + n + 1, s0 // 2 + 4 * i + (n + 1) // 2, (n + 1) % 2)
        if kind == 1:
            return
        await_slot(act, k, s0 + 8 * i + n)
        if kind in (0, 2):
            to = k.stage[h][kind]
            if units and kind == 2 and h == 0:
                act.wait_ge(sem["x_done"], X_PAIR * i - X_PAIR + 1)
            act.activation(to[:, HALF:T], k.proj[:, 0, 0:T - HALF], ACT.Copy).then_inc(sem["p_evac0"], 1)
            act.activation(to[:, 0:HALF], k.proj_lo[:, 0:HALF], ACT.Copy).then_inc(sem["s_evac"], 1)
        else:
            if h:
                act.wait_ge(sem["s_evac"], u0 + 8 * i + 4)
            elif units:
                act.wait_ge(sem["b_head"], 2 * i - 2)
            chain(act.activation(k.tgb[:, HALF:T], k.proj[:, 1, 0:T - HALF], ACT.Tanh, scale=0.5))
            act.activation(k.tgb[:, 0:HALF], k.proj_lo[:, 0:HALF], ACT.Tanh, scale=0.5).then_inc(sem["tgb_ready"], 1)

    def after_slot(u, n):
        q, f = n % 4, r_weights(n)
        if n:
            act.wait_ge(sem["x_done"], X_PAIR * u + x_prompt(n - 1) + 1)
        await_fill(act, k, "r", u, f)
        act.activation(k.wt[:, 0:q + 1, :], k.r[:, f % 2, 0:P * (q + 1)].rearrange("p (g c) -> p g c", c=P),
                       ACT.Copy).then_inc(sem[f"r_read{f % 2}"], 1)
        if n:
            act.wait_ge(sem["x_done"], X_PAIR * u + x_weights(n - 1) + 1)
        act.wait_ge(sem["sm_ready"], 8 * u + n + 1)
        chain(act.activation(k.ppn[:], k.ppn[:], ACT.Exp, bias=k.st[:, 2:3], accum_out=k.st[:, 4:5]))
        act.activation(k.pps[:], k.s[0:64, :, :].rearrange("p b c -> p (b c)"), ACT.Exp, bias=k.st[:, 2:3],
                       accum_out=k.st[:, 3:4]).then_inc(sem["s_read"], 1)

    def stage(i, u, slots, units):
        for n in range(8):
            if units:
                before_slot(u, n)
            if slots:
                slot(i, n, units)
            if units:
                after_slot(u, n)
        if units:
            act.wait_ge(sem["x_read"], X_PAIR * u + X_PAIR)
        for h in range(2):
            if units:
                act.activation(k.sq[h][:, 0, :], k.ot[h][:], ACT.Square).then_inc(sem["o_squared"], 1)
        if slots:
            act.wait_ge(sem["p_evac0"], u0 // 2 + 4 * i + 4)
            act.wait_ge(sem["p_evac1"], u0 // 2 + 4 * i + 4)
            act.wait_ge(sem["s_evac"], u0 + 8 * i + 8)
            for h in range(2):
                for m in range(2):
                    lo, src = slice(64 * m, 64 * m + 64), k.stage[h][0]
                    chain(act.activation(k.qz[h][lo, m, :], src[lo, 0:SEQ], ACT.Copy, scale=DH ** -0.5))
                    chain(act.activation(k.qs[h][lo, :, 4 * m:4 * m + 4], src[lo, SEQ:T].rearrange("p (b t) -> p b t", b=NB),
                                         ACT.Copy, scale=DH ** -0.5))
                step = act.activation(k.kt[h][:], k.stage[h][1][:], ACT.Copy)
                chain(step) if h == 0 else step.then_inc(sem["q_ready"], 1)
        for h in range(2):
            if units:
                await_fill(act, k, "s", u, s_rms(h))
                if h:
                    act.wait_ge(sem["b_head"], 2 * u + 1)
                chain(act.activation(k.rs[:, 0:SEQ], k.s[:, 0, :], ACT.Sqrt, bias=k.eps[:], scale=float(D // P)))
                act.activation(k.rs[:, SEQ:T], k.s[:, 1, 0:NS], ACT.Sqrt, bias=k.eps[:], scale=float(D // P)).then_inc(sem["s_read"], 1)

    stage(0, -1, True, False)
    with chain.loop("b", 3) as j:
        stage(j + 1, j, True, True)
    stage(4, 3, False, True)
    out_scalar(act, k, s0 + 32, chain, 1 == k.last)
    ln_scalar(act, k, 1, chain)


def b_vector(dve, k, chain):
    sem, s0, u0 = k.sem, SLOT_B, USE_B
    dve.wait_ge(sem["b_consts"], 1)
    dve.wait_ge(sem["b_params"], 32)
    lam = k.blam[:].rearrange("p (a c d) -> p a c d", a=2, c=2)
    chain(dve.tensor_tensor(lam[:, :, 0, :], lam[:, :, 0, :], lam[:, :, 1, :], ALU.mult))
    dve.tensor_reduce(k.lam[:, 0:2], lam[:, :, 0, :], AX.X, ALU.add).then_inc(sem["lam_in"], 1)
    dve.wait_ge(sem["lam_exp"], 1)
    chain(dve.tensor_tensor(k.lam[:, 2:3], k.lam[:, 1:2], k.lam[:, 0:1], ALU.subtract))
    chain(dve.tensor_scalar(k.lam[:, 3:4], k.lam[:, 2:3], LAM_INIT, None, ALU.subtract))
    chain(dve.tensor_scalar(k.cp[:, 1, :], k.cp[:, 1, :], k.lam[0:64, 3:4], None, ALU.mult))
    chain(dve.tensor_tensor(k.cp[:, 2, :], k.cp[:, 0, :], k.cp[:, 1, :], ALU.add))
    chain(dve.tensor_scalar(k.subw[:], k.subw[:], 0.5 * (1.0 - LAM_INIT), None, ALU.mult))

    def keys_copy(u, n, q):
        f = r_keys(n, q)
        await_fill(dve, k, "r", u, f)
        if n:
            dve.wait_ge(sem["s_done"], S_PAIR * u + s_sample(n - 1) + 1)
        dve.tensor_copy(k.kts[:, :, 2 * q:2 * q + 2, :].rearrange("p h g c -> p g h c"),
                        k.r[:, f % 2, :].rearrange("p (g h c) -> p g h c", g=2, h=2)).then_inc(sem[f"r_read{f % 2}"], 1)

    def factors(u, n):
        dve.wait_ge(sem["s_read"], S_PAIR * u + s_sample(n) + 1)
        chain(dve.tensor_tensor(k.st[:, 5:6], k.st[:, 3:4], k.st[:, 4:5], ALU.add))
        chain(dve.reciprocal(k.st[:, 5:6], k.st[:, 5:6]))
        dve.tensor_scalar(k.cmat[:], k.cp[:, 2, :], k.st[:, 5:6], None, ALU.mult).then_inc(sem["c_ready"], 1)

    def maxima(u, n):
        q = n % 4
        await_fill(dve, k, "s", u, s_prompt(n))
        diagonal = k.s[:, :, q * P:(q + 1) * P]
        chain(dve.tensor_tensor(diagonal, diagonal, k.negq[:].unsqueeze(1).broadcast_to([P, 2, P]), ALU.add))
        chain(dve.tensor_reduce(k.pm[:], k.s[:, :, 0:P * (q + 1)], AX.X, ALU.max))
        dve.tensor_scalar(k.pm[:], k.pm[:], -1.0, None, ALU.mult).then_inc(sem["pm_ready"], 1)

    def slot(i, n, units):
        h, kind = n // 4, n % 4
        if kind == 1:
            if units and h == 0:
                dve.wait_ge(sem["q_ready"], i)
            await_slot(dve, k, s0 + 8 * i + n)
            dve.tensor_copy(k.stage[h][1][:, HALF:T], k.proj[:, 1, 0:T - HALF]).then_inc(sem["p_evac1"], 1)
            dve.tensor_copy(k.stage[h][1][:, 0:HALF], k.proj_lo[:, 0:HALF]).then_inc(sem["s_evac"], 1)
        if kind == 3:
            dve.wait_ge(sem["tgb_ready"], 2 * i + h + 1)
            to = k.stage[h][3]
            dve.scalar_tensor_tensor(to[:, HALF:T], k.tgb[:, HALF:T], 1.0, k.proj[:, 1, 0:T - HALF], ALU.add, ALU.mult).then_inc(sem["p_evac1"], 1)
            dve.scalar_tensor_tensor(to[:, 0:HALF], k.tgb[:, 0:HALF], 1.0, k.proj_lo[:, 0:HALF], ALU.add, ALU.mult).then_inc(sem["s_evac"], 1)

    def weights(u, n):
        q = n % 4
        dve.wait_ge(sem["s_read"], S_PAIR * u + s_prompt(n) + 1)
        chain(dve.reciprocal(k.pl[:], k.pl[:]))
        chain(dve.tensor_scalar(k.pl[:, 1:2], k.pl[:, 1:2], k.lam[:, 3:4], None, ALU.mult))
        w0, w1 = k.pp[:, 0, 0:P * (q + 1)], k.pp[:, 1, 0:P * (q + 1)]
        chain(dve.tensor_scalar(w0, w0, k.pl[:, 0:1], None, ALU.mult))
        dve.scalar_tensor_tensor(w0, w1, k.pl[:, 1:2], w0, ALU.mult, ALU.add).then_inc(sem["w_ready"], 1)

    def sample_weights(u, n):
        await_fill(dve, k, "x", u, x_weights(n))
        chain(dve.tensor_copy(k.ws[:, 0:64], k.x[:, 0:64]))
        dve.tensor_copy(k.ws[0:NS, 64:72], k.x[0:NS, 64:72]).then_inc(sem["x_read"], 1)

    def sample_maxima(u, n):
        await_fill(dve, k, "x", u, x_new(n))
        dve.tensor_copy(k.ppn[:], k.x[0:64, 0:NS]).then_inc(sem["x_read"], 1)
        chain(dve.tensor_reduce(k.st[:, 0:1], k.s[0:64, :, :], AX.XY, ALU.max))
        dve.wait_ge(sem["x_read"], X_PAIR * u + x_new(n) + 1)
        chain(dve.tensor_reduce(k.st[:, 1:2], k.ppn[:], AX.X, ALU.max))
        chain(dve.tensor_tensor(k.st[:, 2:3], k.st[:, 0:1], k.st[:, 1:2], ALU.max))
        dve.tensor_scalar(k.st[:, 2:3], k.st[:, 2:3], -1.0, None, ALU.mult).then_inc(sem["sm_ready"], 1)

    def sample_output(u, n):
        await_fill(dve, k, "x", u, x_sample(n))
        at = SEQ + DT * n
        chain(dve.tensor_copy(k.ot[0][:, at:at + DT], k.x[:, 0:DT]))
        dve.tensor_copy(k.ot[1][:, at:at + DT], k.x[:, DT:2 * DT]).then_inc(sem["x_read"], 1)

    def tokens(i):
        dve.wait_ge(sem["kv_out"], 64 * i)
        for c in range(4):
            await_fill(dve, k, "r", i, r_turn(c))
            dve.tensor_copy((k.ktok, k.vtok)[c % 2][:, 0:QB, c // 2, :],
                            k.r[:, c % 2, :].rearrange("p (g d) -> p g d", g=QB)).then_inc(sem[f"r_read{c % 2}"], 1)
        await_fill(dve, k, "x", i, 0)
        new = k.x[0:NS, :].rearrange("p (h c d) -> p h c d", h=2, c=2)
        chain(dve.tensor_copy(k.ktok[0:NS, QB], new[:, :, 0, :]))
        dve.tensor_copy(k.vtok[0:NS, QB], new[:, :, 1, :]).then_inc(sem["x_read"], 1)
        dve.wait_ge(sem["x_read"], X_PAIR * i + 1)
        for b in range(2):
            dve.wait_ge(sem[f"r_read{b}"], R_PAIR // 2 * i + 2)
        dve.sem_inc(sem["tok_ready"], 1)

    def normalise(u, h):
        dve.wait_ge(sem["s_read"], S_PAIR * u + s_rms(h) + 1)
        chain(dve.reciprocal(k.rs[:], k.rs[:]))
        chain(dve.scalar_tensor_tensor(k.ot[h][:], k.ot[h][:], k.subw[:], k.rs[:], ALU.mult, ALU.mult))
        chain(dve.tensor_tensor(k.ot[h][:], k.ot[h][:], k.sgb[h][:], ALU.mult))
        high = k.gh[:, bass.ds(2 * u + h, 1), :].rearrange("p o t -> p (o t)")
        low = k.gl[:, bass.ds(2 * u + h, 1), :].rearrange("p o t -> p (o t)")
        chain(dve.tensor_scalar(high, k.ot[h][:], 1.0, None, ALU.mult))
        dve.tensor_tensor(low, k.ot[h][:], high, ALU.subtract).then_inc(sem["b_head"], 1)
        dve.wait_ge(sem["b_head"], 2 * u + h + 1)

    def stage(i, u, slots, units):
        for n in range(9):
            if units and n:
                factors(u, n - 1)
            if units and n < 8:
                keys_copy(u, n, 1)
                keys_copy(u, n, 3)
                maxima(u, n)
            if slots and n < 8:
                split_low(dve, k, s0 + 8 * i + n + 1, (n + 1) % 2)
            if units and n < 8:
                weights(u, n)
            if slots and n < 8:
                slot(i, n, units)
            if units and n:
                sample_weights(u, n - 1)
            if units and n < 8:
                await_fill(dve, k, "s", u, s_sample(n))
                sample_maxima(u, n)
            if units and n:
                sample_output(u, n - 1)
            if units and n < 8:
                await_fill(dve, k, "x", u, x_prompt(n))
                q = n % 4
                dve.tensor_copy(k.ot[n // 4][:, q * P:(q + 1) * P], k.x[:, 0:P]).then_inc(sem["x_read"], 1)
        if slots:
            tokens(i)
        if units:
            dve.wait_ge(sem["x_read"], X_PAIR * u + X_PAIR)
        for h in range(2):
            if units:
                normalise(u, h)
            if slots:
                if not units:
                    dve.wait_ge(sem["s_evac"], u0 + 8 * i + 8)
                    dve.wait_ge(sem["p_evac1"], u0 // 2 + 4 * i + 4)
                copy = dve.tensor_copy(k.sgb[h][:], k.stage[h][3][:])
                chain(copy) if h == 0 else copy.then_inc(sem["gates_copied"], 1)

    stage(0, -1, True, False)
    with chain.loop("b", 3) as j:
        stage(j + 1, j, True, True)
    stage(4, 3, False, True)
    dve.wait_ge(sem["x_back"], 1)
    out_vector(dve, k, s0 + 32, u0 + 32, chain, 1 == k.last)
    ln_vector(dve, k, 1, chain)



CS_TURN, CR_TURN, CX_TURN = 12, 14, 5


def cs_tok(n):
    return n


def cs_sums(c):
    return 3 + c


def cs_state(n):
    return 8 + n


CR_TOK = 0


def cr_scores(c):
    return 1 + 2 * c


def cr_update(c):
    return 2 + 2 * c


def cr_state(n):
    return 10 + n


def c_filled(eng, k, bank, g, local):
    per = {"s": CS_TURN, "r": CR_TURN, "x": CX_TURN}[bank]
    eng.wait_ge(k.sem[f"c{bank}_done"], per * g + local + 1)


def c_read(k, bank, local):
    return k.sem["cx_read" if bank == "x" else f"c{bank}_read{local % 2}"]


def c_was_read(eng, k, bank, g, local):
    per = {"s": CS_TURN, "r": CR_TURN, "x": CX_TURN}[bank]
    if bank == "x":
        eng.wait_ge(k.sem["cx_read"], per * g + local + 1)
    else:
        eng.wait_ge(k.sem[f"c{bank}_read{local % 2}"], per // 2 * g + local // 2 + 1)


def c_may_fill(pe, k, bank, g, local):
    per = {"s": CS_TURN, "r": CR_TURN, "x": CX_TURN}[bank]
    if bank == "x":
        pe.wait_ge(k.sem["cx_read"], per * g + local)
    else:
        pe.wait_ge(k.sem[f"c{bank}_read{local % 2}"], per // 2 * g + local // 2)


def layer_c_buffers(k):
    k.st0 = k.sb("st0", [P, 2, NB, STATE])
    k.btok, k.xtok = k.sb("b_tok", [P, CH, STATE]), k.sb("x_tok", [P, CH, 2 * P])
    k.dt, k.adt, k.cs, k.dec = (k.sb(n, [P, CH, SSDH]) for n in ("dt", "adt", "cs", "dec"))
    k.dt_g, k.adt_g, k.cs_g, k.dec_g = (k.sb(n, [P, CH, HPG]) for n in ("dt_g", "adt_g", "cs_g", "dec_g"))
    k.wdt = k.sb("w_dt", [P, KT, SSDH])
    k.rowp = k.sb("row_params", [P, 3, SSDH])
    k.dsk = k.sb("d_skip", [P, CT])
    k.curc = k.sb("curc", [P, 4, 29])
    k.nw = k.sb("norm_w", [P, CT])
    k.feat = [k.sb(n, [P, T]) for n in ("b_feat", "c_feat", "x_feat0", "x_feat1")]
    k.cc, k.th = k.sb("cc", [P, T]), k.sb("th", [P, T])
    k.sz = [k.sb(f"sz{j}", [P, T]) for j in range(2)]
    k.xdt, k.xdd = k.sb("xdt", [P, 2 * P]), k.sb("xdd", [P, 2 * P])
    k.dm, k.e, k.m = (k.sb(n, [P, HPG, P]) for n in ("dm", "e", "m"))
    k.edec = k.sb("edec", [P, HPG])
    k.decp = k.sb("decp", [P, 2, NB])
    k.ht = k.sb("h_feat", [P, 2 * P])
    k.featn = [k.sb(n, [P, T]) for n in ("b_next", "c_next", "x_next0", "x_next1")]
    k.szn = [k.sb(f"sz_next{j}", [P, T]) for j in range(2)]
    k.hout = k.sb("h_out", [P, 2, P])
    k.hts = [k.sb(f"h_sample{j}", [P, 4, P]) for j in range(2)]
    k.bm = k.sq[0].rearrange("p a t -> p (a t)")[0:NS, 0:NB * STATE].rearrange("p (b n) -> p b n", b=NB)
    k.acc = k.sb("acc", [P, T])
    k.negc = k.sb("mask_c", [P, P])
    k.negcs = k.sb("mask_cs", [NS, NS])
    k.tris = k.sb("tri_s", [NS, NS])
    k.blk = k.sb("block_s", [NS, NS])
    k.ctails = k.sb("c_tails", [P, CONV_C // P, HN])


def c_cols(g, n):
    return [INNER * 2 + P * g, INNER * 2 + GROUPS * STATE + P * g, INNER + 2 * P * g, INNER + 2 * P * g + P,
            2 * P * g, 2 * P * g + P][n]


def c_sync(sp, k, a, nxt):
    sem, s0, w = k.sem, SLOT_C, a["c_in_w"][0]
    sp.wait_ge(sem["x_ready"], 3)
    sp.wait_ge(sem["kv_out"], 256)
    sp.dma_start(k.wdt[:], w[:, INNER + CONV_C:].rearrange("(k p) n -> p k n", p=P)).then_inc(sem["c_params"], 16)
    for n, v in enumerate((a["c_dt_bias"], a["c_a_log"], a["c_d"])):
        sp.dma_start(k.rowp[:, n, :], v.broadcast_to([P, SSDH])).then_inc(sem["c_params"], 16)
    states = a["state_ssd_h"][0].rearrange("b (q j h) p n -> q j (h p) b n", j=2, h=2)

    def stage(i, u, slots, units, final=False):
        fixed = final or not (slots and units)
        cols = [c_cols(i, n) for n in range(2, 6)] + [c_cols(i + 1, n) for n in range(2)]
        if not fixed:
            cols = [sp.snap(c_cols(u, n % 6) + (1 + n // 6) * (c_cols(1, n % 6) - c_cols(0, n % 6))) for n in range(2, 8)]
        for n in range(6):
            if slots and not (final and n >= 4):
                load_slot(sp, k, s0 + 6 * i + n + 2, n % 2, w[:, bass.ds(cols[n], P)])
            elif slots:
                load_slot(sp, k, s0 + 44 + n, n % 2, ow[(n - 4) * D:(n - 3) * D, 0:P])
            if units and n == 2:
                sp.wait_ge(sem["st_out"], 32 * u)
                for j in range(2):
                    sp.dma_start(k.st0[:, j], states[bass.ds(u, 1), j].rearrange("o p b n -> (o p) b n")).then_inc(sem["st_landed"], 16)

    ow = a["c_out_w"][0]
    stage(0, -1, True, False)
    with sp.Fori(0, GROUPS - 2) as j:
        stage(j + 1, j, True, True)
    stage(GROUPS - 1, GROUPS - 2, True, True, final=True)
    stage(GROUPS, GROUPS - 1, False, True)
    with sp.Fori(1, KT) as m:
        col = sp.snap(m * P)
        for n in range(2):
            load_slot(sp, k, SLOT_C + 48 + 2 * m + n, n, ow[n * D:(n + 1) * D, bass.ds(col, P)])
    for h in range(2):
        if nxt:
            load_slot(sp, k, SLOT_C + 64 + h, h, nxt[h])


def c_pool(pool, k, o, chain):
    sem = k.sem
    pool.wait_ge(sem["x_ready"], 3)
    pool.wait_ge(sem["kv_out"], 256)
    for t, v in ((k.negc, 0.0), (k.negcs, 0.0), (k.tris, 1.0), (k.blk, 1.0), (k.acc, 0.0), (k.dt, 0.0), (k.cs, 0.0), (k.dec, 0.0)):
        chain(pool.memset(t[:], v))
    chain(pool.affine_select(out=k.negc[:], in_=k.negc[:], compare_op=ALU.is_ge, fill=NEG,
                             base=0, pattern=[[1, P]], channel_multiplier=-1))
    for t, fill, causal in ((k.negcs, NEG, True), (k.tris, 0.0, True), (k.blk, 0.0, False)):
        v = t[:].rearrange("p (b t) -> p b t", b=NB)
        chain(pool.affine_select(out=v, in_=v, compare_op=ALU.is_ge, fill=fill, base=0,
                                 pattern=[[-DT, NB], [0, DT]], channel_multiplier=1))
        if causal:
            chain(pool.affine_select(out=t[:], in_=t[:], compare_op=ALU.is_ge, fill=fill, base=0,
                                     pattern=[[1, NS]], channel_multiplier=-1))
        else:
            chain(pool.affine_select(out=v, in_=v, compare_op=ALU.is_ge, fill=fill, base=DT - 1,
                                     pattern=[[DT, NB], [0, DT]], channel_multiplier=-1))
    pool.memset(k.edec[:], 0.0).then_inc(sem["c_consts"], 1)
    hp = o["ssd_h_prompt"][0, 0].rearrange("(g j h) p n -> g (h p) j n", j=2, h=2)
    hs = o["ssd_h_sample"][0].rearrange("b (q j h) p n -> q j (h p) b n", j=2, h=2)
    for g in range(GROUPS):
        pool.wait_ge(sem["hout_ready"], g + 1)
        pool.dma_start(hp[g], k.hout[:]).then_inc(sem["hp_out"], 16)
        pool.wait_ge(sem["st_ready"], g + 1)
        for j in range(2):
            pool.dma_start(hs[g, j], k.st0[:, j]).then_inc(sem["st_out"], 16)
        for j in range(2):
            pool.wait_ge(sem["g_squared"], 2 * g + j + 1)
            pool.tensor_tensor(k.acc[:], k.acc[:], k.sq[1][:, j, :], ALU.add).then_inc(sem["acc_added"], 1)
            pool.wait_ge(sem["acc_added"], 2 * g + j + 1)
    pool.wait_ge(sem["ctails_read"], 1)
    cp = o["ssd_conv_prompt"][0, 0].rearrange("n (u r p) -> n u r p", r=4, p=P)
    cs = o["ssd_conv_sample"][0].rearrange("b n (u r p) -> (b n) u r p", r=4, p=P)
    for r in range(4):
        src = k.rows[1][HN * r:HN * r + HN, :].rearrange("n (u p) -> n u p", p=P)
        pool.dma_start(cp[:, :, r, :], src[0:HIST]).then_inc(sem["ctails_out"], 16)
        pool.dma_start(cs[:, :, r, :], src[HIST:HN]).then_inc(sem["ctails_out"], 16)


def c_tensor(pe, k):
    sem, s0, u0 = k.sem, SLOT_C, USE_C
    pe.wait_ge(sem["x_ready"], 3)
    pe.wait_ge(sem["c_consts"], 1)
    pe.wait_ge(sem["c_params"], 64)
    for c in range(CH):
        n = P if c < QB else NS
        for i in range(KT):
            mm = pe.matmul(k.x[0:n, c * SSDH:(c + 1) * SSDH], k.xT[:, i, c * P:c * P + n], k.wdt[:, i, :],
                           start=i == 0, stop=i == KT - 1)
    mm.then_inc(sem["dt_raw"], 1)

    def totals():
        pe.wait_ge(sem["adt_ready"], 1)
        prompt, sample = k.adt[:, 0:QB, :], k.adt[0:NS, QB, :]
        pe.matmul(k.s[:, 0, 0:P], k.tri[:], prompt, start=True, stop=True)
        pe.matmul(k.s[0:NS, 0, P:P + SSDH], k.tris[:], sample, start=True, stop=True)
        pe.matmul(k.s[:, 1, 0:P], k.ones_d[:], prompt, start=True, stop=True)
        pe.matmul(k.s[0:NS, 1, P:P + SSDH], k.blk[:], sample, start=True, stop=True).then_inc(sem["sums_done"], 1)
        pe.wait_ge(sem["dt_made"], 1)

    def sums(g, c):
        f = cs_sums(c)
        c_may_fill(pe, k, "s", g, f)
        n, tri = (P, k.tri) if c < QB else (NS, k.tris)
        for r in range(HPG):
            mm = pe.matmul(k.s[:, f % 2, r * n:(r + 1) * n], k.adt_g[0:n, c, r:r + 1].broadcast_to([n, P]), tri[:],
                           start=True, stop=True)
        mm.then_inc(sem["cs_done"], 1)
        f, cols = cr_scores(c), slice(c * P, c * P + n)
        c_may_fill(pe, k, "r", g, f)
        mm = pe.matmul(k.r[0:n, f % 2, 0:n], k.feat[0][:, cols], k.feat[1][:, cols], start=True, stop=True)
        if c == QB:
            c_was_read(pe, k, "r", g, cr_update(QB - 1))
            for j in range(2):
                mm = pe.transpose(k.r[:, f % 2, P + j * P:2 * P + j * P], k.ht[:, j * P:(j + 1) * P], k.ident[:])
        mm.then_inc(sem["cr_done"], 1)

    def outputs(g, c):
        pe.wait_ge(sem["y_in"], 5 * g + c + 1)
        c_may_fill(pe, k, "x", g, c)
        if c:
            c_was_read(pe, k, "r", g, cr_update(c - 1))
        for r in range(HPG):
            out = k.x[64 * (r % 2):64 * (r % 2) + 64, r // 2 * P:r // 2 * P + P]
            pe.matmul(out, k.xdt[:, 64 * r:64 * r + 64], k.m[:, r, :], start=True, stop=False)
            mm = pe.matmul(out, k.ht[:, 64 * r:64 * r + 64], k.e[:, r, :], start=False, stop=True)
        mm.then_inc(sem["cx_done"], 1)
        f = cr_update(c)
        c_may_fill(pe, k, "r", g, f)
        pe.matmul(k.r[:, f % 2, 0:2 * P], k.btok[:, c, :], k.xdd[:], start=True, stop=True).then_inc(sem["cr_done"], 1)

    def old_states(g, n):
        f = cr_state(n)
        c_may_fill(pe, k, "r", g, f)
        for b in range(2):
            for j in range(2):
                t = pe.transpose(k.r[:, f % 2, (2 * b + j) * P:(2 * b + j + 1) * P], k.st0[:, j, 2 * n + b, :], k.ident[:])
        t.then_inc(sem["cr_done"], 1)

    def sample_outputs(g):
        pe.wait_ge(sem["y_in"], 5 * g + QB + 1)
        c_may_fill(pe, k, "x", g, QB)
        for r in range(HPG):
            out = k.x[64 * (r % 2):64 * (r % 2) + 64, r // 2 * P:r // 2 * P + NS]
            pe.matmul(out, k.xdt[0:NS, 64 * r:64 * r + 64], k.m[0:NS, r, 0:NS], start=r < 2, stop=False, skip_group_check=True)
        for n in range(4):
            if n < 3:
                old_states(g, n + 1)
            c_was_read(pe, k, "r", g, cr_state(n))
            for b in range(2):
                for r in range(HPG):
                    at = (2 * n + b) * DT
                    out = k.x[64 * (r % 2):64 * (r % 2) + 64, r // 2 * P + at:r // 2 * P + at + DT]
                    mm = pe.matmul(out, k.hts[n % 2][:, 2 * b + r // 2, 64 * (r % 2):64 * (r % 2) + 64],
                                   k.e[:, r, at:at + DT], start=False, stop=n == 3 and b == 1, skip_group_check=True)
            if n == 3:
                mm.then_inc(sem["cx_done"], 1)
            else:
                mm.then_inc(sem["hts_used"], 1)
        for n in range(4):
            f = cs_state(n)
            c_may_fill(pe, k, "s", g, f)
            pe.matmul(k.s[:, f % 2, :], k.xdd[0:NS, n // 2 * P:n // 2 * P + P], k.bm[:, n % 2 * 4:n % 2 * 4 + 4, :],
                      start=True, stop=True).then_inc(sem["cs_done"], 1)

    def tokens(i):
        pe.wait_ge(sem["feat_ready"], 4 * i + 4)
        for n in range(3):
            src = (k.featn[0], k.featn[2], k.featn[3])[n]
            c_may_fill(pe, k, "s", i, cs_tok(n))
            if n == 0:
                c_may_fill(pe, k, "r", i, CR_TOK)
            for c in range(QB):
                t = pe.transpose(k.s[:, n % 2, c * P:(c + 1) * P], src[:, c * P:(c + 1) * P], k.ident[:])
            t.then_inc(sem["cs_done"], 1)
            t = pe.transpose(k.r[0:NS, 0, n * P:(n + 1) * P], src[:, SEQ:T], k.ident[:])
        t.then_inc(sem["cr_done"], 1)

    def stage(i, u, slots, units):
        if units:
            pe.wait_ge(sem["group_params"], u + 1)
        for n in range(6):
            if units and n < QB:
                sums(u, n)
            if slots:
                multiply_slot(pe, k, s0 + 6 * i + n, n % 2, u0 + 6 * i + n, u0 // 2 + 3 * i + n // 2, n % 2, k.xh, k.xl)
            if units and n < QB:
                outputs(u, n)
            if units and n == QB:
                sums(u, QB)
                pe.wait_ge(sem["st_landed"], 32 * u + 32)
                old_states(u, 0)
            if units and n == 5:
                sample_outputs(u)
        if slots and not units:
            totals()
        if slots:
            tokens(i)

    stage(0, -1, True, False)
    with pe.Fori(0, GROUPS - 1) as j:
        stage(j + 1, j, True, True)
    stage(GROUPS, GROUPS - 1, False, True)
    pe.wait_ge(sem["acc_added"], 2 * GROUPS)
    pe.matmul(k.s[:, 0, :], k.ones_d[:], k.acc[:, 0:SEQ], start=True, stop=True)
    pe.matmul(k.s[:, 1, 0:NS], k.ones_d[:], k.acc[:, SEQ:T], start=True, stop=True).then_inc(sem["ms_done"], 1)
    for u in range(8):
        t = pe.transpose(k.r[0:4 * HN, u // 4, (u % 4) * P:(u % 4) * P + P],
                         k.ctails[:, 4 * u:4 * u + 4, :].rearrange("p i c -> p (i c)"), k.ident[:])
    t.then_inc(sem["ctails_turned"], 1)
    pe.wait_ge(sem["g_split"], 3)
    s, u = s0 + 48, u0 + 48
    with pe.Fori(0, KT // 2) as i:
        for h in range(2):
            for n in range(2):
                multiply_slot(pe, k, s + 4 * i + 2 * h + n, n, u + 2 * i + h, u // 2 + i, h,
                              (k.xh, k.xl)[n], (k.gh, k.gl)[n], first=n == 0, last=n == 1)
    ln_tensor(pe, k, 2)


def c_scalar(act, k, chain):
    sem, s0, u0 = k.sem, SLOT_C, USE_C
    act.wait_ge(sem["c_consts"], 1)
    act.wait_ge(sem["c_params"], 64)
    softplus_scalar(act, k, k.spa[:], 2)
    act.activation(k.rowp[:, 1, :], k.rowp[:, 1, :], ACT.Exp).then_inc(sem["a_exp"], 1)

    def slot(i, n):
        split_high(act, k, s0 + 6 * i + n + 1, s0 // 2 + 3 * i + (n + 1) // 2, (n + 1) % 2)
        await_slot(act, k, s0 + 6 * i + n)
        if n < 4:
            act.wait_ge(sem["c_conv"], 4 * i + n)
            row_of_inputs(act, k, n % 2, chain)
            act.wait_ge(sem["c_conv"], 4 * i + n + 1)
            act.activation(k.th[:], k.cc[:], ACT.Tanh).then_inc(sem["c_tanh"], 1)
        else:
            if n == 4:
                act.wait_ge(sem["feat_ready"], 4 * i + 4)
            else:
                act.wait_ge(sem["s_evac"], u0 + 6 * i + 5)
                act.wait_ge(sem["p_evac0"], u0 // 2 + 3 * i + 3)
            chain(act.activation(k.th[:, HALF:T], k.proj[:, n % 2, 0:T - HALF], ACT.Tanh, scale=0.5))
            act.activation(k.th[:, 0:HALF], k.proj_lo[:, 0:HALF], ACT.Tanh, scale=0.5).then_inc(sem["c_tanh"], 1)

    def chunk(u, c):
        f, m = cs_sums(c), P if c < QB else NS
        act.wait_ge(sem["dm_ready"], 5 * u + c + 1)
        chain(act.activation(k.dm[0:m, :, 0:m], k.dm[0:m, :, 0:m], ACT.Exp))
        if c:
            c_filled(act, k, "x", u, c - 1)
        act.activation(k.e[:, :, 0:m], k.s[:, f % 2, 0:HPG * m].rearrange("p (r l) -> p r l", r=HPG),
                       ACT.Exp).then_inc(c_read(k, "s", f), 1)

    def old_states(u, n):
        f = cr_state(n)
        c_filled(act, k, "r", u, f)
        if n >= 2:
            act.wait_ge(sem["hts_used"], 3 * u + n - 1)
        act.activation(k.hts[n % 2][:].rearrange("p q n -> p (q n)"), k.r[:, f % 2, :], ACT.Copy).then_inc(c_read(k, "r", f), 1)

    def stage(i, u, slots, units):
        for n in range(6):
            if units and n < QB:
                chunk(u, n)
            if slots:
                slot(i, n)
            if units and n == QB:
                chunk(u, QB)
                old_states(u, 0)
        for n in range(1, 4):
            if units:
                old_states(u, n)
        for j in range(2):
            if units:
                act.wait_ge(sem["g_made"], 2 * u + j + 1)
                act.wait_ge(sem["acc_added"], 2 * u)
                act.activation(k.sq[1][:, j, :], k.feat[2 + j][:], ACT.Square).then_inc(sem["g_squared"], 1)
        if slots and not units:
            act.wait_ge(sem["dec_in"], 1)
            act.activation(k.dec[:], k.dec[:], ACT.Exp).then_inc(sem["dt_made"], 1)
        for n in (1, 2):
            if slots:
                f = cs_tok(n)
                c_filled(act, k, "s", i, f)
                act.activation(k.xtok[:, 0:QB, (n - 1) * P:n * P], k.s[:, f % 2, :].rearrange("p (c q) -> p c q", c=QB),
                               ACT.Copy).then_inc(c_read(k, "s", f), 1)

    def high_parts(lo, hi):
        for at in (0, KT):
            l, h = max(lo, at), min(hi, at + KT)
            if l < h:
                chain(act.activation((k.xh, k.xl)[at // KT][:, l - at:h - at, :], k.out[:, l:h, :], ACT.Copy))

    stage(0, -1, True, False)
    with chain.loop("c", GROUPS - 1) as j:
        stage(j + 1, j, True, True)
    await_slot(act, k, s0 + 47)
    for n, (lo, hi) in enumerate(((0, KT), (KT, CT - 2))):
        act.wait_ge(sem["g_ready"], hi)
        high_parts(lo, hi)
        act.sem_inc(sem["g_high"], 1)
    stage(GROUPS, GROUPS - 1, False, True)
    act.wait_ge(sem["g_ready"], CT)
    high_parts(CT - 2, CT)
    act.sem_inc(sem["g_high"], 1)
    act.wait_ge(sem["ms_done"], 1)
    chain(act.activation(k.rs[:, 0:SEQ], k.s[:, 0, :], ACT.Sqrt, bias=k.eps[:], scale=D / INNER))
    act.activation(k.rs[:, SEQ:T], k.s[:, 1, 0:NS], ACT.Sqrt, bias=k.eps[:], scale=D / INNER).then_inc(sem["c_rms"], 1)
    s = s0 + 48

    def body(i, final):
        for n in range(4):
            if not (final and n == 3 and k.last == 2):
                split_high(act, k, s + 4 * i + n + 1, s // 2 + 2 * i + (n + 1) // 2, (n + 1) % 2)
    turns_of(chain, "c_out", KT // 2, body, peel=True)
    act.wait_ge(sem["ctails_out"], 128)
    ln_scalar(act, k, 2, chain)


def c_vector(dve, k, chain):
    sem, s0, u0 = k.sem, SLOT_C, USE_C
    dve.wait_ge(sem["c_consts"], 1)
    dve.wait_ge(sem["c_params"], 64)
    chain(dve.tensor_scalar(k.par_c[:, :, 0:5], k.par_c[:, :, 0:5], 0.5, None, ALU.mult))
    for r in range(2):
        chain(dve.tensor_copy(k.nw[:, r * KT:(r + 1) * KT], k.par_m[:, :, 8 + r]))
    for r in range(2):
        chain(dve.tensor_copy(k.dsk[64 * r:64 * r + 64, :], k.rowp[64 * r:64 * r + 64, 2, r::2]))
    dve.wait_ge(sem["dt_raw"], 1)
    bias = k.rowp[:, 0, :].unsqueeze(1)
    chain(dve.tensor_tensor(k.dt[:, 0:QB], k.x[:, 0:P].rearrange("p (c h) -> p c h", c=QB), bias.broadcast_to([P, QB, SSDH]), ALU.add))
    chain(dve.tensor_tensor(k.dt[0:NS, QB], k.x[0:NS, P:P + SSDH], k.rowp[0:NS, 0, :], ALU.add))
    flat = [t[:].rearrange("p c h -> p (c h)") for t in (k.dt, k.adt)]
    softplus_vector(dve, k, chain, flat[0], flat[1], k.spa[:], 2)
    chain(dve.tensor_copy(k.dt[:], k.adt[:]))
    dve.wait_ge(sem["a_exp"], 1)
    chain(dve.tensor_scalar(k.rowp[:, 1, :], k.rowp[:, 1, :], -1.0, None, ALU.mult))
    dve.tensor_tensor(k.adt[:], k.dt[:], k.rowp[:, 1:2, :].broadcast_to([P, CH, SSDH]), ALU.mult).then_inc(sem["adt_ready"], 1)

    def totals():
        dve.wait_ge(sem["sums_done"], 1)
        chain(dve.tensor_copy(k.cs[:, 0:QB], k.s[:, 0, 0:P].rearrange("p (c h) -> p c h", c=QB)))
        chain(dve.tensor_copy(k.cs[0:NS, QB], k.s[0:NS, 0, P:P + SSDH]))
        chain(dve.scalar_tensor_tensor(k.dec[:, 0:QB], k.s[:, 1, 0:P].rearrange("p (c h) -> p c h", c=QB), float(D), k.cs[:, 0:QB],
                                       ALU.mult, ALU.subtract))
        dve.tensor_tensor(k.dec[0:NS, QB], k.s[0:NS, 1, P:P + SSDH], k.cs[0:NS, QB], ALU.subtract).then_inc(sem["dec_in"], 1)
        dve.wait_ge(sem["dt_made"], 1)

    def convolutions(g):
        for n, tile in enumerate((CT + g, CT + GROUPS + g, 2 * g, 2 * g + 1)):
            chain(dve.tensor_scalar(k.curc[:, n, :], k.par_c[:, bass.ds(tile, 1), :].rearrange("p o c -> p (o c)"), 1.0, None, ALU.mult))

    def slot(g, n):
        if n < 4:
            cur = k.curc[:, n, :]
            chain(dve.tensor_copy(k.u_s[:, :, 0:HIST], cur[:, 5:29].rearrange("p (b t) -> p b t", b=NB)))
            dve.wait_ge(sem["s_evac"], u0 + 6 * g + n + 1)
            dve.wait_ge(sem[f"p_evac{n % 2}"], u0 // 2 + 3 * g + n // 2 + 1)
            tile = (CT + g, CT + GROUPS + g, 2 * g, 2 * g + 1)[n]
            tail = k.ctails[:, bass.ds(tile, 1), :].rearrange("p o c -> p (o c)")
            chain(dve.tensor_scalar(tail[:, 0:HIST], k.u[:, SEQ:SROW], 1.0, None, ALU.mult))
            chain(dve.tensor_scalar(tail[:, HIST:HN].rearrange("p (b t) -> p b t", b=NB), k.u_s[:, :, DT:WIN], 1.0, None, ALU.mult))
            convolve(dve, k, chain, cur, k.cc, "c_conv")
            dve.wait_ge(sem["c_tanh"], 6 * g + n + 1)
            dve.scalar_tensor_tensor(k.featn[n][:], k.th[:], 1.0, k.cc[:], ALU.add, ALU.mult).then_inc(sem["feat_ready"], 1)
            dve.wait_ge(sem["feat_ready"], 4 * g + n + 1)
        else:
            dve.wait_ge(sem["c_tanh"], 6 * g + n + 1)
            sz = k.szn[n - 4]
            dve.scalar_tensor_tensor(sz[:, 0:HALF], k.th[:, 0:HALF], 1.0, k.proj_lo[:, 0:HALF], ALU.add, ALU.mult).then_inc(sem["s_evac"], 1)
            dve.scalar_tensor_tensor(sz[:, HALF:T], k.th[:, HALF:T], 1.0, k.proj[:, n % 2, 0:T - HALF], ALU.add, ALU.mult).then_inc(sem[f"p_evac{n % 2}"], 1)

    def differences(g, c):
        n, mask, f = (P, k.negc, cs_sums(c)) if c < QB else (NS, k.negcs, cs_sums(c))
        c_filled(dve, k, "s", g, f)
        for r in range(HPG):
            step = dve.scalar_tensor_tensor(k.dm[0:n, r, 0:n], k.s[0:n, f % 2, r * n:r * n + n], k.cs_g[0:n, c, r:r + 1],
                                            mask[:], ALU.subtract, ALU.add)
            chain(step) if r < HPG - 1 else step.then_inc(sem["dm_ready"], 1)

    def chunk(g, c):
        n = P if c < QB else NS
        cols = slice(c * P, c * P + n)
        differences(g, c)
        if c:
            c_filled(dve, k, "x", g, c - 1)
            c_filled(dve, k, "r", g, cr_update(c - 1))
        x3 = k.xtok[0:n, c].rearrange("p (r q) -> p r q", r=HPG)
        xdt, xdd = (t[0:n].rearrange("p (r q) -> p r q", r=HPG) for t in (k.xdt, k.xdd))
        chain(dve.tensor_tensor(xdt, x3, k.dt_g[0:n, c].unsqueeze(2).broadcast_to([n, HPG, HD]), ALU.mult))
        chain(dve.tensor_tensor(xdd, xdt, k.dec_g[0:n, c].unsqueeze(2).broadcast_to([n, HPG, HD]), ALU.mult))
        c_was_read(dve, k, "s", g, cs_sums(c))
        f = cr_scores(c)
        c_filled(dve, k, "r", g, f)
        step = dve.tensor_tensor(k.m[0:n, :, 0:n], k.dm[0:n, :, 0:n], k.r[0:n, f % 2, 0:n].unsqueeze(1).broadcast_to([n, HPG, n]), ALU.mult)
        if c < QB:
            step.then_inc(c_read(k, "r", f), 1)
            chain(dve.tensor_copy(k.edec[:], k.e[:, :, P - 1]))
        else:
            chain(step)
            dve.wait_ge(sem["hp_out"], 16 * g)
            dve.tensor_copy(k.hout[:], k.r[:, f % 2, P:3 * P].rearrange("p (j n) -> p j n", j=2)).then_inc(c_read(k, "r", f), 1)
            c_was_read(dve, k, "r", g, f)
            for h in range(2):
                lo = slice(64 * h, 64 * h + 64)
                chain(dve.tensor_copy(k.decp[lo], k.e[lo, h:HPG:2, DT - 1:NS:DT]))
            dve.sem_inc(sem["hout_ready"], 1)
        dve.tensor_tensor(k.e[:, :, 0:n], k.e[:, :, 0:n], k.feat[1][:, cols].unsqueeze(1).broadcast_to([P, HPG, n]),
                          ALU.mult).then_inc(sem["y_in"], 1)

    def results(g, c):
        n = P if c < QB else NS
        c_filled(dve, k, "x", g, c)
        for j in range(2):
            t = k.feat[2 + j][:, c * P:c * P + n]
            step = dve.scalar_tensor_tensor(t, t, k.dsk[:, bass.ds(2 * g + j, 1)], k.x[:, j * P:j * P + n], ALU.mult, ALU.add)
            chain(step) if j == 0 else step.then_inc(sem["cx_read"], 1)
        if c < QB:
            f = cr_update(c)
            c_filled(dve, k, "r", g, f)
            h3 = k.ht[:].rearrange("p (r q) -> p r q", r=HPG)
            chain(dve.tensor_tensor(h3, h3, k.edec[:].unsqueeze(2).broadcast_to([P, HPG, HD]), ALU.mult))
            dve.tensor_tensor(k.ht[:], k.ht[:], k.r[:, f % 2, 0:2 * P], ALU.add).then_inc(c_read(k, "r", f), 1)
            c_was_read(dve, k, "r", g, f)

    def finish(g):
        for n in range(4):
            f = cs_state(n)
            c_filled(dve, k, "s", g, f)
            for b in range(4):
                at = n % 2 * 4 + b
                h = k.st0[:, n // 2, at, :]
                step = dve.scalar_tensor_tensor(h, h, k.decp[:, n // 2, at:at + 1], k.s[:, f % 2, b * P:(b + 1) * P], ALU.mult, ALU.add)
                chain(step) if b < 3 else step.then_inc(c_read(k, "s", f), 1)
            c_was_read(dve, k, "s", g, f)
        dve.sem_inc(sem["st_ready"], 1)
        c_was_read(dve, k, "x", g, QB)
        for j in range(2):
            t = k.feat[2 + j][:]
            dve.scalar_tensor_tensor(t, t, 0.5, k.sz[j][:], ALU.mult, ALU.mult).then_inc(sem["g_made"], 1)
            dve.wait_ge(sem["g_made"], 2 * g + j + 1)
            out = k.out[:, bass.ds(2 * g + j, 1), :].rearrange("p o t -> p (o t)")
            dve.tensor_scalar(out, t, k.nw[:, bass.ds(2 * g + j, 1)], None, ALU.mult).then_inc(sem["g_ready"], 1)
            dve.wait_ge(sem["g_ready"], 2 * g + j + 1)

    def take_over(g, units):
        if units:
            dve.wait_ge(sem["g_squared"], 2 * g)
        c_filled(dve, k, "s", g, cs_tok(0))
        dve.tensor_copy(k.btok[:, 0:QB], k.s[:, 0, :].rearrange("p (c n) -> p c n", c=QB)).then_inc(c_read(k, "s", 0), 1)
        c_filled(dve, k, "r", g, CR_TOK)
        chain(dve.tensor_copy(k.btok[0:NS, QB], k.r[0:NS, 0, 0:P]))
        dve.tensor_copy(k.xtok[0:NS, QB], k.r[0:NS, 0, P:3 * P]).then_inc(c_read(k, "r", CR_TOK), 1)
        for dst, src in ((k.dt_g, k.dt), (k.adt_g, k.adt), (k.cs_g, k.cs), (k.dec_g, k.dec)):
            chain(dve.tensor_scalar(dst[:], src[:, :, bass.ds(HPG * g, HPG)], 1.0, None, ALU.mult))
        chain(dve.memset(k.ht[:], 0.0))
        dve.wait_ge(sem["s_evac"], u0 + 6 * g + 6)
        for par in range(2):
            dve.wait_ge(sem[f"p_evac{par}"], u0 // 2 + 3 * g + 3)
        for n in range(4):
            chain(dve.tensor_copy(k.feat[n][:], k.featn[n][:]))
        dve.sem_inc(sem["group_params"], 1)
        for j in range(2):
            chain(dve.tensor_copy(k.sz[j][:], k.szn[j][:]))
        c_was_read(dve, k, "r", g, CR_TOK)
        for n in (1, 2):
            c_was_read(dve, k, "s", g, cs_tok(n))
        chain(dve.tensor_tensor(k.bm, k.btok[0:NS, QB:CH].broadcast_to([NS, NB, STATE]),
                                k.blk[:, 0:NS:DT].unsqueeze(2).broadcast_to([NS, NB, STATE]), ALU.mult))

    def stage(i, u, slots, units):
        if slots:
            convolutions(i)
        for n in range(6):
            if units and n < QB:
                chunk(u, n)
            if slots:
                split_low(dve, k, s0 + 6 * i + n + 1, (n + 1) % 2)
            if units and n < QB:
                results(u, n)
            if slots:
                slot(i, n)
            if units and n == QB:
                chunk(u, QB)
        if units:
            results(u, QB)
            finish(u)
        if slots and not units:
            totals()
        if slots:
            take_over(i, units)

    def low_parts(n, lo, hi):
        dve.wait_ge(sem["g_high"], n + 1)
        dve.wait_ge(sem["g_ready"], hi)
        for at in (0, KT):
            l, h = max(lo, at), min(hi, at + KT)
            if l < h:
                chain(dve.tensor_tensor(k.g[:, l:h, :], k.out[:, l:h, :], (k.xh, k.xl)[at // KT][:, l - at:h - at, :], ALU.subtract))
        dve.sem_inc(sem["g_split"], 1)

    stage(0, -1, True, False)
    with chain.loop("c", GROUPS - 1) as j:
        stage(j + 1, j, True, True)
    stage(GROUPS, GROUPS - 1, False, True)
    low_parts(0, 0, KT)
    low_parts(1, KT, CT - 2)
    low_parts(2, CT - 2, CT)
    dve.wait_ge(sem["ctails_turned"], 1)
    dve.tensor_copy(k.rows[1][0:4 * HN, :].rearrange("p (b c) -> p b c", b=2), k.r[0:4 * HN]).then_inc(sem["ctails_read"], 1)
    dve.wait_ge(sem["c_rms"], 1)
    chain(dve.reciprocal(k.rs[:], k.rs[:]))
    s, u = s0 + 48, u0 + 48

    def body(i, final):
        for h in range(2):
            for n in range(2):
                if not (final and h == 1 and n == 1 and k.last == 2):
                    split_low(dve, k, s + 4 * i + 2 * h + n + 1, 1 - n)
            await_slot(dve, k, s + 4 * i + 2 * h + 1)
            dve.tensor_tensor(k.cc[:, HALF:T], k.proj[:, h, 0:T - HALF], k.rs[:, HALF:T], ALU.mult).then_inc(sem[f"p_evac{h}"], 1)
            dve.tensor_tensor(k.cc[:, 0:HALF], k.proj_lo[:, 0:HALF], k.rs[:, 0:HALF], ALU.mult).then_inc(sem["s_evac"], 1)
            dve.wait_ge(sem[f"p_evac{h}"], u // 2 + i + 1)
            dve.wait_ge(sem["s_evac"], u + 2 * i + h + 1)
            x = k.xT[:, bass.ds(2 * i + h, 1), :].rearrange("p o t -> p (o t)")
            dve.scalar_tensor_tensor(x, x, ALPHA, k.cc[:], ALU.mult, ALU.add).then_inc(sem["c_x"], 1)
            dve.wait_ge(sem["c_x"], 2 * i + h + 1)
    turns_of(chain, "c_out", KT // 2, body, peel=True)
    ln_vector(dve, k, 2, chain)



USE_END = [24, 64, 120, 144]


def out_sync(sp, k, s, w):
    with sp.Fori(0, KT // 2) as i:
        col = [sp.snap((2 * i + h) * P) for h in range(2)]
        for h in range(2):
            load_slot(sp, k, s + 2 * i + h, h, w[:, bass.ds(col[h], P)])


def out_tensor(pe, k, s, u):
    with pe.Fori(0, KT // 2) as i:
        for h in range(2):
            multiply_slot(pe, k, s + 2 * i + h, h, u + 2 * i + h, u // 2 + i, h, k.gh, k.gl)


def out_scalar(act, k, s, chain, last, ahead=1):
    def body(i, final):
        for h in range(2):
            n = h + ahead
            if not (final and (n == 3 or n == 2 and last)):
                split_high(act, k, s + 2 * i + n, s // 2 + i + n // 2, n % 2)
    turns_of(chain, "out", KT // 2, body, peel=True)


def out_vector(dve, k, s, u, chain, last, ahead=1):
    def body(i, final):
        for h in range(2):
            n = h + ahead
            if ahead == 2:
                await_slot(dve, k, s + 2 * i + h)
            if not (final and (n == 3 or n == 2 and last)):
                split_low(dve, k, s + 2 * i + n, n % 2)
            if ahead == 1:
                await_slot(dve, k, s + 2 * i + h)
            x = k.xT[:, bass.ds(2 * i + h, 1), :].rearrange("p o t -> p (o t)")
            dve.scalar_tensor_tensor(x[:, HALF:T], x[:, HALF:T], ALPHA, k.proj[:, h, 0:T - HALF], ALU.mult, ALU.add).then_inc(k.sem[f"p_evac{h}"], 1)
            dve.scalar_tensor_tensor(x[:, 0:HALF], x[:, 0:HALF], ALPHA, k.proj_lo[:, 0:HALF], ALU.mult, ALU.add).then_inc(k.sem["s_evac"], 1)
    turns_of(chain, "out", KT // 2, body, peel=True)


def ln_tensor(pe, k, layer):
    sem, u = k.sem, USE_END[layer]
    for h in range(2):
        pe.wait_ge(sem[f"p_evac{h}"], u // 2)
    pe.wait_ge(sem["s_evac"], u)
    if layer == 2:
        pe.wait_ge(sem["c_x"], KT)
    for i in range(KT):
        pe.matmul(k.s[:, 0, :], k.ones_d[:], k.xT[:, i, 0:SEQ], start=i == 0, stop=i == KT - 1)
    for i in range(KT):
        mm = pe.matmul(k.r[:, 0, 0:NS], k.ones_d[:], k.xT[:, i, SEQ:T], start=i == 0, stop=i == KT - 1)
    mm.then_inc(sem["ln_mean"], 1)
    for i in range(KT):
        if i % 2 == 0:
            pe.wait_ge(sem["ln_sq"], 4 * layer + i // 2 + 1)
        pe.matmul(k.s[:, 1, :], k.ones_d[:], k.sq[i // 2 % 2][:, i % 2, 0:SEQ], start=i == 0, stop=i == KT - 1)
        mm = pe.matmul(k.r[:, 1, 0:NS], k.ones_d[:], k.sq[i // 2 % 2][:, i % 2, SEQ:T], start=i == 0, stop=i == KT - 1)
        if i % 2:
            mm.then_inc(sem["ln_acc"], 1)


def ln_scalar(act, k, layer, chain):
    sem = k.sem
    for j in range(KT // 2):
        act.wait_ge(sem["ln_sub"], 4 * layer + j + 1)
        if 4 * layer + j >= 2:
            act.wait_ge(sem["ln_acc"], 4 * layer + j - 1)
        act.activation(k.sq[j % 2][:], k.xT[:, 2 * j:2 * j + 2, :], ACT.Square).then_inc(sem["ln_sq"], 1)
    act.wait_ge(sem["ln_acc"], 4 * layer + 4)
    chain(act.activation(k.rs[:, 0:SEQ], k.s[:, 1, :], ACT.Sqrt, bias=k.eps[:]))
    act.activation(k.rs[:, SEQ:T], k.r[:, 1, 0:NS], ACT.Sqrt, bias=k.eps[:]).then_inc(sem["ln_sd"], 1)
    for i in range(KT):
        act.wait_ge(sem["ln_norm"], 8 * layer + i + 1)
        bias = k.par_m[:, i, 4 + layer:5 + layer]
        act.activation(k.xT[:, i, :], k.xT[:, i, :], ACT.Identity, bias=bias).then_inc(sem["ln_x"], 1)
        if layer < k.last:
            act.wait_ge(sem["ln_x"], 8 * layer + i + 1)
            act.activation(k.xh[:, i, :], k.xT[:, i, :], ACT.Copy).then_inc(sem["ln_xh"], 1)


def ln_vector(dve, k, layer, chain):
    sem = k.sem
    dve.wait_ge(sem["ln_mean"], layer + 1)
    for j in range(KT // 2):
        x = k.xT[:, 2 * j:2 * j + 2, :]
        chain(dve.tensor_tensor(x[:, :, 0:SEQ], x[:, :, 0:SEQ], k.s[:, 0:1, :].broadcast_to([P, 2, SEQ]), ALU.subtract))
        dve.tensor_tensor(x[:, :, SEQ:T], x[:, :, SEQ:T], k.r[:, 0:1, 0:NS].broadcast_to([P, 2, NS]),
                          ALU.subtract).then_inc(sem["ln_sub"], 1)
    dve.wait_ge(sem["ln_sd"], layer + 1)
    chain(dve.reciprocal(k.rs[:], k.rs[:]))
    dve.wait_ge(sem["ln_sub"], 4 * layer + 4)

    def low(i):
        dve.wait_ge(sem["ln_xh"], 8 * layer + i + 1)
        sub = dve.tensor_tensor(k.xl[:, i, :], k.xT[:, i, :], k.xh[:, i, :], ALU.subtract)
        chain(sub) if i < KT - 1 else sub.then_inc(sem["x_ready"], 1)

    for i in range(KT + 1):
        if i < KT:
            dve.scalar_tensor_tensor(k.xT[:, i, :], k.xT[:, i, :], k.par_m[:, i, layer:layer + 1], k.rs[:],
                                     ALU.mult, ALU.mult).then_inc(sem["ln_norm"], 1)
        if i and layer < k.last:
            low(i - 1)



def y_tensor(pe, k, layer):
    pe.wait_ge(k.sem["ln_x"], 8 * layer + 8)
    for c in range(CH):
        n = P if c < QB else NS
        bank = (k.s, k.r)[c % 2]
        if c >= 2:
            pe.wait_ge(k.sem[f"y_read{c % 2}"], c // 2)
        for i in range(KT):
            t = pe.transpose(bank[0:n, i // 4, (i % 4) * P:(i % 4) * P + P], k.xT[:, i, c * P:c * P + n], k.ident[:, :])
        t.then_inc(k.sem["y_turned"], 1)


def y_copy(eng, k, c, op):
    n = P if c < QB else NS
    eng.wait_ge(k.sem["y_turned"], c + 1)
    if c >= 2:
        eng.wait_ge(k.sem[f"y_out{c % 2}"], 16 * (c // 2))
    op(k.rows[c % 2][0:n, :].rearrange("p (b c) -> p b c", b=2), (k.s, k.r)[c % 2][0:n, :, :]).then_inc(k.sem[f"y_read{c % 2}"], 1)


def y_sync(sp, k, o):
    for c in range(CH):
        n = P if c < QB else NS
        dst = o["y_prompt"][0, c * P:(c + 1) * P, :] if c < QB else o["y_sample"].rearrange("b t d -> (b t) d")
        sp.wait_ge(k.sem[f"y_read{c % 2}"], c // 2 + 1)
        sp.dma_start(dst, k.rows[c % 2][0:n, :]).then_inc(k.sem[f"y_out{c % 2}"], 16)
    sp.wait_ge(k.sem["y_out0"], 48)
    sp.wait_ge(k.sem["y_out1"], 32)



def layer_a_buffers(k):
    k.cur = k.sb("cur", [P, 45])
    k.gw = k.sb("gate_w", [P, 2, P])
    k.tg, k.tr, k.ti, k.t, k.rt = (k.sb(n, [P, T]) for n in ("tg", "tr", "ti", "t", "rt"))
    k.sg, k.q, k.a, k.a2, k.gi, k.h, k.cx = (k.sb(n, [P, T]) for n in ("sg", "q", "a", "a2", "gi", "h", "cx"))
    k.h0a = k.sb("h0a", [P, NB])
    k.tails_sb = k.sb("tails_sb", [P, 3 * P])
    k.tails = k.sb("tails", [P, KT, AN])


def conv_buffers(k):
    k.u = k.sb("u", [P, UW])
    k.u_s = k.u[:, SROW:UW].rearrange("p (b t) -> p b t", b=NB)
    conv = k.sb("conv", [P, UW])
    k.conv_s = conv[:, SROW:UW].rearrange("p (b t) -> p b t", b=NB)
    k.conv = conv[:, 0:CW]


def scoped(nc, k, make):
    with ExitStack() as ctx:
        k.sb = lambda name, shape, dtype=F32: ctx.enter_context(nc.sbuf_tensor(name, shape, dtype))
        make(k)


def build(nc, a, o):
    with ExitStack() as ctx:
        k = allocate(nc, ctx)
        k.last = DEPTH - 1
        k.par_c = k.sb("par_c", [P, CONV_C // P, 29])
        k.par_d = [k.sb(f"par_d{j}", [P, 5, KT]) for j in range(2)]
        k.spx, k.spy = k.sb("spx", [P, 2 * KT]), k.sb("spy", [P, 2 * KT])
        k.spa = k.rs[:, 0:3 * CH * SSDH].rearrange("p (a n) -> p a n", a=3)
        conv_buffers(k)
        scoped(nc, k, layer_a_buffers)
        scoped(nc, k, layer_b_buffers)
        scoped(nc, k, layer_c_buffers)
        block = ctx.enter_context(nc.Block())

        @block.sync
        def _(sp):
            prologue_sync(sp, k, a)
            a_sync(sp, k, a, 0, [b_cols(a, 0, 0), b_cols(a, 1, 0)])
            b_sync(sp, k, a, [a["c_in_w"][0][:, c_cols(0, n):c_cols(0, n) + P] for n in range(2)])
            c_sync(sp, k, a, [a_slot(a, 1, n) for n in range(2)])
            a_sync(sp, k, a, 1, None)
            y_sync(sp, k, o)

        @block.gpsimd
        def _(pool):
            chain = Chain(pool, k.sem["chain_pool"], STEPS, "pool")
            prologue_pool(pool, k, chain)
            tails_stores(pool, k, a, o, 0)
            b_pool(pool, k, o, chain)
            c_pool(pool, k, o, chain)
            pool.wait_ge(k.sem["ctails_out"], 128)
            pool.wait_ge(k.sem["st_out"], 256)
            pool.wait_ge(k.sem["hp_out"], 128)
            pool.wait_ge(k.sem["x_ready"], 4)
            pool.memset(k.gw[:], 0.0).then_inc(k.sem["consts"], 1)
            tails_stores(pool, k, a, o, 1)
            pool.wait_ge(k.sem["kv_out"], 256)
            pool.wait_ge(k.sem["tails_out"], TAILS_OUT * 2)

        @block.tensor
        def _(pe):
            pe.sem_inc(k.sem["pe_slot"], 1)
            prologue_tensor(pe, k, a)
            a_tensor(pe, k, 0)
            b_tensor(pe, k)
            c_tensor(pe, k)
            a_tensor(pe, k, 1)
            y_tensor(pe, k, k.last)

        @block.scalar
        def _(act):
            chain = Chain(act, k.sem["chain_act"], STEPS, "act")
            prologue_scalar(act, k, a)
            a_scalar(act, k, 0, chain)
            b_scalar(act, k, chain)
            c_scalar(act, k, chain)
            a_scalar(act, k, 1, chain)
            for c in range(0, CH, 2):
                y_copy(act, k, c, lambda d, s: act.activation(d, s, ACT.Copy))

        @block.vector
        def _(dve):
            chain = Chain(dve, k.sem["chain_dve"], STEPS, "dve")
            dve.sem_inc(k.sem["w_lo"], 1)
            prologue_vector(dve, k, a, chain)
            a_vector(dve, k, 0, chain)
            b_vector(dve, k, chain)
            c_vector(dve, k, chain)
            a_vector(dve, k, 1, chain)
            for c in range(1, CH, 2):
                y_copy(dve, k, c, dve.tensor_copy)


INS = """x_prompt x_sample cache_k cache_v page_table state_lru_conv state_lru_h state_ssd_conv state_ssd_h
    ln_g ln_b a_in_w a_conv_w a_conv_b a_gate_r_w a_gate_r_b a_gate_i_w a_gate_i_b a_lambda a_out_w
    b_in_w b_lambda b_subln_w b_out_w c_in_w c_conv_w c_conv_b c_dt_bias c_a_log c_d c_norm_w c_out_w""".split()
OUTS = dict(
    y_prompt=(1, 512, 1024), y_sample=(8, 4, 1024), k_prompt=(1, 1, 512, 8, 2, 64), v_prompt=(1, 1, 512, 8, 128),
    k_sample=(1, 8, 4, 8, 2, 64), v_sample=(1, 8, 4, 8, 128), lru_conv_prompt=(2, 1, 3, 1024),
    lru_h_prompt=(2, 1, 1024), lru_conv_sample=(2, 8, 3, 1024), lru_h_sample=(2, 8, 1024),
    ssd_conv_prompt=(1, 1, 3, 4096), ssd_h_prompt=(1, 1, 32, 64, 128), ssd_conv_sample=(1, 8, 3, 4096),
    ssd_h_sample=(1, 8, 32, 64, 128))


def kernel(**inputs):
    import numpy as np
    import concourse.bacc as bacc
    from concourse.bass_utils import run_bass_kernel_spmd

    nc = bacc.Bacc("TRN2", target_bir_lowering=False, num_devices=1)
    arrays, a, o = {}, {}, {}
    for name in INS:
        arrays[f"in_{name}"] = np.ascontiguousarray(inputs[name])
        a[name] = nc.dram_tensor(f"in_{name}", arrays[f"in_{name}"].shape,
                                 mybir.dt.from_np(arrays[f"in_{name}"].dtype), kind="ExternalInput").ap()
    for name, shape in OUTS.items():
        o[name] = nc.dram_tensor(f"out_{name}", shape, F32, kind="ExternalOutput").ap()
    build(nc, a, o)
    r = run_bass_kernel_spmd(nc, [arrays], core_ids=[0])
    return tuple(r.results[0][f"out_{name}"] for name in OUTS)
```

```python
import math
from contextlib import ExitStack, contextmanager

import concourse.bass as bass
from concourse import mybir

F32 = mybir.dt.float32
F32R = mybir.dt.float32r
I32 = mybir.dt.int32
ALU = mybir.AluOpType
ACT = mybir.ActivationFunctionType
AX = mybir.AxisListType

P = 128
D = 1024
KT = D // P
SEQ, NB, DT = 512, 8, 4
NS = NB * DT
T = SEQ + NS
TAPS = 4
HIST = TAPS - 1
WIN = HIST + DT
UW = HIST + SEQ + NB * WIN
CW = UW - HIST
SROW = HIST + SEQ
HALF = SEQ // 2
DEPTH = 4
ALPHA = (2.0 * DEPTH) ** 0.25
EPS = 1e-5
QB = SEQ // P
CH = QB + 1
HEADS, DH = 8, 64
PAGES, PAGE = 8, 128
GROUPS, HPG, HD, STATE = 8, 4, 64, 128
SSDH = GROUPS * HPG
INNER = SSDH * HD
CT = INNER // P
CONV_C = INNER + 2 * GROUPS * STATE
NEG = -1e30
LAM_INIT = 0.8 - 0.6 * math.exp(-0.3)
HN = HIST + NB * HIST
AN = HN + 1 + NB

TAILS_OUT = 16 * 4 * (3 + 2)

STEPS = {("act", "a"): 6, ("act", "out"): 0, ("act", "b"): 29, ("act", "c"): 11, ("act", "c_out"): 0,
         ("dve", "a"): 18, ("dve", "out"): 0, ("dve", "b"): 106, ("dve", "c"): 98, ("dve", "c_out"): 0}

SLOT_A = [0, 128]
USE_A = [0, 120]
SLOT_B = USE_B = 24
SLOT_C = USE_C = 64


class Chain:

    def __init__(self, eng, sem, steps, engine):
        self.eng, self.sem, self.steps, self.engine = eng, sem, steps, engine
        self.count, self.turn, self.per = 0, None, 0

    def __call__(self, instruction):
        instruction.then_inc(self.sem, 1)
        self.count += 1
        value = self.count if self.turn is None else self.turn * self.per + self.count
        self.eng.wait_ge(self.sem, value)

    @contextmanager
    def loop(self, name, turns):
        start = self.count
        self.per = self.steps[self.engine, name]
        with self.eng.Fori(0, turns) as i:
            self.turn = i
            yield i
            took = self.count - start
        assert took == self.per, (self.engine, name, took)
        self.turn = None
        self.count = start + turns * self.per


def turns_of(chain, name, n, body, peel=False):
    with chain.loop(name, n - peel) as i:
        body(i, False)
    if peel:
        body(n - 1, True)


def tokens_of(ap):
    return ap[:, 0:SEQ], ap[:, SEQ:T]


class Chip:
    pass


def allocate(nc, ctx):
    k = Chip()

    def sb(name, shape, dtype=F32):
        return ctx.enter_context(nc.sbuf_tensor(name, shape, dtype))

    def ps(name, shape):
        return ctx.enter_context(nc.psum_tensor(name, shape, F32))

    k.sb = sb
    k.xT = sb("xT", [P, KT, T])
    k.xh = sb("xh", [P, KT, T], F32R)
    k.xl = sb("xl", [P, KT, T], F32R)
    with nc.sbuf_tensor("branch", [P, CT, T], F32) as k.out:
        pass
    k.g = sb("g", [P, 2 * KT, T], F32R)
    k.gh, k.gl = k.g[:, 0:KT, :], k.g[:, KT:2 * KT, :]
    k.sq = [sb(f"sq{j}", [P, 2, T]) for j in range(2)]
    k.rows = [q.rearrange("p a t -> p (a t)")[:, 0:D] for q in k.sq]
    k.raw = [sb(f"w_raw{j}", [P, KT, P]) for j in range(2)]
    k.wh = [sb(f"w_high{j}", [P, KT, P], F32R) for j in range(2)]
    k.wl = [sb(f"w_low{j}", [P, KT, P], F32R) for j in range(2)]
    k.ident = sb("ident", [P, P])
    k.tri = sb("tri", [P, P])
    k.ones_d = sb("ones_d", [P, P])
    k.eps = sb("eps", [P, 1])
    k.par_a = [sb(f"par_a{j}", [P, KT, 40]) for j in range(2)]
    k.par_m = sb("par_m", [P, KT, 10])
    k.rs = sb("rs", [P, T])

    k.proj = ps("proj", [P, 2, 512])
    k.proj_lo = ps("proj_lo", [P, 512])
    k.s = ps("s", [P, 2, 512])
    k.r = ps("r", [P, 2, 512])
    k.x = ps("x", [P, 512])

    names = """w_landed0 w_landed1 w_hi w_lo pe_slot p_evac0 p_evac1 s_evac x_ready x_tile ln_sum
        rows_landed0 rows_landed1 rows_turned rows_read consts chain_act chain_dve chain_pool
        sp_in sp_out params x_split
        gw_landed  conv_done gates_done a_rest al_ready gi_ready q_in ti_ready t_ready rt_ready tg_ready
        tails_turned tails_read tails_out
        ln_mean ln_sub ln_sq ln_acc ln_sd ln_norm ln_x ln_xh
        table_in b_params b_consts lam_in lam_exp r_done r_read0 r_read1 s_done s_read x_done x_read
        q_ready gates_copied x_back o_copied k_landed0 k_landed1 v_landed0 v_landed1 tok_ready kv_out tgb_ready pm_ready w_ready sm_ready
        c_ready o_squared b_head
        c_params c_consts dt_raw adt_ready sums_done a_exp dec_in dt_made st_landed st_ready st_out hout_ready hp_out
        g_squared g_made g_ready g_high g_split acc_added ctails_turned ctails_read ctails_out y_in hts_used feat_ready group_params
        ms_done c_rms c_x c_conv c_tanh dm_ready cs_done cs_read0 cs_read1 cr_done cr_read0 cr_read1 cx_done cx_read
        y_turned y_read0 y_read1 y_out0 y_out1 done""".split()
    k.sem = {}
    for name in names:
        k.sem[name] = ctx.enter_context(nc.semaphore(name))
    return k



def load_slot(sp, k, s, par, rows):
    sp.wait_ge(k.sem["w_lo"], s)
    sp.dma_start(k.raw[par][:], rows.rearrange("(k p) n -> p k n", p=P)).then_inc(k.sem[f"w_landed{par}"], 16)


def split_high(act, k, s, half, par):
    act.wait_ge(k.sem[f"w_landed{par}"], 16 * half + 16)
    act.wait_ge(k.sem["pe_slot"], s)
    act.activation(k.wh[par][:], k.raw[par][:], ACT.Copy).then_inc(k.sem["w_hi"], 1)


def split_low(pool, k, s, par):
    pool.wait_ge(k.sem["w_hi"], s + 1)
    pool.wait_ge(k.sem["pe_slot"], s)
    pool.tensor_tensor(k.wl[par][:], k.raw[par][:], k.wh[par][:], ALU.subtract).then_inc(k.sem["w_lo"], 1)


def low_parts(pool, k, first, count):
    with pool.Fori(0, count // 2) as i:
        for n in range(2):
            split_low(pool, k, first + 2 * i + n, (first + n) % 2)
    if count % 2:
        split_low(pool, k, first + count - 1, (first + count - 1) % 2)


def multiply_slot(pe, k, s, par, use, use_half, upar, mh, ml, k0=0, first=True, last=True):
    pe.wait_ge(k.sem["w_lo"], s + 2)
    if first:
        pe.wait_ge(k.sem[f"p_evac{upar}"], use_half)
    for cols, out in ((slice(HALF, T), k.proj[:, upar, 0:T - HALF]), (slice(0, HALF), k.proj_lo[:, 0:HALF])):
        if first and cols.start == 0:
            pe.wait_ge(k.sem["s_evac"], use)
        for i in range(KT):
            for n, (w, m) in enumerate(((k.wh, mh), (k.wh, ml), (k.wl, mh))):
                mm = pe.matmul(out, w[par][:, i, :], m[:, k0 + i, cols],
                               start=first and i == 0 and n == 0, stop=last and i == KT - 1 and n == 2)
    mm.then_inc(k.sem["pe_slot"], 1)


def multiply_as_made(pe, k, s, use, mh, ml, made, steps):
    pe.wait_ge(k.sem["w_lo"], s + 2)
    pe.wait_ge(k.sem["p_evac0"], use // 2)
    pe.wait_ge(k.sem["s_evac"], use)
    for count, tiles in steps:
        pe.wait_ge(k.sem[made], count)
        for cols, out in ((slice(HALF, T), k.proj[:, 0, 0:T - HALF]), (slice(0, HALF), k.proj_lo[:, 0:HALF])):
            for i in tiles:
                for n, (w, m) in enumerate(((k.wh, mh), (k.wh, ml), (k.wl, mh))):
                    mm = pe.matmul(out, w[0][:, i, :], m[:, i, cols],
                                   start=i == 0 and n == 0, stop=i == KT - 1 and n == 2)
    mm.then_inc(k.sem["pe_slot"], 1)


def multiply_new_x(pe, k, s, use, layer):
    multiply_as_made(pe, k, s, use, k.xh, k.xl, "x_tile", [(KT * (layer - 1) + i + 1, (i,)) for i in range(KT)])


def multiply_last_made(pe, k, s, use, made, count):
    multiply_as_made(pe, k, s, use, k.gh, k.gl, made, [(count - 1, range(KT - 1)), (count, (KT - 1,))])


def await_slot(eng, k, s):
    eng.wait_ge(k.sem["pe_slot"], s + 2)



def row_jobs(a):
    xp = a["x_prompt"].rearrange("b t d -> (b t) d")
    jobs = [("x", c, P, [(0, P, xp[c * P:(c + 1) * P, :])]) for c in range(QB)]
    jobs.append(("x", QB, NS, [(0, NS, a["x_sample"].rearrange("b t d -> (b t) d"))]))
    for j in range(2):
        one = [a["a_conv_b"], a["a_gate_r_b"], a["a_gate_i_b"], a["a_lambda"]]
        jobs.append(("a", j, 40, [(0, 4, a["a_conv_w"][j])]
                     + [(4 + n, 1, v[j:j + 1, :]) for n, v in enumerate(one)]
                     + [(8, 24, a["state_lru_conv"][j].rearrange("b k d -> (b k) d")),
                        (32, 8, a["state_lru_h"][j])]))
    jobs.append(("m", 0, 10, [(0, 4, a["ln_g"]), (4, 4, a["ln_b"]),
                              (8, 2, a["c_norm_w"].rearrange("a (r d) -> (a r) d", r=2))]))
    for q in range(CONV_C // D):
        cols = slice(q * D, (q + 1) * D)
        jobs.append(("c", q, 29, [(0, 4, a["c_conv_w"][0][:, cols]), (4, 1, a["c_conv_b"][:, cols]),
                                  (5, 24, a["state_ssd_conv"][0].rearrange("b k d -> (b k) d")[:, cols])]))
    return jobs


def prologue_sync(sp, k, a):
    landed = [0, 0]
    for j, (_, _, _, parts) in enumerate(row_jobs(a)):
        if j == 2:
            for s in range(2):
                load_slot(sp, k, s, s, a_slot(a, 0, s))
        if j >= 2:
            sp.wait_ge(k.sem["rows_turned"], j - 1)
        for at, n, src in parts:
            sp.dma_start(k.rows[j % 2][at:at + n, :], src).then_inc(k.sem[f"rows_landed{j % 2}"], 16)


def a_slot(a, j, n):
    col = (1 - n % 2) * D + (n // 2) * P
    return a["a_in_w"][j][:, col:col + P]


def prologue_pool(pool, k, chain):
    sem = k.sem
    for t, v in ((k.ident, 0.0), (k.tri, 1.0), (k.ones_d, 1.0 / D), (k.eps, EPS), (k.gw, 0.0), (k.u, 0.0)):
        chain(pool.memset(t[:], v))
    chain(pool.affine_select(out=k.ident[:], in_=k.ident[:], compare_op=ALU.not_equal, fill=1.0,
                             base=0, pattern=[[-1, P]], channel_multiplier=1))
    pool.affine_select(out=k.tri[:], in_=k.tri[:], compare_op=ALU.is_ge, fill=0.0,
                       base=0, pattern=[[1, P]], channel_multiplier=-1).then_inc(sem["consts"], 1)
    split_low(pool, k, 0, 0)


def prologue_tensor(pe, k, a):
    sem = k.sem
    pe.wait_ge(sem["consts"], 1)
    landed = [0, 0]
    for j, (_, _, n, parts) in enumerate(row_jobs(a)):
        landed[j % 2] += 16 * len(parts)
        pe.wait_ge(sem[f"rows_landed{j % 2}"], landed[j % 2])
        if j >= 2:
            pe.wait_ge(sem["rows_read"], j - 1)
        bank = (k.s, k.r)[j % 2]
        for i in range(KT):
            t = pe.transpose(bank[:, i // 4, (i % 4) * n:(i % 4) * n + n],
                             k.rows[j % 2][0:n, i * P:(i + 1) * P], k.ident[0:n, 0:n])
        t.then_inc(sem["rows_turned"], 1)


def prologue_vector(dve, k, a, chain):
    sem = k.sem
    dve.wait_ge(sem["consts"], 1)
    for j, (kind, c, n, _) in enumerate(row_jobs(a)):
        dve.wait_ge(sem["rows_turned"], j + 1)
        bank = (k.s, k.r)[j % 2]
        dst = {"x": lambda: k.xT[:, :, c * P:c * P + n], "a": lambda: k.par_a[c][:],
               "m": lambda: k.par_m[:], "c": lambda: k.par_c[:, c * KT:(c + 1) * KT, :]}[kind]()
        dve.tensor_copy(dst.rearrange("p (b i) n -> p b i n", b=2),
                        bank[:, :, 0:4 * n].rearrange("p b (i n) -> p b i n", i=4)).then_inc(sem["rows_read"], 1)
        if j == CH - 1:
            dve.wait_ge(sem["x_split"], 1)
            dve.tensor_tensor(k.xl[:], k.xT[:], k.xh[:], ALU.subtract).then_inc(sem["x_ready"], 1)
    dve.wait_ge(sem["rows_read"], len(row_jobs(a)))
    for j in range(2):
        d = k.par_d[j]
        chain(dve.tensor_scalar(d[:, 0:2, :].rearrange("p c i -> p i c"), k.par_a[j][:, :, 5:7], 0.5, None, ALU.mult))
        chain(dve.tensor_scalar(k.spx[:, j * KT:(j + 1) * KT], k.par_a[j][:, :, 7], -1.0, None, ALU.mult))
    softplus_vector(dve, k, chain, k.spx[:], k.spy[:], k.spa[:, :, 0:2 * KT], 1)
    for j in range(2):
        for n, factor in enumerate((4.0, -4.0, -8.0)):
            chain(dve.tensor_scalar(k.par_d[j][:, 2 + n, :], k.spy[:, j * KT:(j + 1) * KT], factor, None, ALU.mult))


def softplus_vector(dve, k, chain, x, y, tmp, call):
    a, s, p = tmp[:, 0], tmp[:, 1], tmp[:, 2]
    chain(dve.tensor_scalar(a, x, -1.0, None, ALU.mult))
    dve.tensor_tensor(a, a, x, ALU.max).then_inc(k.sem["sp_in"], 1)
    dve.wait_ge(k.sem["sp_out"], call)
    chain(dve.tensor_scalar(s, a, 2.0, None, ALU.add))
    chain(dve.reciprocal(s, s))
    chain(dve.tensor_tensor(s, s, a, ALU.mult))
    chain(dve.tensor_tensor(a, s, s, ALU.mult))
    chain(dve.tensor_scalar(p, a, 1.0 / 15, None, ALU.mult))
    for n in (13, 11, 9, 7, 5, 3):
        chain(dve.scalar_tensor_tensor(p, p, 1.0 / n, a, ALU.add, ALU.mult))
    chain(dve.scalar_tensor_tensor(p, p, 1.0, s, ALU.add, ALU.mult))
    chain(dve.tensor_scalar(a, x, 0.0, None, ALU.max))
    chain(dve.scalar_tensor_tensor(y, p, 2.0, a, ALU.mult, ALU.add))


def softplus_scalar(act, k, tmp, call):
    act.wait_ge(k.sem["sp_in"], call)
    act.activation(tmp[:, 0], tmp[:, 0], ACT.Exp, scale=-1.0).then_inc(k.sem["sp_out"], 1)


def prologue_scalar(act, k, a):
    split_high(act, k, 0, 0, 0)
    act.wait_ge(k.sem["rows_read"], CH)
    act.activation(k.xh[:], k.xT[:], ACT.Copy).then_inc(k.sem["x_split"], 1)
    softplus_scalar(act, k, k.spa[:, :, 0:2 * KT], 1)



def a_sync(sp, k, a, o, j, nxt):
    s0, sem = SLOT_A[j], k.sem
    g_w = [a["a_gate_r_w"][j], a["a_gate_i_w"][j]]

    def gates(i, block):
        sp.wait_ge(sem["gates_done"], 8 * j + i)
        for n in range(2):
            for h in range(2):
                sp.dma_start(k.gw[h * 64:h * 64 + 64, n, h * 64:h * 64 + 64],
                             g_w[n][bass.ds(block[h], 1), :, :].rearrange("o a b -> (o a) b")).then_inc(sem["gw_landed"], 16)

    sp.wait_ge(sem["consts"], 1 + j)
    with sp.Fori(0, KT - 1) as i:
        cols = [sp.snap(i * P + P + D), sp.snap(i * P + P)]
        block = [sp.snap(2 * i), sp.snap(2 * i + 1)]
        for h in range(2):
            load_slot(sp, k, s0 + 2 + 2 * i + h, h, a["a_in_w"][j][:, bass.ds(cols[h], P)])
        gates(i, block)
    gates(KT - 1, [2 * KT - 2, 2 * KT - 1])
    out_sync(sp, k, s0 + 16, a["a_out_w"][j], 0, 2)
    tails_stores(sp, k, o, j)
    out_sync(sp, k, s0 + 16, a["a_out_w"][j], 2, 4)
    for h in range(2):
        if nxt:
            load_slot(sp, k, s0 + 24 + h, h, nxt[h])


def a_tensor(pe, k, j):
    s0, u0, sem = SLOT_A[j], USE_A[j], k.sem

    def tile(i, new_x):
        if new_x:
            multiply_new_x(pe, k, s0, u0, 3)
        else:
            multiply_slot(pe, k, s0 + 2 * i, 0, u0 + 2 * i, u0 // 2 + i, 0, k.xh, k.xl)
        multiply_slot(pe, k, s0 + 2 * i + 1, 1, u0 + 2 * i + 1, u0 // 2 + i, 1, k.xh, k.xl)
        n = 8 * j + i
        pe.wait_ge(sem["gw_landed"], 64 * n + 64)
        pe.wait_ge(sem["conv_done"], n + 1)
        pe.wait_ge(sem["ti_ready"], n)
        for g in range(2):
            pe.matmul(k.s[:, g, :], k.gw[:, g, :], k.cx[:, 0:SEQ], start=True, stop=True)
        for g in range(2):
            mm = pe.matmul(k.r[:, 0, g * NS:g * NS + NS], k.gw[:, g, :], k.cx[:, SEQ:T], start=True, stop=True)
        mm.then_inc(sem["gates_done"], 1)

    if j == 0:
        pe.wait_ge(sem["x_ready"], 1)
    else:
        tile(0, True)
    with pe.Fori(j, KT) as i:
        tile(i, False)
    multiply_last_made(pe, k, s0 + 16, u0 + 16, "a_rest", 8 * j + 8)
    for q in range(3):
        n = 3 if q < 2 else 2
        t = pe.transpose(k.x[0:n * AN, q * P:(q + 1) * P], k.tails[:, 3 * q:3 * q + n, :].rearrange("p i c -> p (i c)"), k.ident[:, :])
    t.then_inc(sem["tails_turned"], 1)
    out_tensor(pe, k, s0 + 16, u0 + 16)
    ln_tensor(pe, k, 3 * j)


def row_of_inputs(act, k, par, chain):
    bank = k.proj[:, par]
    act.activation(k.u[:, HIST:HIST + HALF], k.proj_lo[:, 0:HALF], ACT.Copy).then_inc(k.sem["s_evac"], 1)
    chain(act.activation(k.u[:, HIST + HALF:SROW], bank[:, 0:SEQ - HALF], ACT.Copy))
    act.activation(k.u_s[:, :, HIST:WIN], bank[:, SEQ - HALF:T - HALF].rearrange("p (b t) -> p b t", b=NB),
                   ACT.Copy).then_inc(k.sem[f"p_evac{par}"], 1)


def a_scalar(act, k, j, chain):
    s0, u0, sem = SLOT_A[j], USE_A[j], k.sem
    if j == 0:
        split_high(act, k, s0 + 1, s0 // 2, 1)
    with chain.loop("a", KT) as i:
        n = 8 * j + i
        await_slot(act, k, s0 + 2 * i)
        act.wait_ge(sem["conv_done"], n)
        row_of_inputs(act, k, 0, chain)
        split_high(act, k, s0 + 2 * i + 2, s0 // 2 + i + 1, 0)
        await_slot(act, k, s0 + 2 * i + 1)
        act.wait_ge(sem["s_evac"], u0 + 2 * i)
        chain(act.activation(k.tg[:, HALF:T], k.proj[:, 1, 0:T - HALF], ACT.Tanh, scale=0.5))
        act.activation(k.tg[:, 0:HALF], k.proj_lo[:, 0:HALF], ACT.Tanh, scale=0.5).then_inc(sem["tg_ready"], 1)
        split_high(act, k, s0 + 2 * i + 3, s0 // 2 + i + 1, 1)
        act.wait_ge(sem["gates_done"], n + 1)
        chain(act.activation(k.tr[:, 0:SEQ], k.s[:, 0, :], ACT.Tanh, scale=0.5, bias=k.cur[:, 40:41]))
        chain(act.activation(k.tr[:, SEQ:T], k.r[:, 0, 0:NS], ACT.Tanh, scale=0.5, bias=k.cur[:, 40:41]))
        act.wait_ge(sem["gi_ready"], n)
        chain(act.activation(k.ti[:, 0:SEQ], k.s[:, 1, :], ACT.Tanh, scale=0.5, bias=k.cur[:, 41:42]))
        act.activation(k.ti[:, SEQ:T], k.r[:, 0, NS:2 * NS], ACT.Tanh, scale=0.5,
                       bias=k.cur[:, 41:42]).then_inc(sem["ti_ready"], 1)
        chain(act.activation(k.a2[:], k.tr[:], ACT.Exp, scale=k.cur[:, 44:45], bias=k.cur[:, 44:45]))
        act.activation(k.t[:], k.tr[:], ACT.Tanh, scale=k.cur[:, 42:43], bias=k.cur[:, 42:43]).then_inc(sem["t_ready"], 1)
        act.wait_ge(sem["a_rest"], n)
        act.activation(k.a[:], k.tr[:], ACT.Exp, scale=k.cur[:, 43:44], bias=k.cur[:, 43:44]).then_inc(sem["al_ready"], 1)
        act.wait_ge(sem["q_in"], n + 1)
        act.activation(k.rt[:], k.q[:], ACT.Sqrt, scale=0.25).then_inc(sem["rt_ready"], 1)
    out_scalar(act, k, s0 + 16, chain, 3 * j == k.last, ahead=2)
    ln_scalar(act, k, 3 * j, chain)


def convolve(dve, k, chain, cur, out, done):
    acc = k.conv
    chain(dve.tensor_scalar(acc[:], k.u[:, 0:CW], cur[:, 0:1], cur[:, 4:5], ALU.mult, ALU.add))
    for tap in (1, 2):
        chain(dve.scalar_tensor_tensor(acc[:], k.u[:, tap:tap + CW], cur[:, tap:tap + 1], acc[:], ALU.mult, ALU.add))
    chain(dve.scalar_tensor_tensor(out[:, 0:SEQ], k.u[:, HIST:SROW], cur[:, 3:4], acc[:, 0:SEQ], ALU.mult, ALU.add))
    ends = k.conv_s
    dve.scalar_tensor_tensor(out[:, SEQ:T].rearrange("p (b t) -> p b t", b=NB), k.u_s[:, :, HIST:WIN], cur[:, 3:4],
                             ends[:, :, 0:DT], ALU.mult, ALU.add).then_inc(k.sem[done], 1)


def a_vector(dve, k, j, chain):
    s0, u0, sem = SLOT_A[j], USE_A[j], k.sem
    first = slice(SEQ, T, DT)

    def convolution(i):
        n = 8 * j + i
        dve.wait_ge(sem["al_ready"], n)
        chain(dve.tensor_scalar(k.cur[:, 0:40], k.par_a[j][:, bass.ds(i, 1), :].rearrange("p o c -> p (o c)"), 1.0, None, ALU.mult))
        chain(dve.tensor_scalar(k.cur[:, 40:45], k.par_d[j][:, :, bass.ds(i, 1)].rearrange("p c o -> p (c o)"), 1.0, None, ALU.mult))
        chain(dve.tensor_copy(k.u_s[:, :, 0:HIST], k.cur[:, 8:32].rearrange("p (b t) -> p b t", b=NB)))
        dve.wait_ge(sem["p_evac0"], u0 // 2 + i + 1)
        dve.wait_ge(sem["s_evac"], u0 + 2 * i + 1)
        dve.wait_ge(sem["gates_done"], n)
        tail = k.tails[:, bass.ds(i, 1), :].rearrange("p o c -> p (o c)")
        chain(dve.tensor_scalar(tail[:, 0:HIST], k.u[:, SEQ:SROW], 1.0, None, ALU.mult))
        chain(dve.tensor_scalar(tail[:, HIST:HN].rearrange("p (b t) -> p b t", b=NB), k.u_s[:, :, DT:WIN], 1.0, None, ALU.mult))
        convolve(dve, k, chain, k.cur, k.cx, "conv_done")

    def gates(i):
        n = 8 * j + i
        dve.wait_ge(sem["tg_ready"], n + 1)
        dve.scalar_tensor_tensor(k.sg[:, 0:HALF], k.tg[:, 0:HALF], 1.0, k.proj_lo[:, 0:HALF], ALU.add, ALU.mult).then_inc(sem["s_evac"], 1)
        dve.scalar_tensor_tensor(k.sg[:, HALF:T], k.tg[:, HALF:T], 1.0, k.proj[:, 1, 0:T - HALF], ALU.add, ALU.mult).then_inc(sem["p_evac1"], 1)
        dve.wait_ge(sem["t_ready"], n + 1)
        dve.scalar_tensor_tensor(k.q[:], k.a2[:], 1.0, k.t[:], ALU.add, ALU.mult).then_inc(sem["q_in"], 1)
        dve.wait_ge(sem["ti_ready"], n + 1)
        dve.wait_ge(sem["conv_done"], n + 1)
        dve.scalar_tensor_tensor(k.gi[:], k.ti[:], 1.0, k.cx[:], ALU.add, ALU.mult).then_inc(sem["gi_ready"], 1)
        dve.wait_ge(sem["al_ready"], n + 1)
        chain(dve.tensor_tensor(k.h0a[:], k.a[:, first], k.cur[:, 32:40], ALU.mult))

    def scan(i):
        n = 8 * j + i
        tail = k.tails[:, bass.ds(i, 1), :].rearrange("p o c -> p (o c)")
        dve.wait_ge(sem["rt_ready"], n + 1)
        dve.wait_ge(sem["gi_ready"], n + 1)
        chain(dve.tensor_tensor(k.gi[:], k.gi[:], k.rt[:], ALU.mult))
        chain(dve.tensor_tensor(k.gi[:, first], k.gi[:, first], k.h0a[:], ALU.add))
        chain(dve.memset(k.a[:, first], 0.0))
        chain(dve.tensor_tensor_scan(k.h[:], k.a[:], k.gi[:], 0.0, ALU.mult, ALU.add))
        chain(dve.tensor_scalar(tail[:, HN:HN + 1], k.h[:, SEQ - 1:SEQ], 1.0, None, ALU.mult))
        chain(dve.tensor_scalar(tail[:, HN + 1:AN], k.h[:, SEQ + DT - 1:T:DT], 1.0, None, ALU.mult))
        dve.wait_ge(sem["s_evac"], u0 + 2 * i + 2)
        dve.wait_ge(sem["p_evac1"], u0 // 2 + i + 1)
        chain(dve.scalar_tensor_tensor(k.h[:], k.h[:], 0.5, k.sg[:], ALU.mult, ALU.mult))
        high = k.gh[:, bass.ds(i, 1), :].rearrange("p o t -> p (o t)")
        low = k.gl[:, bass.ds(i, 1), :].rearrange("p o t -> p (o t)")
        chain(dve.tensor_scalar(high, k.h[:], 1.0, None, ALU.mult))
        dve.tensor_tensor(low, k.h[:], high, ALU.subtract).then_inc(sem["a_rest"], 1)
        dve.wait_ge(sem["a_rest"], n + 1)

    convolution(0)
    gates(0)
    with chain.loop("a", KT - 1) as i:
        convolution(i + 1)
        scan(i)
        gates(i + 1)
    scan(KT - 1)
    dve.wait_ge(sem["tails_turned"], 1 + j)
    if j:
        dve.wait_ge(sem["tails_out"], TAILS_OUT)
    dve.tensor_copy(k.tails_sb[0:3 * AN, 0:2 * P], k.x[0:3 * AN, 0:2 * P]).then_inc(sem["tails_read"], 1)
    dve.tensor_copy(k.tails_sb[0:2 * AN, 2 * P:3 * P], k.x[0:2 * AN, 2 * P:3 * P]).then_inc(sem["tails_read"], 1)
    out_vector(dve, k, s0 + 16, u0 + 16, chain, 3 * j)
    ln_vector(dve, k, 3 * j, chain)


def tails_stores(sp, k, o, j):
    sp.wait_ge(k.sem["tails_read"], 2 * j + 2)
    outputs = ((o["lru_conv_prompt"][j, 0], 0, HIST), (o["lru_conv_sample"][j].rearrange("b k d -> (b k) d"), HIST, NB * HIST),
               (o["lru_h_prompt"][j], HN, 1), (o["lru_h_sample"][j], HN + 1, NB))
    for r in range(3):
        for dst, at, rows in outputs:
            row = slice(r * AN + at, r * AN + at + rows)
            sp.dma_start(dst[:, 0:6 * P].rearrange("n (q r p) -> n q r p", q=2, r=3)[:, :, r, :],
                           k.tails_sb[row, 0:2 * P].rearrange("n (q p) -> n q p", q=2)).then_inc(k.sem["tails_out"], 16)
            if r < 2:
                sp.dma_start(dst[:, (6 + r) * P:(7 + r) * P], k.tails_sb[row, 2 * P:3 * P]).then_inc(k.sem["tails_out"], 16)



R_PAIR, S_PAIR, X_PAIR = 44, 18, 41


def r_turn(c):
    return c


def r_keys(n, q):
    return 4 + 5 * n + q


def r_weights(n):
    return 4 + 5 * n + 4


def s_prompt(n):
    return 2 * n


def s_sample(n):
    return 2 * n + 1


def s_rms(h):
    return 16 + h


def x_new(n):
    return 5 * n - 1 if n else 1


def x_prompt(n):
    return 5 * n + 1 if n else 2


def x_weights(n):
    return 5 * n + 3


def x_values(n):
    return 5 * n + 5 if n < 7 else 39


def x_sample(n):
    return 5 * n + 7 if n < 7 else 40


def await_fill(eng, k, bank, i, local):
    per = {"r": R_PAIR, "s": S_PAIR, "x": X_PAIR}[bank]
    eng.wait_ge(k.sem[f"{bank}_done"], per * i + local + 1)


def may_fill(pe, k, bank, i, local):
    if bank == "r":
        pe.wait_ge(k.sem[f"r_read{local % 2}"], R_PAIR // 2 * i + local // 2)
    else:
        pe.wait_ge(k.sem[f"{bank}_read"], {"s": S_PAIR, "x": X_PAIR}[bank] * i + local)


def layer_b_buffers(k):
    k.qz = [k.sb(f"q_split{h}", [P, 2, SEQ]) for h in range(2)]
    k.qs = [k.sb(f"q_sample{h}", [P, NB, 32]) for h in range(2)]
    k.kt = [k.sb(f"k_feat{h}", [P, T]) for h in range(2)]
    k.ot = [k.sb(f"o_feat{h}", [P, T]) for h in range(2)]
    k.stage = [[k.xT[:, 4 * h + n, :] for n in range(4)] for h in range(2)]
    k.sgb = [k.sq[h][:, 1, :] for h in range(2)]
    k.ktok = k.sb("k_tok", [P, CH, 2, P])
    k.vtok = k.sb("v_tok", [P, CH, 2, P])
    k.pp = k.sb("p_prompt", [P, 2, SEQ])
    k.tgb = k.rs
    k.wt = k.u[:, HIST:SROW].rearrange("p (g t) -> p g t", g=QB)
    k.kts = k.sb("past_k_feat", [P, 2, PAGES, P])
    k.pps = k.sb("p_sample", [64, PAGES * P])
    k.ppn = k.sb("p_new", [64, NS])
    k.ws = k.sb("w_sample", [P, PAGES + 1, 2, 32])
    k.vo = k.conv[:, 0:P]
    k.vsel = k.sb("v_select", [P, 8])
    k.kb = [k.sb(f"k_pages{h}", [P, 4, 2 * P]) for h in range(2)]
    k.vb = [k.sb(f"v_pages{n}", [P, PAGES, 2 * P]) for n in range(2)]
    k.pm, k.pl, k.st = k.sb("p_max", [P, 2]), k.sb("p_sum", [P, 2]), k.sb("s_stats", [64, 6])
    k.negq = k.conv[:, P:2 * P]
    k.qsel = k.sb("q_select", [NS, NB, 32])
    k.negs = k.sb("mask_s", [NS, NS])
    k.cp = k.sb("c_pattern", [64, 3, 8])
    k.cmat = k.sb("c_matrix", [64, 8])
    k.lam = k.sb("lam", [P, 4])
    k.blam = k.conv[:, 2 * P:2 * P + 4 * DH]
    k.subw = k.sb("subln", [P, 1])
    k.table = k.sb("table", [1, NB * PAGES], I32)


def b_cols(a, kind, h):
    return a["b_in_w"][0][:, (kind * HEADS + h) * P:(kind * HEADS + h + 1) * P]


def b_sync(sp, k, a, o, nxt):
    sem, s0 = k.sem, SLOT_B
    sp.wait_ge(sem["tails_out"], TAILS_OUT)
    sp.dma_start(k.table[:], a["page_table"].rearrange("(o b) n -> o (b n)", o=1)).then_inc(sem["table_in"], 16)
    sp.dma_start(k.blam[:], a["b_lambda"].rearrange("o a d -> o (a d)").broadcast_to([P, 4 * DH])).then_inc(sem["b_params"], 16)
    sp.dma_start(k.subw[:], a["b_subln_w"].rearrange("o d -> d o")).then_inc(sem["b_params"], 16)
    sp.wait_ge(sem["table_in"], 16)
    keys = a["cache_k"][0].rearrange("n t h c d -> n t (h c d)")
    values = a["cache_v"][0].rearrange("n t h d -> n t (h d)")

    def pages(n, col, places, cache, landed, free=None):
        page = [sp.value_load(k.table[0:1, n * PAGES + g:n * PAGES + g + 1], min_val=0, max_val=79) for g in range(PAGES)]
        if free:
            sp.wait_ge(sem[free[0]], free[1])
        for g in range(PAGES):
            sp.dma_start(places[g], cache[bass.ds(page[g], 1), :, bass.ds(col, 2 * P)]
                         .rearrange("o t c -> (o t) c")).then_inc(sem[landed[g]], 16)

    def key_pages(n, col, after=None):
        places = [k.kb[g // 4][:, g % 4, :] for g in range(PAGES)]
        pages(n, col, places, keys, [f"k_landed{g // 4}" for g in range(PAGES)],
              after and ("r_done", R_PAIR * after[0] + r_keys(after[1], 3) + 1))

    def value_pages(n, col, after=None):
        pages(n, col, [k.vb[n % 2][:, g, :] for g in range(PAGES)], values, [f"v_landed{n % 2}"] * PAGES,
              after and ("x_done", X_PAIR * after[0] + x_values(after[1]) + 1))

    kp = o["k_prompt"][0, 0].rearrange("(c p) h m d -> p c (h m d)", p=P)
    vp = o["v_prompt"][0, 0].rearrange("(c p) h d -> p c (h d)", p=P)
    ks = o["k_sample"][0].rearrange("b t h m d -> (b t) (h m d)")
    vs = o["v_sample"][0].rearrange("b t h d -> (b t) (h d)")

    def stores(col):
        for dst, dst_s, src in ((kp, ks, k.ktok), (vp, vs, k.vtok)):
            sp.dma_start(dst[:, :, bass.ds(col, 2 * P)], src[:, 0:QB].rearrange("p c h d -> p c (h d)")).then_inc(sem["kv_out"], 16)
            sp.dma_start(dst_s[:, bass.ds(col, 2 * P)], src[0:NS, QB].rearrange("p h d -> p (h d)")).then_inc(sem["kv_out"], 16)

    def stage(i, u, slots, units, final=False):
        fixed = final or not (slots and units)
        cols = [(i * 2 + n // 4) * P + n % 4 * D for n in range(8)] + [(i * 2 + 2) * P, (i * 2 + 2) * P + D]
        at, following = i * 2 * P - 2 * P, i * 2 * P
        if not fixed:
            cols = [sp.snap(c) for c in cols]
            at, following = sp.snap(at), sp.snap(following)
        if not units:
            key_pages(0, 0)
            for n in range(2):
                value_pages(n, 0)
        for n in range(8):
            if slots and final and n >= 6:
                load_slot(sp, k, s0 + 26 + n, n % 2, a["b_out_w"][0][:, (n - 6) * P:(n - 5) * P])
            elif slots:
                load_slot(sp, k, s0 + 8 * i + n + 2, n % 2, a["b_in_w"][0][:, bass.ds(cols[n + 2], P)])
            if units and n < 7:
                key_pages(n + 1, at, (u, n))
            elif units and slots:
                key_pages(0, following, (u, 7))
            if units and n == 1:
                stores(at)
            if units and n and (n < 7 or slots):
                value_pages((n + 1) % 8, at if n < 7 else following, (u, n - 1))
        if slots and units:
            value_pages(1, following, (u, 7))

    stage(0, -1, True, False)
    with sp.Fori(1, 3) as i:
        stage(i, i - 1, True, True)
    stage(3, 2, True, True, final=True)
    stage(4, 3, False, True)
    out_sync(sp, k, s0 + 32, a["b_out_w"][0], 1, 4)
    for h in range(2):
        if nxt:
            load_slot(sp, k, s0 + 40 + h, h, nxt[h])


def b_pool(pool, k, chain):
    sem = k.sem
    pool.wait_ge(sem["tails_out"], TAILS_OUT)
    for t in [*k.qz, *k.qs, k.negq, k.negs, k.cp, k.qsel, k.vsel]:
        chain(pool.memset(t[:], 0.0))
    chain(pool.affine_select(out=k.negq[:], in_=k.negq[:], compare_op=ALU.is_ge, fill=NEG,
                             base=0, pattern=[[-1, P]], channel_multiplier=1))
    chain(pool.affine_select(out=k.negs[:], in_=k.negs[:], compare_op=ALU.is_ge, fill=NEG,
                             base=0, pattern=[[-1, NS]], channel_multiplier=1))
    blocks = k.negs[:].rearrange("p (b t) -> p b t", b=NB)
    chain(pool.affine_select(out=blocks, in_=blocks, compare_op=ALU.is_ge, fill=NEG,
                             base=DT - 1, pattern=[[DT, NB], [0, DT]], channel_multiplier=-1))
    sel = k.qsel[:].rearrange("p b (c t) -> p b c t", t=DT)
    chain(pool.affine_select(out=sel, in_=sel, compare_op=ALU.not_equal, fill=1.0,
                             base=0, pattern=[[-DT, NB], [0, 8], [-1, DT]], channel_multiplier=1))
    for m in range(2):
        c = k.cp[:, m, :].rearrange("p (h t) -> p h t", h=2)
        chain(pool.affine_select(out=c, in_=c, compare_op=ALU.not_equal, fill=1.0,
                                 base=-DT * m, pattern=[[-32, 2], [-1, DT]], channel_multiplier=1))
    for half in range(2):
        c = k.vsel[:].rearrange("p (h t) -> p h t", h=2)
        chain(pool.affine_select(out=c, in_=c, compare_op=ALU.not_equal, fill=1.0,
                                 base=-64 * half, pattern=[[-32, 2], [-1, DT]], channel_multiplier=1))
    pool.memset(k.ws[:], 0.0).then_inc(sem["b_consts"], 1)
    low_parts(pool, k, SLOT_B + 1, 32)
    pool.wait_ge(sem["q_ready"], 4)
    pool.wait_ge(sem["gates_copied"], 4)
    pool.tensor_tensor(k.xT[:], k.xh[:], k.xl[:], ALU.add).then_inc(sem["x_back"], 1)
    low_parts(pool, k, SLOT_B + 33, 7 if k.last == 1 else 8)


def b_tensor(pe, k):
    sem, s0, u0 = k.sem, SLOT_B, USE_B
    pe.wait_ge(sem["b_consts"], 1)

    def prompt_scores(i, n):
        h, q = n // 4, n % 4
        may_fill(pe, k, "s", i, s_prompt(n))
        for m in range(2):
            mm = pe.matmul(k.s[:, m, 0:P * (q + 1)], k.qz[h][:, m, q * P:(q + 1) * P], k.kt[h][:, 0:P * (q + 1)],
                           start=True, stop=True)
        mm.then_inc(sem["s_done"], 1)

    def past_keys(i, n):
        for q in range(4):
            if q % 2 == 0:
                pe.wait_ge(sem[f"k_landed{q // 2}"], 64 * (8 * i + n) + 64)
            may_fill(pe, k, "r", i, r_keys(n, q))
            bank = r_keys(n, q) % 2
            for g in range(2):
                for h in range(2):
                    c = (2 * g + h) * P
                    t = pe.transpose(k.r[:, bank, c:c + P], k.kb[q // 2][:, 2 * (q % 2) + g, h * P:(h + 1) * P], k.ident[:])
            t.then_inc(sem["r_done"], 1)

    def sample_weights(i, n):
        pe.wait_ge(sem["c_ready"], 8 * i + n + 1)
        may_fill(pe, k, "x", i, x_weights(n))
        for g in range(PAGES):
            pe.matmul(k.x[:, 8 * g:8 * g + 8], k.pps[:, g * P:(g + 1) * P], k.cmat[:], start=True, stop=True)
        mm = pe.matmul(k.x[0:NS, 64:72], k.ppn[:], k.cmat[:], start=True, stop=True)
        mm.then_inc(sem["x_done"], 1)

    def sample_values(i, n):
        may_fill(pe, k, "x", i, x_values(n))
        pe.wait_ge(sem[f"v_landed{n % 2}"], 128 * (4 * i + n // 2) + 128)
        for g in range(4):
            for half in range(2):
                for h in range(2):
                    at = 64 * half + 32 * h
                    pe.matmul(k.x[at:at + 32, 0:P], k.ws[:, 4 * half + g, h, :], k.vb[n % 2][:, 4 * half + g, h * P:(h + 1) * P],
                              start=g == 0, stop=g == 3 and half == 1)
        for h in range(2):
            mm = pe.matmul(k.x[32 * h:32 * h + 32, 0:P], k.ws[0:NS, PAGES, h, :], k.vtok[0:NS, QB, h, :], start=False, stop=True)
        mm.then_inc(sem["x_done"], 1)

    def sample_output(i, n):
        pe.wait_ge(sem["o_copied"], 8 * i + n + 1)
        may_fill(pe, k, "x", i, x_sample(n))
        pe.matmul(k.x[:, 0:8], k.vo[:], k.vsel[:], start=True, stop=True).then_inc(sem["x_done"], 1)

    def sample_scores(i, n):
        may_fill(pe, k, "s", i, s_sample(n))
        for q in range(2):
            last = r_keys(n, 2 + q)
            pe.wait_ge(sem[f"r_read{last % 2}"], R_PAIR // 2 * i + last // 2 + 1)
        for half in range(2):
            for h in range(2):
                mm = pe.matmul(k.s[32 * h:32 * h + 32, half, :], k.qs[h][:, n, :],
                               k.kts[:, h, 4 * half:4 * half + 4, :], start=True, stop=True)
        mm.then_inc(sem["s_done"], 1)
        may_fill(pe, k, "x", i, x_new(n))
        for h in range(2):
            out = k.x[32 * h:32 * h + 32, 0:NS]
            pe.matmul(out, k.qs[h][:, n, :], k.kt[h][:, SEQ:T], start=True, stop=False)
            mm = pe.matmul(out, k.qsel[:, n, :], k.negs[:], start=False, stop=True)
        mm.then_inc(sem["x_done"], 1)

    def prompt_weights(i, n):
        q = n % 4
        pe.wait_ge(sem["w_ready"], 8 * i + n + 1)
        f = r_weights(n)
        may_fill(pe, k, "r", i, f)
        for g in range(q + 1):
            t = pe.transpose(k.r[:, f % 2, g * P:(g + 1) * P], k.pp[:, 0, g * P:(g + 1) * P], k.ident[:])
        t.then_inc(sem["r_done"], 1)

    def prompt_output(i, n):
        h, q, f = n // 4, n % 4, r_weights(n)
        pe.wait_ge(sem[f"r_read{f % 2}"], R_PAIR // 2 * i + f // 2 + 1)
        may_fill(pe, k, "x", i, x_prompt(n))
        for g in range(q + 1):
            mm = pe.matmul(k.x[:, 0:P], k.vtok[:, g, h, :], k.wt[:, g, :], start=g == 0, stop=g == q)
        mm.then_inc(sem["x_done"], 1)

    def stage(i, u, slots, units):
        if units:
            pe.wait_ge(sem["q_ready"], u + 1)
            pe.wait_ge(sem["tok_ready"], u + 1)
        for n in range(9):
            if units and n < 8:
                past_keys(u, n)
                prompt_scores(u, n)
            if slots and n == 0 and not units:
                multiply_new_x(pe, k, s0, u0, 1)
            elif slots and n < 8:
                multiply_slot(pe, k, s0 + 8 * i + n, n % 2, u0 + 8 * i + n, u0 // 2 + 4 * i + n // 2, n % 2, k.xh, k.xl)
            if units:
                if n:
                    sample_weights(u, n - 1)
                if n < 8:
                    prompt_weights(u, n)
                    sample_scores(u, n)
                if n:
                    sample_values(u, n - 1)
                if n < 8:
                    prompt_output(u, n)
                if n:
                    sample_output(u, n - 1)
        if slots:
            pe.wait_ge(sem["p_evac0"], u0 // 2 + 4 * i + 4)
            pe.wait_ge(sem["p_evac1"], u0 // 2 + 4 * i + 4)
            pe.wait_ge(sem["s_evac"], u0 + 8 * i + 8)
            may_fill(pe, k, "x", i, 0)
            for c in range(4):
                src = k.stage[c // 2][1 + c % 2]
                may_fill(pe, k, "r", i, r_turn(c))
                for g in range(QB):
                    t = pe.transpose(k.r[:, c % 2, g * P:(g + 1) * P], src[:, g * P:(g + 1) * P], k.ident[:])
                t.then_inc(sem["r_done"], 1)
                t = pe.transpose(k.x[0:NS, c * P:(c + 1) * P], src[:, SEQ:T], k.ident[:])
            t.then_inc(sem["x_done"], 1)
        for h in range(2):
            if units:
                pe.wait_ge(sem["o_squared"], 2 * u + h + 1)
                may_fill(pe, k, "s", u, s_rms(h))
                pe.matmul(k.s[:, 0, :], k.ones_d[:], k.sq[h][:, 0, 0:SEQ], start=True, stop=True)
                mm = pe.matmul(k.s[:, 1, 0:NS], k.ones_d[:], k.sq[h][:, 0, SEQ:T], start=True, stop=True)
                mm.then_inc(sem["s_done"], 1)

    stage(0, -1, True, False)
    with pe.Fori(0, 3) as j:
        stage(j + 1, j, True, True)
    stage(4, 3, False, True)
    multiply_last_made(pe, k, s0 + 32, u0 + 32, "b_head", 8)
    out_tensor(pe, k, s0 + 32, u0 + 32)
    ln_tensor(pe, k, 1)


def b_scalar(act, k, chain):
    sem, s0, u0 = k.sem, SLOT_B, USE_B
    act.wait_ge(sem["b_consts"], 1)
    act.wait_ge(sem["lam_in"], 1)
    act.activation(k.lam[:, 0:2], k.lam[:, 0:2], ACT.Exp).then_inc(sem["lam_exp"], 1)

    def keys_copy(u, n, q):
        f = r_keys(n, q)
        if n:
            act.wait_ge(sem["s_done"], S_PAIR * u + s_sample(n - 1) + 1)
        await_fill(act, k, "r", u, f)
        act.activation(k.kts[:, :, 2 * q:2 * q + 2, :].rearrange("p h g c -> p g h c"),
                       k.r[:, f % 2, :].rearrange("p (g h c) -> p g h c", g=2, h=2), ACT.Copy).then_inc(sem[f"r_read{f % 2}"], 1)

    def before_slot(u, n):
        q = n % 4
        keys_copy(u, n, 0)
        keys_copy(u, n, 2)
        act.wait_ge(sem["pm_ready"], 8 * u + n + 1)
        for m in range(2):
            step = act.activation(k.pp[:, m, 0:P * (q + 1)], k.s[:, m, 0:P * (q + 1)], ACT.Exp,
                                  bias=k.pm[:, m:m + 1], accum_out=k.pl[:, m:m + 1])
            chain(step) if m == 0 else step.then_inc(sem["s_read"], 1)

    def slot(i, n, units):
        h, kind = n // 4, n % 4
        if units or n:
            split_high(act, k, s0 + 8 * i + n + 1, s0 // 2 + 4 * i + (n + 1) // 2, (n + 1) % 2)
        if kind == 1:
            return
        await_slot(act, k, s0 + 8 * i + n)
        if kind in (0, 2):
            to = k.stage[h][kind]
            if units and kind == 2 and h == 0:
                act.wait_ge(sem["x_done"], X_PAIR * i - X_PAIR + 1)
            act.activation(to[:, HALF:T], k.proj[:, 0, 0:T - HALF], ACT.Copy).then_inc(sem["p_evac0"], 1)
            act.activation(to[:, 0:HALF], k.proj_lo[:, 0:HALF], ACT.Copy).then_inc(sem["s_evac"], 1)
        else:
            if h:
                act.wait_ge(sem["s_evac"], u0 + 8 * i + 4)
            elif units:
                act.wait_ge(sem["b_head"], 2 * i - 2)
            chain(act.activation(k.tgb[:, HALF:T], k.proj[:, 1, 0:T - HALF], ACT.Tanh, scale=0.5))
            act.activation(k.tgb[:, 0:HALF], k.proj_lo[:, 0:HALF], ACT.Tanh, scale=0.5).then_inc(sem["tgb_ready"], 1)

    def after_slot(u, n):
        q, f = n % 4, r_weights(n)
        if n:
            act.wait_ge(sem["x_done"], X_PAIR * u + x_prompt(n - 1) + 1)
        await_fill(act, k, "r", u, f)
        act.activation(k.wt[:, 0:q + 1, :], k.r[:, f % 2, 0:P * (q + 1)].rearrange("p (g c) -> p g c", c=P),
                       ACT.Copy).then_inc(sem[f"r_read{f % 2}"], 1)
        if n:
            act.wait_ge(sem["x_done"], X_PAIR * u + x_weights(n - 1) + 1)
        act.wait_ge(sem["sm_ready"], 8 * u + n + 1)
        chain(act.activation(k.ppn[:], k.ppn[:], ACT.Exp, bias=k.st[:, 2:3], accum_out=k.st[:, 4:5]))
        act.activation(k.pps[:], k.s[0:64, :, :].rearrange("p b c -> p (b c)"), ACT.Exp, bias=k.st[:, 2:3],
                       accum_out=k.st[:, 3:4]).then_inc(sem["s_read"], 1)

    def stage(i, u, slots, units):
        for n in range(8):
            if units:
                before_slot(u, n)
            if slots:
                slot(i, n, units)
            if units:
                after_slot(u, n)
        if units:
            act.wait_ge(sem["x_read"], X_PAIR * u + X_PAIR)
        for h in range(2):
            if units:
                act.activation(k.sq[h][:, 0, :], k.ot[h][:], ACT.Square).then_inc(sem["o_squared"], 1)
        if slots:
            act.wait_ge(sem["p_evac0"], u0 // 2 + 4 * i + 4)
            act.wait_ge(sem["p_evac1"], u0 // 2 + 4 * i + 4)
            act.wait_ge(sem["s_evac"], u0 + 8 * i + 8)
            for h in range(2):
                for m in range(2):
                    lo, src = slice(64 * m, 64 * m + 64), k.stage[h][0]
                    chain(act.activation(k.qz[h][lo, m, :], src[lo, 0:SEQ], ACT.Copy, scale=DH ** -0.5))
                    chain(act.activation(k.qs[h][lo, :, 4 * m:4 * m + 4], src[lo, SEQ:T].rearrange("p (b t) -> p b t", b=NB),
                                         ACT.Copy, scale=DH ** -0.5))
                step = act.activation(k.kt[h][:], k.stage[h][1][:], ACT.Copy)
                chain(step) if h == 0 else step.then_inc(sem["q_ready"], 1)
        for h in range(2):
            if units:
                await_fill(act, k, "s", u, s_rms(h))
                if h:
                    act.wait_ge(sem["b_head"], 2 * u + 1)
                chain(act.activation(k.rs[:, 0:SEQ], k.s[:, 0, :], ACT.Sqrt, bias=k.eps[:], scale=float(D // P)))
                act.activation(k.rs[:, SEQ:T], k.s[:, 1, 0:NS], ACT.Sqrt, bias=k.eps[:], scale=float(D // P)).then_inc(sem["s_read"], 1)

    stage(0, -1, True, False)
    with chain.loop("b", 3) as j:
        stage(j + 1, j, True, True)
    stage(4, 3, False, True)
    out_scalar(act, k, s0 + 32, chain, 1 == k.last)
    ln_scalar(act, k, 1, chain)


def b_vector(dve, k, chain):
    sem, s0, u0 = k.sem, SLOT_B, USE_B
    dve.wait_ge(sem["b_consts"], 1)
    dve.wait_ge(sem["b_params"], 32)
    lam = k.blam[:].rearrange("p (a c d) -> p a c d", a=2, c=2)
    chain(dve.tensor_tensor(lam[:, :, 0, :], lam[:, :, 0, :], lam[:, :, 1, :], ALU.mult))
    dve.tensor_reduce(k.lam[:, 0:2], lam[:, :, 0, :], AX.X, ALU.add).then_inc(sem["lam_in"], 1)
    dve.wait_ge(sem["lam_exp"], 1)
    chain(dve.tensor_tensor(k.lam[:, 2:3], k.lam[:, 1:2], k.lam[:, 0:1], ALU.subtract))
    chain(dve.tensor_scalar(k.lam[:, 3:4], k.lam[:, 2:3], LAM_INIT, None, ALU.subtract))
    chain(dve.tensor_scalar(k.cp[:, 1, :], k.cp[:, 1, :], k.lam[0:64, 3:4], None, ALU.mult))
    chain(dve.tensor_tensor(k.cp[:, 2, :], k.cp[:, 0, :], k.cp[:, 1, :], ALU.add))
    chain(dve.tensor_scalar(k.subw[:], k.subw[:], 0.5 * (1.0 - LAM_INIT), None, ALU.mult))

    def keys_copy(u, n, q):
        f = r_keys(n, q)
        await_fill(dve, k, "r", u, f)
        if n:
            dve.wait_ge(sem["s_done"], S_PAIR * u + s_sample(n - 1) + 1)
        dve.tensor_copy(k.kts[:, :, 2 * q:2 * q + 2, :].rearrange("p h g c -> p g h c"),
                        k.r[:, f % 2, :].rearrange("p (g h c) -> p g h c", g=2, h=2)).then_inc(sem[f"r_read{f % 2}"], 1)

    def factors(u, n):
        dve.wait_ge(sem["s_read"], S_PAIR * u + s_sample(n) + 1)
        chain(dve.tensor_tensor(k.st[:, 5:6], k.st[:, 3:4], k.st[:, 4:5], ALU.add))
        chain(dve.reciprocal(k.st[:, 5:6], k.st[:, 5:6]))
        dve.tensor_scalar(k.cmat[:], k.cp[:, 2, :], k.st[:, 5:6], None, ALU.mult).then_inc(sem["c_ready"], 1)

    def maxima(u, n):
        q = n % 4
        await_fill(dve, k, "s", u, s_prompt(n))
        diagonal = k.s[:, :, q * P:(q + 1) * P]
        chain(dve.tensor_tensor(diagonal, diagonal, k.negq[:].unsqueeze(1).broadcast_to([P, 2, P]), ALU.add))
        chain(dve.tensor_reduce(k.pm[:], k.s[:, :, 0:P * (q + 1)], AX.X, ALU.max))
        dve.tensor_scalar(k.pm[:], k.pm[:], -1.0, None, ALU.mult).then_inc(sem["pm_ready"], 1)

    def slot(i, n, units):
        h, kind = n // 4, n % 4
        if kind == 1:
            if units and h == 0:
                dve.wait_ge(sem["q_ready"], i)
            await_slot(dve, k, s0 + 8 * i + n)
            dve.tensor_copy(k.stage[h][1][:, HALF:T], k.proj[:, 1, 0:T - HALF]).then_inc(sem["p_evac1"], 1)
            dve.tensor_copy(k.stage[h][1][:, 0:HALF], k.proj_lo[:, 0:HALF]).then_inc(sem["s_evac"], 1)
        if kind == 3:
            dve.wait_ge(sem["tgb_ready"], 2 * i + h + 1)
            to = k.stage[h][3]
            dve.scalar_tensor_tensor(to[:, HALF:T], k.tgb[:, HALF:T], 1.0, k.proj[:, 1, 0:T - HALF], ALU.add, ALU.mult).then_inc(sem["p_evac1"], 1)
            dve.scalar_tensor_tensor(to[:, 0:HALF], k.tgb[:, 0:HALF], 1.0, k.proj_lo[:, 0:HALF], ALU.add, ALU.mult).then_inc(sem["s_evac"], 1)

    def weights(u, n):
        q = n % 4
        dve.wait_ge(sem["s_read"], S_PAIR * u + s_prompt(n) + 1)
        chain(dve.reciprocal(k.pl[:], k.pl[:]))
        chain(dve.tensor_scalar(k.pl[:, 1:2], k.pl[:, 1:2], k.lam[:, 3:4], None, ALU.mult))
        w0, w1 = k.pp[:, 0, 0:P * (q + 1)], k.pp[:, 1, 0:P * (q + 1)]
        chain(dve.tensor_scalar(w0, w0, k.pl[:, 0:1], None, ALU.mult))
        dve.scalar_tensor_tensor(w0, w1, k.pl[:, 1:2], w0, ALU.mult, ALU.add).then_inc(sem["w_ready"], 1)

    def sample_weights(u, n):
        await_fill(dve, k, "x", u, x_weights(n))
        chain(dve.tensor_copy(k.ws[:, 0:PAGES, :, 0:DT], k.x[:, 0:64].rearrange("p (g h t) -> p g h t", g=PAGES, h=2)))
        dve.tensor_copy(k.ws[0:NS, PAGES, :, 0:DT], k.x[0:NS, 64:72].rearrange("p (h t) -> p h t", h=2)).then_inc(sem["x_read"], 1)

    def sample_values(u, n):
        await_fill(dve, k, "x", u, x_values(n))
        dve.tensor_copy(k.vo[:], k.x[:, 0:P]).then_inc(sem["x_read"], 1)
        dve.wait_ge(sem["x_read"], X_PAIR * u + x_values(n) + 1)
        dve.sem_inc(sem["o_copied"], 1)

    def sample_maxima(u, n):
        await_fill(dve, k, "x", u, x_new(n))
        dve.tensor_copy(k.ppn[:], k.x[0:64, 0:NS]).then_inc(sem["x_read"], 1)
        chain(dve.tensor_reduce(k.st[:, 0:1], k.s[0:64, :, :], AX.XY, ALU.max))
        dve.wait_ge(sem["x_read"], X_PAIR * u + x_new(n) + 1)
        chain(dve.tensor_reduce(k.st[:, 1:2], k.ppn[:], AX.X, ALU.max))
        chain(dve.tensor_tensor(k.st[:, 2:3], k.st[:, 0:1], k.st[:, 1:2], ALU.max))
        dve.tensor_scalar(k.st[:, 2:3], k.st[:, 2:3], -1.0, None, ALU.mult).then_inc(sem["sm_ready"], 1)

    def sample_output(u, n):
        await_fill(dve, k, "x", u, x_sample(n))
        at = SEQ + DT * n
        chain(dve.tensor_copy(k.ot[0][:, at:at + DT], k.x[:, 0:DT]))
        dve.tensor_copy(k.ot[1][:, at:at + DT], k.x[:, DT:2 * DT]).then_inc(sem["x_read"], 1)

    def tokens(i):
        dve.wait_ge(sem["kv_out"], 64 * i)
        for c in range(4):
            await_fill(dve, k, "r", i, r_turn(c))
            dve.tensor_copy((k.ktok, k.vtok)[c % 2][:, 0:QB, c // 2, :],
                            k.r[:, c % 2, :].rearrange("p (g d) -> p g d", g=QB)).then_inc(sem[f"r_read{c % 2}"], 1)
        await_fill(dve, k, "x", i, 0)
        new = k.x[0:NS, :].rearrange("p (h c d) -> p h c d", h=2, c=2)
        chain(dve.tensor_copy(k.ktok[0:NS, QB], new[:, :, 0, :]))
        dve.tensor_copy(k.vtok[0:NS, QB], new[:, :, 1, :]).then_inc(sem["x_read"], 1)
        dve.wait_ge(sem["x_read"], X_PAIR * i + 1)
        for b in range(2):
            dve.wait_ge(sem[f"r_read{b}"], R_PAIR // 2 * i + 2)
        dve.sem_inc(sem["tok_ready"], 1)

    def normalise(u, h):
        dve.wait_ge(sem["s_read"], S_PAIR * u + s_rms(h) + 1)
        chain(dve.reciprocal(k.rs[:], k.rs[:]))
        chain(dve.scalar_tensor_tensor(k.ot[h][:], k.ot[h][:], k.subw[:], k.rs[:], ALU.mult, ALU.mult))
        chain(dve.tensor_tensor(k.ot[h][:], k.ot[h][:], k.sgb[h][:], ALU.mult))
        high = k.gh[:, bass.ds(2 * u + h, 1), :].rearrange("p o t -> p (o t)")
        low = k.gl[:, bass.ds(2 * u + h, 1), :].rearrange("p o t -> p (o t)")
        chain(dve.tensor_scalar(high, k.ot[h][:], 1.0, None, ALU.mult))
        dve.tensor_tensor(low, k.ot[h][:], high, ALU.subtract).then_inc(sem["b_head"], 1)
        dve.wait_ge(sem["b_head"], 2 * u + h + 1)

    def stage(i, u, slots, units):
        for n in range(9):
            if units and n:
                factors(u, n - 1)
            if units and n < 8:
                keys_copy(u, n, 1)
                keys_copy(u, n, 3)
                maxima(u, n)
            if units and n < 8:
                weights(u, n)
            if slots and n < 8:
                slot(i, n, units)
            if units and n:
                sample_weights(u, n - 1)
            if units and n < 8:
                await_fill(dve, k, "s", u, s_sample(n))
                sample_maxima(u, n)
            if units and n:
                sample_values(u, n - 1)
            if units and n < 8:
                await_fill(dve, k, "x", u, x_prompt(n))
                q = n % 4
                dve.tensor_copy(k.ot[n // 4][:, q * P:(q + 1) * P], k.x[:, 0:P]).then_inc(sem["x_read"], 1)
            if units and n:
                sample_output(u, n - 1)
        if slots:
            tokens(i)
        if units:
            dve.wait_ge(sem["x_read"], X_PAIR * u + X_PAIR)
        for h in range(2):
            if units:
                normalise(u, h)
            if slots:
                if not units:
                    dve.wait_ge(sem["s_evac"], u0 + 8 * i + 8)
                    dve.wait_ge(sem["p_evac1"], u0 // 2 + 4 * i + 4)
                copy = dve.tensor_copy(k.sgb[h][:], k.stage[h][3][:])
                chain(copy) if h == 0 else copy.then_inc(sem["gates_copied"], 1)

    stage(0, -1, True, False)
    with chain.loop("b", 3) as j:
        stage(j + 1, j, True, True)
    stage(4, 3, False, True)
    dve.wait_ge(sem["x_back"], 1)
    out_vector(dve, k, s0 + 32, u0 + 32, chain, 1)
    ln_vector(dve, k, 1, chain)



CS_TURN, CR_TURN, CX_TURN = 12, 14, 5


def cs_tok(n):
    return n


def cs_sums(c):
    return 3 + c


def cs_state(n):
    return 8 + n


CR_TOK = 0


def cr_scores(c):
    return 1 + 2 * c


def cr_update(c):
    return 2 + 2 * c


def cr_state(n):
    return 10 + n


def c_filled(eng, k, bank, g, local):
    per = {"s": CS_TURN, "r": CR_TURN, "x": CX_TURN}[bank]
    eng.wait_ge(k.sem[f"c{bank}_done"], per * g + local + 1)


def c_read(k, bank, local):
    return k.sem["cx_read" if bank == "x" else f"c{bank}_read{local % 2}"]


def c_was_read(eng, k, bank, g, local):
    per = {"s": CS_TURN, "r": CR_TURN, "x": CX_TURN}[bank]
    if bank == "x":
        eng.wait_ge(k.sem["cx_read"], per * g + local + 1)
    else:
        eng.wait_ge(k.sem[f"c{bank}_read{local % 2}"], per // 2 * g + local // 2 + 1)


def c_may_fill(pe, k, bank, g, local):
    per = {"s": CS_TURN, "r": CR_TURN, "x": CX_TURN}[bank]
    if bank == "x":
        pe.wait_ge(k.sem["cx_read"], per * g + local)
    else:
        pe.wait_ge(k.sem[f"c{bank}_read{local % 2}"], per // 2 * g + local // 2)


def layer_c_buffers(k):
    k.st0 = k.sb("st0", [P, 2, NB, STATE])
    k.btok, k.xtok = k.sb("b_tok", [P, CH, STATE]), k.sb("x_tok", [P, CH, 2 * P])
    k.dt, k.adt, k.cs, k.dec = (k.sb(n, [P, CH, SSDH]) for n in ("dt", "adt", "cs", "dec"))
    k.dt_g, k.adt_g, k.cs_g, k.dec_g = (k.sb(n, [P, CH, HPG]) for n in ("dt_g", "adt_g", "cs_g", "dec_g"))
    k.wdt = k.sb("w_dt", [P, KT, SSDH])
    k.rowp = k.sb("row_params", [P, 3, SSDH])
    k.dsk = k.sb("d_skip", [P, CT])
    k.curc = k.sb("curc", [P, 4, 29])
    k.nw = k.sb("norm_w", [P, CT])
    k.feat = [k.sb(n, [P, T]) for n in ("b_feat", "c_feat", "x_feat0", "x_feat1")]
    k.cc, k.th = k.sb("cc", [P, T]), k.sb("th", [P, T])
    k.sz = [k.sb(f"sz{j}", [P, T]) for j in range(2)]
    k.xdt, k.xdd = k.sb("xdt", [P, 2 * P]), k.sb("xdd", [P, 2 * P])
    k.dm, k.e, k.m = (k.sb(n, [P, HPG, P]) for n in ("dm", "e", "m"))
    k.edec = k.sb("edec", [P, HPG])
    k.decp = k.sb("decp", [P, 2, NB])
    k.ht = k.sb("h_feat", [P, 2 * P])
    k.featn = [k.sb(n, [P, T]) for n in ("b_next", "c_next", "x_next0", "x_next1")]
    k.szn = [k.sb(f"sz_next{j}", [P, T]) for j in range(2)]
    k.hout = k.sb("h_out", [P, 2, P])
    k.hts = [k.sb(f"h_sample{j}", [P, 4, P]) for j in range(2)]
    k.bm = k.sq[0].rearrange("p a t -> p (a t)")[0:NS, 0:NB * STATE].rearrange("p (b n) -> p b n", b=NB)
    k.acc = k.sb("acc", [P, T])
    k.negc = k.sb("mask_c", [P, P])
    k.negcs = k.sb("mask_cs", [NS, NS])
    k.tris = k.sb("tri_s", [NS, NS])
    k.blk = k.sb("block_s", [NS, NS])
    k.ctails = k.sb("c_tails", [P, CONV_C // P, HN])


def c_cols(g, n):
    return [INNER * 2 + P * g, INNER * 2 + GROUPS * STATE + P * g, INNER + 2 * P * g, INNER + 2 * P * g + P,
            2 * P * g, 2 * P * g + P][n]


def c_sync(sp, k, a, o, nxt):
    sem, s0, w = k.sem, SLOT_C, a["c_in_w"][0]
    sp.wait_ge(sem["x_ready"], 3)
    sp.wait_ge(sem["kv_out"], 256)
    sp.dma_start(k.wdt[:], w[:, INNER + CONV_C:].rearrange("(k p) n -> p k n", p=P)).then_inc(sem["c_params"], 16)
    for n, v in enumerate((a["c_dt_bias"], a["c_a_log"], a["c_d"])):
        sp.dma_start(k.rowp[:, n, :], v.broadcast_to([P, SSDH])).then_inc(sem["c_params"], 16)
    states = a["state_ssd_h"][0].rearrange("b (q j h) p n -> q j (h p) b n", j=2, h=2)

    def stage(i, u, slots, units, final=False):
        fixed = final or not (slots and units)
        cols = [c_cols(i, n) for n in range(2, 6)] + [c_cols(i + 1, n) for n in range(2)]
        if not fixed:
            cols = [sp.snap(c_cols(u, n % 6) + (1 + n // 6) * (c_cols(1, n % 6) - c_cols(0, n % 6))) for n in range(2, 8)]
        for n in range(6):
            if slots and not (final and n >= 4):
                load_slot(sp, k, s0 + 6 * i + n + 2, n % 2, w[:, bass.ds(cols[n], P)])
            elif slots:
                load_slot(sp, k, s0 + 44 + n, n % 2, ow[(n - 4) * D:(n - 3) * D, 0:P])
            if units and n == 2:
                sp.wait_ge(sem["st_out"], 32 * u)
                for j in range(2):
                    sp.dma_start(k.st0[:, j], states[bass.ds(u, 1), j].rearrange("o p b n -> (o p) b n")).then_inc(sem["st_landed"], 16)
        if units:
            stores(u)

    hp = o["ssd_h_prompt"][0, 0].rearrange("(g j h) p n -> g (h p) j n", j=2, h=2)
    hs = o["ssd_h_sample"][0].rearrange("b (q j h) p n -> q j (h p) b n", j=2, h=2)

    def stores(u):
        sp.wait_ge(sem["hout_ready"], u + 1)
        sp.dma_start(hp[bass.ds(u, 1)].rearrange("o p j n -> (o p) j n"), k.hout[:]).then_inc(sem["hp_out"], 16)
        sp.wait_ge(sem["st_ready"], u + 1)
        for j in range(2):
            sp.dma_start(hs[bass.ds(u, 1), j].rearrange("o p b n -> (o p) b n"), k.st0[:, j]).then_inc(sem["st_out"], 16)

    ow = a["c_out_w"][0]
    stage(0, -1, True, False)
    with sp.Fori(0, GROUPS - 2) as j:
        stage(j + 1, j, True, True)
    stage(GROUPS - 1, GROUPS - 2, True, True, final=True)
    stage(GROUPS, GROUPS - 1, False, True)

    def out_slots(lo, hi):
        with sp.Fori(lo, hi) as m:
            col = sp.snap(m * P)
            for n in range(2):
                load_slot(sp, k, SLOT_C + 48 + 2 * m + n, n, ow[n * D:(n + 1) * D, bass.ds(col, P)])

    out_slots(1, 3)
    sp.wait_ge(sem["ctails_read"], 1)
    cp = o["ssd_conv_prompt"][0, 0].rearrange("n (u r p) -> n u r p", r=4, p=P)
    cs = o["ssd_conv_sample"][0].rearrange("b n (u r p) -> (b n) u r p", r=4, p=P)
    for r in range(4):
        src = k.rows[1][HN * r:HN * r + HN, :].rearrange("n (u p) -> n u p", p=P)
        sp.dma_start(cp[:, :, r, :], src[0:HIST]).then_inc(sem["ctails_out"], 16)
        sp.dma_start(cs[:, :, r, :], src[HIST:HN]).then_inc(sem["ctails_out"], 16)
    out_slots(3, KT)
    for h in range(2):
        if nxt:
            load_slot(sp, k, SLOT_C + 64 + h, h, nxt[h])


def c_pool(pool, k, chain):
    sem = k.sem
    pool.wait_ge(sem["b_head"], HEADS)
    pool.wait_ge(sem["kv_out"], 256)
    for t, v in ((k.negc, 0.0), (k.negcs, 0.0), (k.tris, 1.0), (k.blk, 1.0), (k.acc, 0.0), (k.dt, 0.0), (k.cs, 0.0), (k.dec, 0.0)):
        chain(pool.memset(t[:], v))
    chain(pool.affine_select(out=k.negc[:], in_=k.negc[:], compare_op=ALU.is_ge, fill=NEG,
                             base=0, pattern=[[1, P]], channel_multiplier=-1))
    for t, fill, causal in ((k.negcs, NEG, True), (k.tris, 0.0, True), (k.blk, 0.0, False)):
        v = t[:].rearrange("p (b t) -> p b t", b=NB)
        chain(pool.affine_select(out=v, in_=v, compare_op=ALU.is_ge, fill=fill, base=0,
                                 pattern=[[-DT, NB], [0, DT]], channel_multiplier=1))
        if causal:
            chain(pool.affine_select(out=t[:], in_=t[:], compare_op=ALU.is_ge, fill=fill, base=0,
                                     pattern=[[1, NS]], channel_multiplier=-1))
        else:
            chain(pool.affine_select(out=v, in_=v, compare_op=ALU.is_ge, fill=fill, base=DT - 1,
                                     pattern=[[DT, NB], [0, DT]], channel_multiplier=-1))
    pool.memset(k.edec[:], 0.0).then_inc(sem["c_consts"], 1)
    low_parts(pool, k, SLOT_C + 1, 6)

    def squares(u):
        for j in range(2):
            pool.wait_ge(sem["g_squared"], 2 * u + j + 1)
            pool.tensor_tensor(k.acc[:], k.acc[:], k.sq[1][:, j, :], ALU.add).then_inc(sem["acc_added"], 1)
            pool.wait_ge(sem["acc_added"], 2 * u + j + 1)

    with pool.Fori(0, GROUPS - 1) as u:
        for n in range(6):
            split_low(pool, k, SLOT_C + 7 + 6 * u + n, (n + 1) % 2)
        squares(u)
    squares(GROUPS - 1)
    low_parts(pool, k, SLOT_C + 49, 15 if k.last == 2 else 16)


def c_tensor(pe, k):
    sem, s0, u0 = k.sem, SLOT_C, USE_C
    pe.wait_ge(sem["c_consts"], 1)

    def time_steps():
        pe.wait_ge(sem["c_params"], 64)
        for c in range(CH):
            n = P if c < QB else NS
            for i in range(KT):
                mm = pe.matmul(k.x[0:n, c * SSDH:(c + 1) * SSDH], k.xT[:, i, c * P:c * P + n], k.wdt[:, i, :],
                               start=i == 0, stop=i == KT - 1)
        mm.then_inc(sem["dt_raw"], 1)

    def totals():
        pe.wait_ge(sem["adt_ready"], 1)
        prompt, sample = k.adt[:, 0:QB, :], k.adt[0:NS, QB, :]
        pe.matmul(k.s[:, 0, 0:P], k.tri[:], prompt, start=True, stop=True)
        pe.matmul(k.s[0:NS, 0, P:P + SSDH], k.tris[:], sample, start=True, stop=True)
        pe.matmul(k.s[:, 1, 0:P], k.ones_d[:], prompt, start=True, stop=True)
        pe.matmul(k.s[0:NS, 1, P:P + SSDH], k.blk[:], sample, start=True, stop=True).then_inc(sem["sums_done"], 1)
        pe.wait_ge(sem["dt_made"], 1)

    def sums(g, c):
        f = cs_sums(c)
        c_may_fill(pe, k, "s", g, f)
        n, tri = (P, k.tri) if c < QB else (NS, k.tris)
        for r in range(HPG):
            mm = pe.matmul(k.s[:, f % 2, r * n:(r + 1) * n], k.adt_g[0:n, c, r:r + 1].broadcast_to([n, P]), tri[:],
                           start=True, stop=True)
        mm.then_inc(sem["cs_done"], 1)
        f, cols = cr_scores(c), slice(c * P, c * P + n)
        c_may_fill(pe, k, "r", g, f)
        mm = pe.matmul(k.r[0:n, f % 2, 0:n], k.feat[0][:, cols], k.feat[1][:, cols], start=True, stop=True)
        if c == QB:
            c_was_read(pe, k, "r", g, cr_update(QB - 1))
            for j in range(2):
                mm = pe.transpose(k.r[:, f % 2, P + j * P:2 * P + j * P], k.ht[:, j * P:(j + 1) * P], k.ident[:])
        mm.then_inc(sem["cr_done"], 1)

    def outputs(g, c):
        pe.wait_ge(sem["y_in"], 5 * g + c + 1)
        c_may_fill(pe, k, "x", g, c)
        if c:
            c_was_read(pe, k, "r", g, cr_update(c - 1))
        for r in range(HPG):
            out = k.x[64 * (r % 2):64 * (r % 2) + 64, r // 2 * P:r // 2 * P + P]
            pe.matmul(out, k.xdt[:, 64 * r:64 * r + 64], k.m[:, r, :], start=True, stop=False)
            mm = pe.matmul(out, k.ht[:, 64 * r:64 * r + 64], k.e[:, r, :], start=False, stop=True)
        mm.then_inc(sem["cx_done"], 1)
        f = cr_update(c)
        c_may_fill(pe, k, "r", g, f)
        pe.matmul(k.r[:, f % 2, 0:2 * P], k.btok[:, c, :], k.xdd[:], start=True, stop=True).then_inc(sem["cr_done"], 1)

    def old_states(g, n):
        f = cr_state(n)
        c_may_fill(pe, k, "r", g, f)
        for b in range(2):
            for j in range(2):
                t = pe.transpose(k.r[:, f % 2, (2 * b + j) * P:(2 * b + j + 1) * P], k.st0[:, j, 2 * n + b, :], k.ident[:])
        t.then_inc(sem["cr_done"], 1)

    def sample_outputs(g):
        pe.wait_ge(sem["y_in"], 5 * g + QB + 1)
        c_may_fill(pe, k, "x", g, QB)
        for r in range(HPG):
            out = k.x[64 * (r % 2):64 * (r % 2) + 64, r // 2 * P:r // 2 * P + NS]
            pe.matmul(out, k.xdt[0:NS, 64 * r:64 * r + 64], k.m[0:NS, r, 0:NS], start=r < 2, stop=False, skip_group_check=True)
        for n in range(4):
            if n < 3:
                old_states(g, n + 1)
            c_was_read(pe, k, "r", g, cr_state(n))
            for b in range(2):
                for r in range(HPG):
                    at = (2 * n + b) * DT
                    out = k.x[64 * (r % 2):64 * (r % 2) + 64, r // 2 * P + at:r // 2 * P + at + DT]
                    mm = pe.matmul(out, k.hts[n % 2][:, 2 * b + r // 2, 64 * (r % 2):64 * (r % 2) + 64],
                                   k.e[:, r, at:at + DT], start=False, stop=n == 3 and b == 1, skip_group_check=True)
            if n == 3:
                mm.then_inc(sem["cx_done"], 1)
            else:
                mm.then_inc(sem["hts_used"], 1)
        for n in range(4):
            f = cs_state(n)
            c_may_fill(pe, k, "s", g, f)
            pe.matmul(k.s[:, f % 2, :], k.xdd[0:NS, n // 2 * P:n // 2 * P + P], k.bm[:, n % 2 * 4:n % 2 * 4 + 4, :],
                      start=True, stop=True).then_inc(sem["cs_done"], 1)

    def tokens(i):
        pe.wait_ge(sem["feat_ready"], 4 * i + 4)
        for n in range(3):
            src = (k.featn[0], k.featn[2], k.featn[3])[n]
            c_may_fill(pe, k, "s", i, cs_tok(n))
            if n == 0:
                c_may_fill(pe, k, "r", i, CR_TOK)
            for c in range(QB):
                t = pe.transpose(k.s[:, n % 2, c * P:(c + 1) * P], src[:, c * P:(c + 1) * P], k.ident[:])
            t.then_inc(sem["cs_done"], 1)
            t = pe.transpose(k.r[0:NS, 0, n * P:(n + 1) * P], src[:, SEQ:T], k.ident[:])
        t.then_inc(sem["cr_done"], 1)

    def stage(i, u, slots, units):
        if units:
            pe.wait_ge(sem["group_params"], u + 1)
        for n in range(6):
            if units and n < QB:
                sums(u, n)
            if slots and not units and n == 0:
                multiply_new_x(pe, k, s0, u0, 2)
                time_steps()
            elif slots:
                multiply_slot(pe, k, s0 + 6 * i + n, n % 2, u0 + 6 * i + n, u0 // 2 + 3 * i + n // 2, n % 2, k.xh, k.xl)
            if units and n < QB:
                outputs(u, n)
            if units and n == QB:
                sums(u, QB)
                pe.wait_ge(sem["st_landed"], 32 * u + 32)
                old_states(u, 0)
            if units and n == 5:
                sample_outputs(u)
        if slots and not units:
            totals()
        if slots:
            tokens(i)

    stage(0, -1, True, False)
    with pe.Fori(0, GROUPS - 1) as j:
        stage(j + 1, j, True, True)
    stage(GROUPS, GROUPS - 1, False, True)
    pe.wait_ge(sem["acc_added"], 2 * GROUPS)
    pe.matmul(k.s[:, 0, :], k.ones_d[:], k.acc[:, 0:SEQ], start=True, stop=True)
    pe.matmul(k.s[:, 1, 0:NS], k.ones_d[:], k.acc[:, SEQ:T], start=True, stop=True).then_inc(sem["ms_done"], 1)
    for u in range(8):
        t = pe.transpose(k.r[0:4 * HN, u // 4, (u % 4) * P:(u % 4) * P + P],
                         k.ctails[:, 4 * u:4 * u + 4, :].rearrange("p i c -> p (i c)"), k.ident[:])
    t.then_inc(sem["ctails_turned"], 1)
    s, u = s0 + 48, u0 + 48

    def column(i, h, split=None):
        for n in range(2):
            if split:
                pe.wait_ge(sem["g_split"], split[n])
            multiply_slot(pe, k, s + 4 * i + 2 * h + n, n, u + 2 * i + h, u // 2 + i, h,
                          (k.xh, k.xl)[n], (k.gh, k.gl)[n], first=n == 0, last=n == 1)

    column(0, 0, (1, 3))
    column(0, 1)
    with pe.Fori(1, KT // 2) as i:
        for h in range(2):
            column(i, h)
    ln_tensor(pe, k, 2)


def c_scalar(act, k, chain):
    sem, s0, u0 = k.sem, SLOT_C, USE_C
    act.wait_ge(sem["c_consts"], 1)
    act.wait_ge(sem["c_params"], 64)

    def time_steps():
        softplus_scalar(act, k, k.spa[:], 2)
        act.activation(k.rowp[:, 1, :], k.rowp[:, 1, :], ACT.Exp).then_inc(sem["a_exp"], 1)

    def slot(i, n, units):
        if units or n:
            split_high(act, k, s0 + 6 * i + n + 1, s0 // 2 + 3 * i + (n + 1) // 2, (n + 1) % 2)
        if 0 < n <= 4:
            act.wait_ge(sem["c_conv"], 4 * i + n)
            act.activation(k.th[:], k.cc[:], ACT.Tanh).then_inc(sem["c_tanh"], 1)
        await_slot(act, k, s0 + 6 * i + n)
        if n < 4:
            if n == 0:
                act.wait_ge(sem["c_conv"], 4 * i)
            row_of_inputs(act, k, n % 2, chain)
        else:
            if n == 4:
                act.wait_ge(sem["feat_ready"], 4 * i + 4)
            else:
                act.wait_ge(sem["s_evac"], u0 + 6 * i + 5)
                act.wait_ge(sem["p_evac0"], u0 // 2 + 3 * i + 3)
            chain(act.activation(k.th[:, HALF:T], k.proj[:, n % 2, 0:T - HALF], ACT.Tanh, scale=0.5))
            act.activation(k.th[:, 0:HALF], k.proj_lo[:, 0:HALF], ACT.Tanh, scale=0.5).then_inc(sem["c_tanh"], 1)

    def chunk(u, c):
        f, m = cs_sums(c), P if c < QB else NS
        act.wait_ge(sem["dm_ready"], 5 * u + c + 1)
        chain(act.activation(k.dm[0:m, :, 0:m], k.dm[0:m, :, 0:m], ACT.Exp))
        if c:
            c_filled(act, k, "x", u, c - 1)
        act.activation(k.e[:, :, 0:m], k.s[:, f % 2, 0:HPG * m].rearrange("p (r l) -> p r l", r=HPG),
                       ACT.Exp).then_inc(c_read(k, "s", f), 1)

    def old_states(u, n):
        f = cr_state(n)
        c_filled(act, k, "r", u, f)
        if n >= 2:
            act.wait_ge(sem["hts_used"], 3 * u + n - 1)
        act.activation(k.hts[n % 2][:].rearrange("p q n -> p (q n)"), k.r[:, f % 2, :], ACT.Copy).then_inc(c_read(k, "r", f), 1)

    def stage(i, u, slots, units):
        for n in range(6):
            if units and n < QB:
                chunk(u, n)
            if slots:
                slot(i, n, units)
            if slots and not units and n == 0:
                time_steps()
            if units and n == QB:
                chunk(u, QB)
                old_states(u, 0)
        for n in range(1, 4):
            if units:
                old_states(u, n)
        for j in range(2):
            if units:
                act.wait_ge(sem["g_made"], 2 * u + j + 1)
                act.wait_ge(sem["acc_added"], 2 * u)
                act.activation(k.sq[1][:, j, :], k.feat[2 + j][:], ACT.Square).then_inc(sem["g_squared"], 1)
        if slots and not units:
            act.wait_ge(sem["dec_in"], 1)
            act.activation(k.dec[:], k.dec[:], ACT.Exp).then_inc(sem["dt_made"], 1)
        for n in (1, 2):
            if slots:
                f = cs_tok(n)
                c_filled(act, k, "s", i, f)
                act.activation(k.xtok[:, 0:QB, (n - 1) * P:n * P], k.s[:, f % 2, :].rearrange("p (c q) -> p c q", c=QB),
                               ACT.Copy).then_inc(c_read(k, "s", f), 1)

    def high_parts(lo, hi):
        for at in (0, KT):
            l, h = max(lo, at), min(hi, at + KT)
            if l < h:
                chain(act.activation((k.xh, k.xl)[at // KT][:, l - at:h - at, :], k.out[:, l:h, :], ACT.Copy))

    stage(0, -1, True, False)
    with chain.loop("c", GROUPS - 1) as j:
        stage(j + 1, j, True, True)
    await_slot(act, k, s0 + 47)
    for n, (lo, hi) in enumerate(((0, KT), (KT, CT - 2))):
        act.wait_ge(sem["g_ready"], hi)
        high_parts(lo, hi)
        act.sem_inc(sem["g_high"], 1)
    stage(GROUPS, GROUPS - 1, False, True)
    act.wait_ge(sem["g_ready"], CT)
    high_parts(CT - 2, CT)
    act.sem_inc(sem["g_high"], 1)
    act.wait_ge(sem["ms_done"], 1)
    chain(act.activation(k.rs[:, 0:SEQ], k.s[:, 0, :], ACT.Sqrt, bias=k.eps[:], scale=D / INNER))
    act.activation(k.rs[:, SEQ:T], k.s[:, 1, 0:NS], ACT.Sqrt, bias=k.eps[:], scale=D / INNER).then_inc(sem["c_rms"], 1)
    s = s0 + 48

    def body(i, final):
        for n in range(4):
            if not (final and n == 3 and k.last == 2):
                split_high(act, k, s + 4 * i + n + 1, s // 2 + 2 * i + (n + 1) // 2, (n + 1) % 2)
    turns_of(chain, "c_out", KT // 2, body, peel=True)
    act.wait_ge(sem["ctails_out"], 128)
    ln_scalar(act, k, 2, chain)


def c_vector(dve, k, chain):
    sem, s0, u0 = k.sem, SLOT_C, USE_C
    dve.wait_ge(sem["c_consts"], 1)
    dve.wait_ge(sem["c_params"], 64)
    chain(dve.tensor_scalar(k.par_c[:, :, 0:5], k.par_c[:, :, 0:5], 0.5, None, ALU.mult))
    for r in range(2):
        chain(dve.tensor_copy(k.nw[:, r * KT:(r + 1) * KT], k.par_m[:, :, 8 + r]))
    for r in range(2):
        chain(dve.tensor_copy(k.dsk[64 * r:64 * r + 64, :], k.rowp[64 * r:64 * r + 64, 2, r::2]))
    dve.wait_ge(sem["dt_raw"], 1)
    bias = k.rowp[:, 0, :].unsqueeze(1)
    chain(dve.tensor_tensor(k.dt[:, 0:QB], k.x[:, 0:P].rearrange("p (c h) -> p c h", c=QB), bias.broadcast_to([P, QB, SSDH]), ALU.add))
    chain(dve.tensor_tensor(k.dt[0:NS, QB], k.x[0:NS, P:P + SSDH], k.rowp[0:NS, 0, :], ALU.add))
    flat = [t[:].rearrange("p c h -> p (c h)") for t in (k.dt, k.adt)]
    softplus_vector(dve, k, chain, flat[0], flat[1], k.spa[:], 2)
    chain(dve.tensor_copy(k.dt[:], k.adt[:]))
    dve.wait_ge(sem["a_exp"], 1)
    chain(dve.tensor_scalar(k.rowp[:, 1, :], k.rowp[:, 1, :], -1.0, None, ALU.mult))
    dve.tensor_tensor(k.adt[:], k.dt[:], k.rowp[:, 1:2, :].broadcast_to([P, CH, SSDH]), ALU.mult).then_inc(sem["adt_ready"], 1)

    def totals():
        dve.wait_ge(sem["sums_done"], 1)
        chain(dve.tensor_copy(k.cs[:, 0:QB], k.s[:, 0, 0:P].rearrange("p (c h) -> p c h", c=QB)))
        chain(dve.tensor_copy(k.cs[0:NS, QB], k.s[0:NS, 0, P:P + SSDH]))
        chain(dve.scalar_tensor_tensor(k.dec[:, 0:QB], k.s[:, 1, 0:P].rearrange("p (c h) -> p c h", c=QB), float(D), k.cs[:, 0:QB],
                                       ALU.mult, ALU.subtract))
        dve.tensor_tensor(k.dec[0:NS, QB], k.s[0:NS, 1, P:P + SSDH], k.cs[0:NS, QB], ALU.subtract).then_inc(sem["dec_in"], 1)
        dve.wait_ge(sem["dt_made"], 1)

    def convolutions(g):
        for n, tile in enumerate((CT + g, CT + GROUPS + g, 2 * g, 2 * g + 1)):
            chain(dve.tensor_scalar(k.curc[:, n, :], k.par_c[:, bass.ds(tile, 1), :].rearrange("p o c -> p (o c)"), 1.0, None, ALU.mult))

    def convolution(g, n):
        cur = k.curc[:, n, :]
        chain(dve.tensor_copy(k.u_s[:, :, 0:HIST], cur[:, 5:29].rearrange("p (b t) -> p b t", b=NB)))
        dve.wait_ge(sem["s_evac"], u0 + 6 * g + n + 1)
        dve.wait_ge(sem[f"p_evac{n % 2}"], u0 // 2 + 3 * g + n // 2 + 1)
        tile = (CT + g, CT + GROUPS + g, 2 * g, 2 * g + 1)[n]
        tail = k.ctails[:, bass.ds(tile, 1), :].rearrange("p o c -> p (o c)")
        chain(dve.tensor_scalar(tail[:, 0:HIST], k.u[:, SEQ:SROW], 1.0, None, ALU.mult))
        chain(dve.tensor_scalar(tail[:, HIST:HN].rearrange("p (b t) -> p b t", b=NB), k.u_s[:, :, DT:WIN], 1.0, None, ALU.mult))
        convolve(dve, k, chain, cur, k.cc, "c_conv")

    def feature(g, n):
        dve.wait_ge(sem["c_tanh"], 6 * g + n + 1)
        dve.wait_ge(sem["c_conv"], 4 * g + n + 1)
        dve.scalar_tensor_tensor(k.featn[n][:], k.th[:], 1.0, k.cc[:], ALU.add, ALU.mult).then_inc(sem["feat_ready"], 1)
        dve.wait_ge(sem["feat_ready"], 4 * g + n + 1)

    def gate(g, n):
        dve.wait_ge(sem["c_tanh"], 6 * g + n + 1)
        sz = k.szn[n - 4]
        dve.scalar_tensor_tensor(sz[:, 0:HALF], k.th[:, 0:HALF], 1.0, k.proj_lo[:, 0:HALF], ALU.add, ALU.mult).then_inc(sem["s_evac"], 1)
        dve.scalar_tensor_tensor(sz[:, HALF:T], k.th[:, HALF:T], 1.0, k.proj[:, n % 2, 0:T - HALF], ALU.add, ALU.mult).then_inc(sem[f"p_evac{n % 2}"], 1)

    def differences(g, c):
        n, mask, f = (P, k.negc, cs_sums(c)) if c < QB else (NS, k.negcs, cs_sums(c))
        c_filled(dve, k, "s", g, f)
        for r in range(HPG):
            step = dve.scalar_tensor_tensor(k.dm[0:n, r, 0:n], k.s[0:n, f % 2, r * n:r * n + n], k.cs_g[0:n, c, r:r + 1],
                                            mask[:], ALU.subtract, ALU.add)
            chain(step) if r < HPG - 1 else step.then_inc(sem["dm_ready"], 1)

    def chunk(g, c):
        n = P if c < QB else NS
        cols = slice(c * P, c * P + n)
        differences(g, c)
        if c:
            c_filled(dve, k, "x", g, c - 1)
            c_filled(dve, k, "r", g, cr_update(c - 1))
        x3 = k.xtok[0:n, c].rearrange("p (r q) -> p r q", r=HPG)
        xdt, xdd = (t[0:n].rearrange("p (r q) -> p r q", r=HPG) for t in (k.xdt, k.xdd))
        chain(dve.tensor_tensor(xdt, x3, k.dt_g[0:n, c].unsqueeze(2).broadcast_to([n, HPG, HD]), ALU.mult))
        chain(dve.tensor_tensor(xdd, xdt, k.dec_g[0:n, c].unsqueeze(2).broadcast_to([n, HPG, HD]), ALU.mult))
        c_was_read(dve, k, "s", g, cs_sums(c))
        f = cr_scores(c)
        c_filled(dve, k, "r", g, f)
        step = dve.tensor_tensor(k.m[0:n, :, 0:n], k.dm[0:n, :, 0:n], k.r[0:n, f % 2, 0:n].unsqueeze(1).broadcast_to([n, HPG, n]), ALU.mult)
        if c < QB:
            step.then_inc(c_read(k, "r", f), 1)
            chain(dve.tensor_copy(k.edec[:], k.e[:, :, P - 1]))
        else:
            chain(step)
            dve.wait_ge(sem["hp_out"], 16 * g)
            dve.tensor_copy(k.hout[:], k.r[:, f % 2, P:3 * P].rearrange("p (j n) -> p j n", j=2)).then_inc(c_read(k, "r", f), 1)
            c_was_read(dve, k, "r", g, f)
            for h in range(2):
                lo = slice(64 * h, 64 * h + 64)
                chain(dve.tensor_copy(k.decp[lo], k.e[lo, h:HPG:2, DT - 1:NS:DT]))
            dve.sem_inc(sem["hout_ready"], 1)
        dve.tensor_tensor(k.e[:, :, 0:n], k.e[:, :, 0:n], k.feat[1][:, cols].unsqueeze(1).broadcast_to([P, HPG, n]),
                          ALU.mult).then_inc(sem["y_in"], 1)

    def results(g, c):
        n = P if c < QB else NS
        c_filled(dve, k, "x", g, c)
        for j in range(2):
            t = k.feat[2 + j][:, c * P:c * P + n]
            step = dve.scalar_tensor_tensor(t, t, k.dsk[:, bass.ds(2 * g + j, 1)], k.x[:, j * P:j * P + n], ALU.mult, ALU.add)
            chain(step) if j == 0 else step.then_inc(sem["cx_read"], 1)
        if c < QB:
            f = cr_update(c)
            c_filled(dve, k, "r", g, f)
            h3 = k.ht[:].rearrange("p (r q) -> p r q", r=HPG)
            chain(dve.tensor_tensor(h3, h3, k.edec[:].unsqueeze(2).broadcast_to([P, HPG, HD]), ALU.mult))
            dve.tensor_tensor(k.ht[:], k.ht[:], k.r[:, f % 2, 0:2 * P], ALU.add).then_inc(c_read(k, "r", f), 1)
            c_was_read(dve, k, "r", g, f)

    def finish(g):
        for n in range(4):
            f = cs_state(n)
            c_filled(dve, k, "s", g, f)
            for b in range(4):
                at = n % 2 * 4 + b
                h = k.st0[:, n // 2, at, :]
                step = dve.scalar_tensor_tensor(h, h, k.decp[:, n // 2, at:at + 1], k.s[:, f % 2, b * P:(b + 1) * P], ALU.mult, ALU.add)
                chain(step) if b < 3 else step.then_inc(c_read(k, "s", f), 1)
            c_was_read(dve, k, "s", g, f)
        dve.sem_inc(sem["st_ready"], 1)
        c_was_read(dve, k, "x", g, QB)
        for j in range(2):
            t = k.feat[2 + j][:]
            dve.scalar_tensor_tensor(t, t, 0.5, k.sz[j][:], ALU.mult, ALU.mult).then_inc(sem["g_made"], 1)
            dve.wait_ge(sem["g_made"], 2 * g + j + 1)
            out = k.out[:, bass.ds(2 * g + j, 1), :].rearrange("p o t -> p (o t)")
            dve.tensor_scalar(out, t, k.nw[:, bass.ds(2 * g + j, 1)], None, ALU.mult).then_inc(sem["g_ready"], 1)
            dve.wait_ge(sem["g_ready"], 2 * g + j + 1)

    def take_parameters(g):
        for dst, src in ((k.dt_g, k.dt), (k.adt_g, k.adt), (k.cs_g, k.cs), (k.dec_g, k.dec)):
            chain(dve.tensor_scalar(dst[:], src[:, :, bass.ds(HPG * g, HPG)], 1.0, None, ALU.mult))
        chain(dve.memset(k.ht[:], 0.0))
        for n in range(2):
            chain(dve.tensor_copy(k.feat[n][:], k.featn[n][:]))
        dve.sem_inc(sem["group_params"], 1)

    def take_over(g, units):
        if units:
            dve.wait_ge(sem["g_squared"], 2 * g)
        c_filled(dve, k, "s", g, cs_tok(0))
        dve.tensor_copy(k.btok[:, 0:QB], k.s[:, 0, :].rearrange("p (c n) -> p c n", c=QB)).then_inc(c_read(k, "s", 0), 1)
        c_filled(dve, k, "r", g, CR_TOK)
        chain(dve.tensor_copy(k.btok[0:NS, QB], k.r[0:NS, 0, 0:P]))
        dve.tensor_copy(k.xtok[0:NS, QB], k.r[0:NS, 0, P:3 * P]).then_inc(c_read(k, "r", CR_TOK), 1)
        dve.wait_ge(sem["s_evac"], u0 + 6 * g + 6)
        for par in range(2):
            dve.wait_ge(sem[f"p_evac{par}"], u0 // 2 + 3 * g + 3)
        for n in (2, 3):
            chain(dve.tensor_copy(k.feat[n][:], k.featn[n][:]))
        for j in range(2):
            chain(dve.tensor_copy(k.sz[j][:], k.szn[j][:]))
        c_was_read(dve, k, "r", g, CR_TOK)
        for n in (1, 2):
            c_was_read(dve, k, "s", g, cs_tok(n))

    def sample_blocks():
        chain(dve.tensor_tensor(k.bm, k.btok[0:NS, QB:CH].broadcast_to([NS, NB, STATE]),
                                k.blk[:, 0:NS:DT].unsqueeze(2).broadcast_to([NS, NB, STATE]), ALU.mult))

    def stage(i, u, slots, units):
        if slots:
            convolutions(i)
        for n in range(6):
            if units and n < QB:
                chunk(u, n)
            if slots and 0 < n <= 4:
                convolution(i, n - 1)
            if units and n < QB:
                results(u, n)
            if slots and 0 < n <= 4:
                feature(i, n - 1)
            if slots and n >= 4:
                gate(i, n)
            if units and n == QB:
                sample_blocks()
                chunk(u, QB)
        if slots and units:
            take_parameters(i)
        if units:
            results(u, QB)
            finish(u)
        if slots and not units:
            totals()
            take_parameters(i)
        if slots:
            take_over(i, units)

    def branch_low(n, lo, hi):
        dve.wait_ge(sem["g_high"], n + 1)
        dve.wait_ge(sem["g_ready"], hi)
        for at in (0, KT):
            l, h = max(lo, at), min(hi, at + KT)
            if l < h:
                chain(dve.tensor_tensor(k.g[:, l:h, :], k.out[:, l:h, :], (k.xh, k.xl)[at // KT][:, l - at:h - at, :], ALU.subtract))
        dve.sem_inc(sem["g_split"], 1)

    stage(0, -1, True, False)
    with chain.loop("c", GROUPS - 1) as j:
        stage(j + 1, j, True, True)
    stage(GROUPS, GROUPS - 1, False, True)
    branch_low(0, 0, KT)
    branch_low(1, KT, CT - 2)
    branch_low(2, CT - 2, CT)
    dve.wait_ge(sem["ctails_turned"], 1)
    dve.tensor_copy(k.rows[1][0:4 * HN, :].rearrange("p (b c) -> p b c", b=2), k.r[0:4 * HN]).then_inc(sem["ctails_read"], 1)
    dve.wait_ge(sem["c_rms"], 1)
    chain(dve.reciprocal(k.rs[:], k.rs[:]))
    s, u = s0 + 48, u0 + 48

    dve.memset(k.xsum, 0.0).then_inc(sem["ln_sum"], 1)
    with chain.loop("c_out", KT // 2) as i:
        for h in range(2):
            await_slot(dve, k, s + 4 * i + 2 * h + 1)
            dve.tensor_tensor(k.cc[:, HALF:T], k.proj[:, h, 0:T - HALF], k.rs[:, HALF:T], ALU.mult).then_inc(sem[f"p_evac{h}"], 1)
            dve.tensor_tensor(k.cc[:, 0:HALF], k.proj_lo[:, 0:HALF], k.rs[:, 0:HALF], ALU.mult).then_inc(sem["s_evac"], 1)
            dve.wait_ge(sem[f"p_evac{h}"], u // 2 + i + 1)
            dve.wait_ge(sem["s_evac"], u + 2 * i + h + 1)
            x = k.xT[:, bass.ds(2 * i + h, 1), :].rearrange("p o t -> p (o t)")
            dve.scalar_tensor_tensor(x, x, ALPHA, k.cc[:], ALU.mult, ALU.add).then_inc(sem["c_x"], 1)
            dve.wait_ge(sem["c_x"], 2 * i + h + 1)
            add_to_sum(dve, k, x, 2, 2 * i + h)
    ln_vector(dve, k, 2, chain)



def out_sync(sp, k, s, w, lo, hi):
    with sp.Fori(lo, hi) as i:
        col = [sp.snap((2 * i + h) * P) for h in range(2)]
        for h in range(2):
            load_slot(sp, k, s + 2 * i + h, h, w[:, bass.ds(col[h], P)])


def out_tensor(pe, k, s, u):
    multiply_slot(pe, k, s + 1, 1, u + 1, u // 2, 1, k.gh, k.gl)
    with pe.Fori(1, KT // 2) as i:
        for h in range(2):
            multiply_slot(pe, k, s + 2 * i + h, h, u + 2 * i + h, u // 2 + i, h, k.gh, k.gl)


def out_scalar(act, k, s, chain, last, ahead=1):
    def body(i, final):
        for h in range(2):
            n = h + ahead
            if not (final and (n == 3 or n == 2 and last)):
                split_high(act, k, s + 2 * i + n, s // 2 + i + n // 2, n % 2)
    turns_of(chain, "out", KT // 2, body, peel=True)


def add_to_sum(dve, k, x, layer, n):
    dve.wait_ge(k.sem["ln_sum"], (KT + 1) * layer + n + 1)
    dve.tensor_tensor(k.xsum, k.xsum, x, ALU.add).then_inc(k.sem["ln_sum"], 1)


def out_vector(dve, k, s, u, chain, layer):
    dve.memset(k.xsum, 0.0).then_inc(k.sem["ln_sum"], 1)
    with chain.loop("out", KT // 2) as i:
        for h in range(2):
            await_slot(dve, k, s + 2 * i + h)
            x = k.xT[:, bass.ds(2 * i + h, 1), :].rearrange("p o t -> p (o t)")
            dve.scalar_tensor_tensor(x[:, HALF:T], x[:, HALF:T], ALPHA, k.proj[:, h, 0:T - HALF], ALU.mult, ALU.add).then_inc(k.sem[f"p_evac{h}"], 1)
            dve.scalar_tensor_tensor(x[:, 0:HALF], x[:, 0:HALF], ALPHA, k.proj_lo[:, 0:HALF], ALU.mult, ALU.add).then_inc(k.sem["s_evac"], 1)
            dve.wait_ge(k.sem[f"p_evac{h}"], u // 2 + i + 1)
            dve.wait_ge(k.sem["s_evac"], u + 2 * i + h + 1)
            add_to_sum(dve, k, x, layer, 2 * i + h)


def ln_tensor(pe, k, layer):
    sem = k.sem
    pe.wait_ge(sem["ln_sum"], (KT + 1) * (layer + 1))
    pe.matmul(k.s[:, 0, :], k.ones_d[:], k.xsum[:, 0:SEQ], start=True, stop=True)
    pe.matmul(k.r[:, 0, 0:NS], k.ones_d[:], k.xsum[:, SEQ:T], start=True, stop=True).then_inc(sem["ln_mean"], 1)
    for i in range(KT):
        if i % 2 == 0:
            pe.wait_ge(sem["ln_sq"], 4 * layer + i // 2 + 1)
        pe.matmul(k.s[:, 1, :], k.ones_d[:], k.sq[i // 2 % 2][:, i % 2, 0:SEQ], start=i == 0, stop=i == KT - 1)
        mm = pe.matmul(k.r[:, 1, 0:NS], k.ones_d[:], k.sq[i // 2 % 2][:, i % 2, SEQ:T], start=i == 0, stop=i == KT - 1)
        if i % 2:
            mm.then_inc(sem["ln_acc"], 1)


def ln_scalar(act, k, layer, chain):
    sem = k.sem
    if layer < k.last:
        s = (SLOT_B, SLOT_C, SLOT_A[1])[layer] + 1
        split_high(act, k, s, s // 2, 1)
    for j in range(KT // 2):
        act.wait_ge(sem["ln_sub"], 4 * layer + j + 1)
        if 4 * layer + j >= 2:
            act.wait_ge(sem["ln_acc"], 4 * layer + j - 1)
        act.activation(k.sq[j % 2][:], k.xT[:, 2 * j:2 * j + 2, :], ACT.Square).then_inc(sem["ln_sq"], 1)
    act.wait_ge(sem["ln_acc"], 4 * layer + 4)
    chain(act.activation(k.rs[:, 0:SEQ], k.s[:, 1, :], ACT.Sqrt, bias=k.eps[:]))
    act.activation(k.rs[:, SEQ:T], k.r[:, 1, 0:NS], ACT.Sqrt, bias=k.eps[:]).then_inc(sem["ln_sd"], 1)
    for i in range(KT):
        act.wait_ge(sem["ln_norm"], 8 * layer + i + 1)
        bias = k.par_m[:, i, 4 + layer:5 + layer]
        act.activation(k.xT[:, i, :], k.xT[:, i, :], ACT.Identity, bias=bias).then_inc(sem["ln_x"], 1)
        if layer < k.last:
            act.wait_ge(sem["ln_x"], 8 * layer + i + 1)
            act.activation(k.xh[:, i, :], k.xT[:, i, :], ACT.Copy).then_inc(sem["ln_xh"], 1)


def ln_vector(dve, k, layer, chain):
    sem = k.sem
    dve.wait_ge(sem["ln_mean"], layer + 1)
    for j in range(KT // 2):
        x = k.xT[:, 2 * j:2 * j + 2, :]
        chain(dve.tensor_tensor(x[:, :, 0:SEQ], x[:, :, 0:SEQ], k.s[:, 0:1, :].broadcast_to([P, 2, SEQ]), ALU.subtract))
        dve.tensor_tensor(x[:, :, SEQ:T], x[:, :, SEQ:T], k.r[:, 0:1, 0:NS].broadcast_to([P, 2, NS]),
                          ALU.subtract).then_inc(sem["ln_sub"], 1)
    dve.wait_ge(sem["ln_sd"], layer + 1)
    chain(dve.reciprocal(k.rs[:], k.rs[:]))
    dve.wait_ge(sem["ln_sub"], 4 * layer + 4)

    def low(i):
        dve.wait_ge(sem["ln_xh"], 8 * layer + i + 1)
        dve.tensor_tensor(k.xl[:, i, :], k.xT[:, i, :], k.xh[:, i, :], ALU.subtract).then_inc(sem["x_tile"], 1)

    for i in range(KT + 1):
        if i < KT:
            dve.scalar_tensor_tensor(k.xT[:, i, :], k.xT[:, i, :], k.par_m[:, i, layer:layer + 1], k.rs[:],
                                     ALU.mult, ALU.mult).then_inc(sem["ln_norm"], 1)
        if i and layer < k.last:
            low(i - 1)
    if layer < k.last:
        dve.wait_ge(sem["x_tile"], KT * (layer + 1))
        dve.sem_inc(sem["x_ready"], 1)



def y_tensor(pe, k, layer):
    pe.wait_ge(k.sem["ln_x"], 8 * layer + 8)
    for c in range(CH):
        n = P if c < QB else NS
        bank = (k.s, k.r)[c % 2]
        if c >= 2:
            pe.wait_ge(k.sem[f"y_read{c % 2}"], c // 2)
        for i in range(KT):
            t = pe.transpose(bank[0:n, i // 4, (i % 4) * P:(i % 4) * P + P], k.xT[:, i, c * P:c * P + n], k.ident[:, :])
        t.then_inc(k.sem["y_turned"], 1)


def y_copy(eng, k, c, op):
    n = P if c < QB else NS
    eng.wait_ge(k.sem["y_turned"], c + 1)
    if c >= 2:
        eng.wait_ge(k.sem[f"y_out{c % 2}"], 16 * (c // 2))
    op(k.rows[c % 2][0:n, :].rearrange("p (b c) -> p b c", b=2), (k.s, k.r)[c % 2][0:n, :, :]).then_inc(k.sem[f"y_read{c % 2}"], 1)


def y_sync(sp, k, o):
    for c in range(CH):
        n = P if c < QB else NS
        dst = o["y_prompt"][0, c * P:(c + 1) * P, :] if c < QB else o["y_sample"].rearrange("b t d -> (b t) d")
        sp.wait_ge(k.sem[f"y_read{c % 2}"], c // 2 + 1)
        sp.dma_start(dst, k.rows[c % 2][0:n, :]).then_inc(k.sem[f"y_out{c % 2}"], 16)
    sp.wait_ge(k.sem["y_out0"], 48)
    sp.wait_ge(k.sem["y_out1"], 32)



def layer_a_buffers(k):
    k.cur = k.sb("cur", [P, 45])
    k.gw = k.sb("gate_w", [P, 2, P])
    k.tg, k.tr, k.ti, k.t, k.rt = (k.sb(n, [P, T]) for n in ("tg", "tr", "ti", "t", "rt"))
    k.sg, k.q, k.a, k.a2, k.gi, k.h, k.cx = (k.sb(n, [P, T]) for n in ("sg", "q", "a", "a2", "gi", "h", "cx"))
    k.h0a = k.sb("h0a", [P, NB])
    k.tails_sb = k.sb("tails_sb", [P, 3 * P])
    k.tails = k.sb("tails", [P, KT, AN])


def conv_buffers(k):
    k.u = k.sb("u", [P, UW])
    k.u_s = k.u[:, SROW:UW].rearrange("p (b t) -> p b t", b=NB)
    conv = k.sb("conv", [P, UW])
    k.conv_s = conv[:, SROW:UW].rearrange("p (b t) -> p b t", b=NB)
    k.conv = conv[:, 0:CW]
    k.xsum = k.u[:, HIST:HIST + T]


def scoped(nc, k, make):
    with ExitStack() as ctx:
        k.sb = lambda name, shape, dtype=F32: ctx.enter_context(nc.sbuf_tensor(name, shape, dtype))
        make(k)


def build(nc, a, o):
    with ExitStack() as ctx:
        k = allocate(nc, ctx)
        k.last = DEPTH - 1
        k.par_c = k.sb("par_c", [P, CONV_C // P, 29])
        k.par_d = [k.sb(f"par_d{j}", [P, 5, KT]) for j in range(2)]
        k.spx, k.spy = k.sb("spx", [P, 2 * KT]), k.sb("spy", [P, 2 * KT])
        k.spa = k.rs[:, 0:3 * CH * SSDH].rearrange("p (a n) -> p a n", a=3)
        conv_buffers(k)
        scoped(nc, k, layer_a_buffers)
        scoped(nc, k, layer_b_buffers)
        scoped(nc, k, layer_c_buffers)
        block = ctx.enter_context(nc.Block())

        @block.sync
        def _(sp):
            prologue_sync(sp, k, a)
            a_sync(sp, k, a, o, 0, [b_cols(a, 0, 0), b_cols(a, 1, 0)])
            b_sync(sp, k, a, o, [a["c_in_w"][0][:, c_cols(0, n):c_cols(0, n) + P] for n in range(2)])
            c_sync(sp, k, a, o, [a_slot(a, 1, n) for n in range(2)])
            a_sync(sp, k, a, o, 1, None)
            y_sync(sp, k, o)
            for name, count in (("tails_out", 2 * TAILS_OUT), ("kv_out", 256), ("ctails_out", 128), ("st_out", 256), ("hp_out", 128)):
                sp.wait_ge(k.sem[name], count)

        @block.gpsimd
        def _(pool):
            chain = Chain(pool, k.sem["chain_pool"], STEPS, "pool")
            pool.sem_inc(k.sem["w_lo"], 1)
            prologue_pool(pool, k, chain)
            low_parts(pool, k, 1, 24)
            b_pool(pool, k, chain)
            c_pool(pool, k, chain)
            pool.wait_ge(k.sem["x_ready"], 4)
            pool.memset(k.gw[:], 0.0).then_inc(k.sem["consts"], 1)
            low_parts(pool, k, SLOT_A[1] + 1, 23)

        @block.tensor
        def _(pe):
            pe.sem_inc(k.sem["pe_slot"], 1)
            prologue_tensor(pe, k, a)
            a_tensor(pe, k, 0)
            b_tensor(pe, k)
            c_tensor(pe, k)
            a_tensor(pe, k, 1)
            y_tensor(pe, k, k.last)

        @block.scalar
        def _(act):
            chain = Chain(act, k.sem["chain_act"], STEPS, "act")
            prologue_scalar(act, k, a)
            a_scalar(act, k, 0, chain)
            b_scalar(act, k, chain)
            c_scalar(act, k, chain)
            a_scalar(act, k, 1, chain)
            for c in range(0, CH, 2):
                y_copy(act, k, c, lambda d, s: act.activation(d, s, ACT.Copy))

        @block.vector
        def _(dve):
            chain = Chain(dve, k.sem["chain_dve"], STEPS, "dve")
            prologue_vector(dve, k, a, chain)
            a_vector(dve, k, 0, chain)
            b_vector(dve, k, chain)
            c_vector(dve, k, chain)
            a_vector(dve, k, 1, chain)
            for c in range(1, CH, 2):
                y_copy(dve, k, c, dve.tensor_copy)


INS = """x_prompt x_sample cache_k cache_v page_table state_lru_conv state_lru_h state_ssd_conv state_ssd_h
    ln_g ln_b a_in_w a_conv_w a_conv_b a_gate_r_w a_gate_r_b a_gate_i_w a_gate_i_b a_lambda a_out_w
    b_in_w b_lambda b_subln_w b_out_w c_in_w c_conv_w c_conv_b c_dt_bias c_a_log c_d c_norm_w c_out_w""".split()
OUTS = dict(
    y_prompt=(1, 512, 1024), y_sample=(8, 4, 1024), k_prompt=(1, 1, 512, 8, 2, 64), v_prompt=(1, 1, 512, 8, 128),
    k_sample=(1, 8, 4, 8, 2, 64), v_sample=(1, 8, 4, 8, 128), lru_conv_prompt=(2, 1, 3, 1024),
    lru_h_prompt=(2, 1, 1024), lru_conv_sample=(2, 8, 3, 1024), lru_h_sample=(2, 8, 1024),
    ssd_conv_prompt=(1, 1, 3, 4096), ssd_h_prompt=(1, 1, 32, 64, 128), ssd_conv_sample=(1, 8, 3, 4096),
    ssd_h_sample=(1, 8, 32, 64, 128))


def kernel(**inputs):
    import numpy as np
    import concourse.bacc as bacc
    from concourse.bass_utils import run_bass_kernel_spmd

    nc = bacc.Bacc("TRN2", target_bir_lowering=False, num_devices=1)
    arrays, a, o = {}, {}, {}
    for name in INS:
        arrays[f"in_{name}"] = np.ascontiguousarray(inputs[name])
        a[name] = nc.dram_tensor(f"in_{name}", arrays[f"in_{name}"].shape,
                                 mybir.dt.from_np(arrays[f"in_{name}"].dtype), kind="ExternalInput").ap()
    for name, shape in OUTS.items():
        o[name] = nc.dram_tensor(f"out_{name}", shape, F32, kind="ExternalOutput").ap()
    build(nc, a, o)
    r = run_bass_kernel_spmd(nc, [arrays], core_ids=[0])
    return tuple(r.results[0][f"out_{name}"] for name in OUTS)
```
